# Optimizing a Trainium2 kernel written in Bass

```python
import math, functools
import jax, jax.numpy as jnp
from jax import lax
import numpy as np

D_MODEL = 1024
BATCH = 1
SEQ = 256
DEPTH = 2
DEC_BATCH = 8
DEC_SEQ = 1
PAST_LEN = 2048
PAGE_SIZE = 128

N_GROUP_HEADS = 4
HEAD_DIM = 64
GROUP_W = N_GROUP_HEADS * HEAD_DIM
MIX_W = 4 * GROUP_W
CONV_K = 31
GLA_LR = 16
GLA_TAU = 16.0
GLA_CHUNK = 16
RET_CHUNK = 128
FOX_BLOCK = 128
D_FF = 2816
N_EXPERTS = 8
TOP_K = 2
D_EXPERT = 3584
EPS = 1e-6
IN_SPLITS = (GROUP_W, GROUP_W,
             GROUP_W, GROUP_W, GROUP_W, N_GROUP_HEADS,
             GROUP_W, GROUP_W, GROUP_W, GLA_LR, GROUP_W,
             GROUP_W, GROUP_W, GROUP_W, GROUP_W)
IN_COLS = 13 * GROUP_W + N_GROUP_HEADS + GLA_LR

kernel_name = 'hybrid_conv_fox_gla_retnet_adaln_decoder_step'

def rms_norm(x, g):
    xf = x.astype(jnp.float32)
    y = xf * lax.rsqrt(jnp.mean(xf * xf, axis=-1, keepdims=True) + EPS)
    return (y * g.astype(jnp.float32)).astype(x.dtype)

def layer_norm(x, g, b):
    xf = x.astype(jnp.float32)
    mu = jnp.mean(xf, axis=-1, keepdims=True)
    xc = xf - mu
    var = jnp.mean(xc * xc, axis=-1, keepdims=True)
    return (xc * lax.rsqrt(var + EPS) * g.astype(jnp.float32) + b.astype(jnp.float32)).astype(x.dtype)

def rope(x, pos):
    half = HEAD_DIM // 2
    inv = 10000.0 ** (-jnp.arange(half, dtype=jnp.float32) / half)
    ang = pos[:, None] * inv[None, :]
    cos = jnp.cos(ang)[None, :, None, :]
    sin = jnp.sin(ang)[None, :, None, :]
    xf = x.astype(jnp.float32)
    x1, x2 = xf[..., :half], xf[..., half:]
    return jnp.concatenate([x1 * cos - x2 * sin, x2 * cos + x1 * sin], axis=-1)

def causal_dwconv(u, buf, w, b):
    full = jnp.concatenate([buf.astype(u.dtype), u], axis=1)
    y = lax.conv_general_dilated(full, w[:, None, :].astype(u.dtype), (1,), 'VALID',
                                 dimension_numbers=('NWC', 'WIO', 'NWC'),
                                 feature_group_count=u.shape[-1])
    return y + b, full[:, full.shape[1] - (CONV_K - 1):]

def to_chunks(x, c):
    b, l, h, d = x.shape
    return x.reshape(b, l // c, c, h, d).transpose(1, 0, 3, 2, 4)

def from_chunks(x):
    n, b, h, c, d = x.shape
    return x.transpose(1, 0, 3, 2, 4).reshape(b, n * c, h, d)

def gla_chunked(q, k, v, glog, s0):
    c = math.gcd(q.shape[1], GLA_CHUNK)
    causal = jnp.tril(jnp.ones((c, c), bool))[:, :, None]

    def step(S, inp):
        qc, kc, vc, gc = inp
        bcum = jnp.cumsum(gc, axis=2)
        diff = jnp.where(causal, bcum[:, :, :, None, :] - bcum[:, :, None, :, :], -jnp.inf)
        att = jnp.einsum('bhid,bhjd,bhijd->bhij', qc, kc, jnp.exp(diff))
        o = (jnp.einsum('bhij,bhjv->bhiv', att, vc)
             + jnp.einsum('bhid,bhdv->bhiv', qc * jnp.exp(bcum), S))
        b_last = bcum[:, :, -1:, :]
        S = (jnp.exp(b_last[:, :, 0, :, None]) * S
             + jnp.einsum('bhjd,bhjv->bhdv', kc * jnp.exp(b_last - bcum), vc))
        return S, o

    xs = tuple(to_chunks(t.astype(jnp.float32), c) for t in (q, k, v, glog))
    S, o = lax.scan(step, s0.astype(jnp.float32), xs)
    return from_chunks(o), S

def retention_chunked(q, k, v, s0):
    c = math.gcd(q.shape[1], RET_CHUNK)
    h = q.shape[2]
    lg = jnp.log(1.0 - jnp.exp2(-5.0 - jnp.arange(h, dtype=jnp.float32)))
    i = jnp.arange(c, dtype=jnp.float32)
    rel = (i[:, None] - i[None, :])[None]
    dmat = jnp.exp(jnp.where(rel >= 0, rel * lg[:, None, None], -jnp.inf))
    dq = jnp.exp((i + 1.0)[None, :] * lg[:, None])[..., None]
    dk = jnp.exp((c - 1.0 - i)[None, :] * lg[:, None])[..., None]
    ds = jnp.exp(c * lg)[:, None, None]

    def step(S, inp):
        qc, kc, vc = inp
        att = jnp.einsum('bhid,bhjd->bhij', qc, kc) * dmat
        o = (jnp.einsum('bhij,bhjv->bhiv', att, vc)
             + jnp.einsum('bhid,bhdv->bhiv', qc * dq, S))
        S = ds * S + jnp.einsum('bhjd,bhjv->bhdv', kc * dk, vc)
        return S, o

    xs = tuple(to_chunks(t.astype(jnp.float32), c) for t in (q, k, v))
    S, o = lax.scan(step, s0.astype(jnp.float32), xs)
    return from_chunks(o), S

def fox_prompt(q, k, v, logf):
    b, l, h, d = q.shape
    blk = math.gcd(l, FOX_BLOCK)
    nb = l // blk
    F = jnp.cumsum(logf, axis=1).transpose(0, 2, 1)
    kpos = jnp.arange(l)
    qb = q.reshape(b, nb, blk, h, d).transpose(1, 0, 2, 3, 4)
    Fb = F.reshape(b, h, nb, blk).transpose(2, 0, 1, 3)
    scale = d ** -0.5

    def one_block(args):
        qi, Fi, idx = args
        s = (jnp.einsum('bqhd,bkhd->bhqk', qi, k).astype(jnp.float32) * scale
             + (Fi[..., :, None] - F[:, :, None, :]))
        qpos = idx * blk + jnp.arange(blk)
        s = jnp.where(kpos[None, :] <= qpos[:, None], s, -jnp.inf)
        p = jax.nn.softmax(s, axis=-1).astype(v.dtype)
        return jnp.einsum('bhqk,bkhd->bqhd', p, v)

    o = lax.map(one_block, (qb, Fb, jnp.arange(nb)))
    return o.transpose(1, 0, 2, 3, 4).reshape(b, l, h, d)

def fox_sample(q, k, v, logf, k_past, v_past, logf_past):
    l = q.shape[1]
    p_len = k_past.shape[1]
    scale = q.shape[-1] ** -0.5
    gp = jnp.cumsum(logf_past.astype(jnp.float32), axis=1)
    gn = gp[:, -1:] + jnp.cumsum(logf, axis=1)
    gp = gp.transpose(0, 2, 1)
    gn = gn.transpose(0, 2, 1)
    s_past = (jnp.einsum('bqhd,bkhd->bhqk', q, k_past).astype(jnp.float32) * scale
              + (gn[..., :, None] - gp[..., None, :]))
    s_new = (jnp.einsum('bqhd,bkhd->bhqk', q, k).astype(jnp.float32) * scale
             + (gn[..., :, None] - gn[..., None, :]))
    s_new = jnp.where(jnp.tril(jnp.ones((l, l), bool)), s_new, -jnp.inf)
    p = jax.nn.softmax(jnp.concatenate([s_past, s_new], axis=-1), axis=-1)
    return (jnp.einsum('bhqk,bkhd->bqhd', p[..., :p_len].astype(v_past.dtype), v_past)
            + jnp.einsum('bhqk,bkhd->bqhd', p[..., p_len:].astype(v.dtype), v))

def mix_layer(h, pos, lw, conv_buf, gla_s, ret_s, past):
    b, l = h.shape[:2]
    nh, d = N_GROUP_HEADS, HEAD_DIM

    def heads(t):
        return t.reshape(b, l, nh, d)

    z = h @ lw['w_in']
    cuts = np.cumsum(IN_SPLITS)[:-1].tolist()
    (c_a, c_g, f_q, f_k, f_v, f_f, g_q, g_k, g_v, g_lr, g_o,
     r_q, r_k, r_v, r_g) = jnp.split(z, cuts, axis=-1)
    u = c_a * jax.nn.sigmoid(c_g)
    y, conv_new = causal_dwconv(u, conv_buf, lw['conv_w'], lw['conv_b'])
    out_a = jax.nn.silu(layer_norm(y, lw['conv_ln_g'], lw['conv_ln_b']))
    q = rms_norm(heads(f_q), lw['fox_qn_g'])
    k = rms_norm(heads(f_k), lw['fox_kn_g'])
    v = heads(f_v)
    logf = jax.nn.log_sigmoid(f_f.astype(jnp.float32) + lw['fox_fb'].astype(jnp.float32))
    if past is None:
        o_b = fox_prompt(q, k, v, logf)
    else:
        o_b = fox_sample(q, k, v, logf, *past)
    out_b = o_b.reshape(b, l, GROUP_W)
    glog = jax.nn.log_sigmoid((g_lr @ lw['gla_w_gate2'] + lw['gla_b_gate']).astype(jnp.float32)) / GLA_TAU
    o_c, gla_new = gla_chunked(heads(g_q) * HEAD_DIM ** -0.5, heads(g_k), heads(g_v), heads(glog), gla_s)
    out_c = rms_norm(o_c, lw['gla_norm_g'].reshape(nh, d)).reshape(b, l, GROUP_W) * jax.nn.silu(g_o)
    rq = rope(heads(r_q), pos)
    rk = rope(heads(r_k), pos) * HEAD_DIM ** -0.5
    o_d, ret_new = retention_chunked(rq, rk, heads(r_v), ret_s)
    out_d = rms_norm(o_d, lw['ret_norm_g'].reshape(nh, d)).reshape(b, l, GROUP_W) * jax.nn.silu(r_g)
    cat = jnp.concatenate([out_a, out_b, out_c, out_d], axis=-1).astype(h.dtype)
    return cat @ lw['w_out'], conv_new, k, v, logf, gla_new, ret_new

def swiglu(h, w1, w3, w2):
    return (jax.nn.silu(h @ w1) * (h @ w3)) @ w2

def moe(h, router, w1, w3, w2):
    logits = (h @ router).astype(jnp.float32)
    vals, idx = lax.top_k(logits, TOP_K)
    gates = jax.nn.softmax(vals, axis=-1)
    y = jnp.zeros_like(h)
    for e in range(N_EXPERTS):
        g_e = jnp.sum(jnp.where(idx == e, gates, 0.0), axis=-1, keepdims=True).astype(h.dtype)
        y = y + g_e * swiglu(h, w1[e], w3[e], w2[e])
    return y

def block(x, c, pos, lw, ffn, conv_buf, gla_s, ret_s, past):
    mod = jax.nn.silu(c) @ lw['w_ada'] + lw['b_ada']
    sh1, sc1, g1, sh2, sc2, g2 = jnp.split(mod[:, None, :], 6, axis=-1)
    h = rms_norm(x, lw['norm1_g']) * (1 + sc1) + sh1
    mix, conv_new, k, v, logf, gla_new, ret_new = mix_layer(h, pos, lw, conv_buf, gla_s, ret_s, past)
    x = x + g1 * mix
    h = rms_norm(x, lw['norm2_g']) * (1 + sc2) + sh2
    x = x + g2 * ffn(h)
    return x, (conv_new, k, v, logf, gla_new, ret_new)

def setup_inputs(seed: int = 0) -> dict:
    key = jax.random.key(seed)
    ks = iter(jax.random.split(key, 48))
    f32 = jnp.float32

    def nrm(shape, scale):
        return scale * jax.random.normal(next(ks), shape, f32)

    nh, d = N_GROUP_HEADS, HEAD_DIM
    n_pages = PAST_LEN // PAGE_SIZE
    n_used = DEC_BATCH * n_pages
    n_phys = n_used + max(1, n_used // 4)
    n_dense = (DEPTH + 1) // 2
    n_moe = DEPTH // 2
    page_table = jax.random.permutation(next(ks), n_phys)[:n_used].reshape(DEC_BATCH, n_pages).astype(jnp.int32)
    return {
        'x_prompt': nrm((BATCH, SEQ, D_MODEL), 1.0),
        'x_sample': nrm((DEC_BATCH, DEC_SEQ, D_MODEL), 1.0),
        'c_prompt': nrm((BATCH, D_MODEL), 1.0),
        'c_sample': nrm((DEC_BATCH, D_MODEL), 1.0),
        'state_conv': nrm((DEPTH, DEC_BATCH, CONV_K - 1, GROUP_W), 0.5),
        'cache_k': nrm((n_phys, DEPTH, PAGE_SIZE, nh, d), 1.0),
        'cache_v': nrm((n_phys, DEPTH, PAGE_SIZE, nh, d), 1.0),
        'cache_logf': jax.nn.log_sigmoid(3.0 + nrm((n_phys, DEPTH, PAGE_SIZE, nh), 0.5)),
        'state_gla': nrm((DEPTH, DEC_BATCH, nh, d, d), 0.3),
        'state_ret': nrm((DEPTH, DEC_BATCH, nh, d, d), 1.0),
        'page_table': page_table,
        'w_in': nrm((DEPTH, D_MODEL, IN_COLS), D_MODEL ** -0.5),
        'w_out': nrm((DEPTH, MIX_W, D_MODEL), MIX_W ** -0.5),
        'conv_w': nrm((DEPTH, CONV_K, GROUP_W), CONV_K ** -0.5),
        'conv_b': nrm((DEPTH, GROUP_W), 0.02),
        'conv_ln_g': 1.0 + nrm((DEPTH, GROUP_W), 0.02),
        'conv_ln_b': nrm((DEPTH, GROUP_W), 0.02),
        'fox_qn_g': 1.0 + nrm((DEPTH, HEAD_DIM), 0.02),
        'fox_kn_g': 1.0 + nrm((DEPTH, HEAD_DIM), 0.02),
        'fox_fb': 3.0 + nrm((DEPTH, N_GROUP_HEADS), 0.5),
        'gla_w_gate2': nrm((DEPTH, GLA_LR, GROUP_W), GLA_LR ** -0.5),
        'gla_b_gate': nrm((DEPTH, GROUP_W), 0.02),
        'gla_norm_g': 1.0 + nrm((DEPTH, GROUP_W), 0.02),
        'ret_norm_g': 1.0 + nrm((DEPTH, GROUP_W), 0.02),
        'norm1_g': 1.0 + nrm((DEPTH, D_MODEL), 0.02),
        'norm2_g': 1.0 + nrm((DEPTH, D_MODEL), 0.02),
        'w_ada': nrm((DEPTH, D_MODEL, 6 * D_MODEL), 0.5 * D_MODEL ** -0.5),
        'b_ada': nrm((DEPTH, 6 * D_MODEL), 0.02),
        'ffn_w1': nrm((n_dense, D_MODEL, D_FF), D_MODEL ** -0.5),
        'ffn_w3': nrm((n_dense, D_MODEL, D_FF), D_MODEL ** -0.5),
        'ffn_w2': nrm((n_dense, D_FF, D_MODEL), D_FF ** -0.5),
        'moe_router': nrm((n_moe, D_MODEL, N_EXPERTS), D_MODEL ** -0.5),
        'moe_w1': nrm((n_moe, N_EXPERTS, D_MODEL, D_EXPERT), D_MODEL ** -0.5),
        'moe_w3': nrm((n_moe, N_EXPERTS, D_MODEL, D_EXPERT), D_MODEL ** -0.5),
        'moe_w2': nrm((n_moe, N_EXPERTS, D_EXPERT, D_MODEL), D_EXPERT ** -0.5),
    }

def reference(x_prompt, x_sample, c_prompt, c_sample, state_conv, cache_k, cache_v, cache_logf,
              state_gla, state_ret, page_table, w_in, w_out, conv_w, conv_b, conv_ln_g, conv_ln_b,
              fox_qn_g, fox_kn_g, fox_fb, gla_w_gate2, gla_b_gate, gla_norm_g, ret_norm_g,
              norm1_g, norm2_g, w_ada, b_ada, ffn_w1, ffn_w3, ffn_w2,
              moe_router, moe_w1, moe_w3, moe_w2):
    nh, d = N_GROUP_HEADS, HEAD_DIM
    b, l = x_prompt.shape[:2]
    bd, ls = x_sample.shape[:2]
    p_len = page_table.shape[1] * cache_k.shape[2]
    pos_p = jnp.arange(l, dtype=jnp.float32)
    pos_s = p_len + jnp.arange(ls, dtype=jnp.float32)
    conv0 = jnp.zeros((b, CONV_K - 1, GROUP_W), x_prompt.dtype)
    rec0 = jnp.zeros((b, nh, d, d), jnp.float32)
    xp, xs = x_prompt, x_sample
    sp_list, ss_list = [], []
    for li in range(DEPTH):
        lw = {'w_in': w_in[li], 'w_out': w_out[li], 'conv_w': conv_w[li], 'conv_b': conv_b[li],
              'conv_ln_g': conv_ln_g[li], 'conv_ln_b': conv_ln_b[li], 'fox_qn_g': fox_qn_g[li],
              'fox_kn_g': fox_kn_g[li], 'fox_fb': fox_fb[li], 'gla_w_gate2': gla_w_gate2[li],
              'gla_b_gate': gla_b_gate[li], 'gla_norm_g': gla_norm_g[li], 'ret_norm_g': ret_norm_g[li],
              'norm1_g': norm1_g[li], 'norm2_g': norm2_g[li], 'w_ada': w_ada[li], 'b_ada': b_ada[li]}
        if li % 2 == 0:
            ffn = functools.partial(swiglu, w1=ffn_w1[li // 2], w3=ffn_w3[li // 2], w2=ffn_w2[li // 2])
        else:
            ffn = functools.partial(moe, router=moe_router[li // 2], w1=moe_w1[li // 2],
                                    w3=moe_w3[li // 2], w2=moe_w2[li // 2])
        past = (cache_k[page_table, li].reshape(bd, p_len, nh, d),
                cache_v[page_table, li].reshape(bd, p_len, nh, d),
                cache_logf[page_table, li].reshape(bd, p_len, nh))
        xp, sp = block(xp, c_prompt, pos_p, lw, ffn, conv0, rec0, rec0, None)
        xs, ss = block(xs, c_sample, pos_s, lw, ffn, state_conv[li], state_gla[li], state_ret[li], past)
        sp_list.append(sp)
        ss_list.append(ss)
    conv_p = jnp.stack([s[0] for s in sp_list], axis=0)
    conv_s = jnp.stack([s[0] for s in ss_list], axis=0)
    k_p = jnp.stack([s[1] for s in sp_list], axis=1)
    k_s = jnp.stack([s[1] for s in ss_list], axis=1)
    v_p = jnp.stack([s[2] for s in sp_list], axis=1)
    v_s = jnp.stack([s[2] for s in ss_list], axis=1)
    lf_p = jnp.stack([s[3] for s in sp_list], axis=1)
    lf_s = jnp.stack([s[3] for s in ss_list], axis=1)
    gla_p = jnp.stack([s[4] for s in sp_list], axis=0)
    gla_s = jnp.stack([s[4] for s in ss_list], axis=0)
    ret_p = jnp.stack([s[5] for s in sp_list], axis=0)
    ret_s = jnp.stack([s[5] for s in ss_list], axis=0)
    return (xp, xs, conv_p, conv_s, k_p, k_s, v_p, v_s, lf_p, lf_s, gla_p, gla_s, ret_p, ret_s)


_drawn_inputs = setup_inputs


def setup_inputs(seed=0):
    import zlib

    import numpy as np

    out = dict(_drawn_inputs(seed))
    spreads = {}
    factors = {'cache_logf': 8.0,
     'conv_b': 8.0,
     'conv_ln_g': 7.707,
     'conv_ln_b': 7.852,
     'fox_qn_g': 8.0,
     'fox_kn_g': 2.996,
     'gla_b_gate': 6.376,
     'gla_norm_g': 7.136,
     'ret_norm_g': 6.139,
     'norm2_g': 3.845}
    for name, (base, spread) in spreads.items():
        noise = np.random.default_rng([zlib.crc32(name.encode()), seed]).standard_normal(out[name].shape)
        drawn = base * np.exp(spread * noise) if base else spread * noise
        out[name] = __import__('jax').numpy.asarray(drawn.astype(out[name].dtype))
    for name, factor in factors.items():
        out[name] = (out[name] * factor).astype(out[name].dtype)
    return out
```

```python
from contextlib import ExitStack

import concourse.bass as bass
import numpy as np
from concourse import mybir

F32 = mybir.dt.float32
I32 = mybir.dt.int32
U32 = mybir.dt.uint32
ALU = mybir.AluOpType
ACT = mybir.ActivationFunctionType
AX = mybir.AxisListType

P = 128
DM = 1024
KC = DM // P
NP = 256
NS = 8
T = NP + NS
L = 2
NH, HD = 4, 64
GW = NH * HD
KW = 31
LR = 16
CH = 16
NCH = NP // CH
PAGE, NPAGE, NPHYS = 128, 16, 160
TPP = PAGE * NPAGE // P
SUB = PAGE // TPP
DFF = 2816
NE, DE = 8, 3584
CAP = P
NPASS = -(-T // CAP)
EPS = 1e-6
SLOT = 4096
NSLOT = 6
COLS = 512

ZT = {'ca': 0, 'cg': 2, 'fq': 4, 'fk': 6, 'fv': 8, 'ff': 10, 'gq': 11, 'gk': 13, 'gv': 15,
      'glr': 17, 'go': 18, 'rq': 20, 'rk': 22, 'rv': 24, 'rg': 26}
NZ = 28
ZCOL = {'ca': 0, 'cg': 256, 'fq': 512, 'fk': 768, 'fv': 1024, 'ff': 1280, 'gq': 1284, 'gk': 1540,
        'gv': 1796, 'glr': 2052, 'go': 2068, 'rq': 2324, 'rk': 2580, 'rv': 2836, 'rg': 3092}
ZW = {k: GW for k in ZT} | {'ff': NH, 'glr': LR}
ZUNITS = [('fq', 'fk'), ('fv', 'ff'), ('ca', 'cg'), ('gq', 'gk'), ('gv', 'glr'), ('go', 'rq'),
          ('rk', 'rv'), ('rg',)]
ZORDER = []
for _u, _gs in enumerate(ZUNITS):
    for _g in _gs:
        for _c in range(0, ZW[_g], P):
            ZORDER.append((ZT[_g] + _c // P, _u, ZCOL[_g] - ZCOL[_gs[0]] + _c, min(P, ZW[_g] - _c)))
ZPOS = {t[0]: n for n, t in enumerate(ZORDER)}

VCOL, _n = {}, 0
for _k, _w in (('norm1', KC), ('norm2', KC), ('b_ada', 6 * KC), ('conv_b', 2), ('ln_g', 2), ('ln_b', 2),
               ('b_gate', 2), ('gla_g', 2), ('ret_g', 2), ('qn', 1), ('kn', 1), ('fb', 1),
               ('conv_w', 2 * KW)):
    VCOL[_k] = _n
    _n += _w
NV = _n

CCOL, _n = {}, 0
for _k, _w in (('ident', P), ('ones', P), ('heads', P), ('swap', P), ('later', P), ('cos', T), ('sin', T),
               ('reset', NP), ('slot', P), ('row8', NS * P), ('row4', NH * P), ('decay', NH * NP), ('causal', 3 * P),
               ('chunk', 8), ('half', 2), ('dk', 2 * NH), ('gamma', 2), ('eio', NE), ('sub', L)):
    CCOL[_k] = (_n, _w)
    _n += _w
NC = _n

JOBS = [('rms1', 'a')] + [(f'fn{i}', 'a') for i in range(4)]
JOBS += [('tkv0', 'a'), ('tkv1', 'a'), ('tqs', 'a')] + [(f'qb{i}', 'a') for i in range(4)]
JOBS += [(f's{h}', 'v') for h in range(NH)]
for _h in range(NH):
    JOBS += [(f'pt{_h}', 'a'), (f'o{_h}', 'a')]
JOBS += [('snew', 'v'), ('suf', 'v'), ('mxt', 'v'), ('mxb', 'v'), ('sumb', 'v'), ('pv', 'a')]
JOBS += [('mean', 'v'), ('var', 'a')]
JOBS += [('gate0', 'v'), ('gate1', 'v')] + [(f'att{i}', 'v') for i in range(CH)]
JOBS += [('gkv0', 'a'), ('gkv1', 'a'), ('gts', 'a')]
JOBS += [(f'kv{_tt}{_pr}', 'v') for _tt in range(2) for _pr in range(2)]
JOBS += [('gi0', 'v'), ('gi1', 'v'), ('gx0', 'v'), ('gx1', 'v'), ('gs0', 'v'), ('gs1', 'v'),
         ('gn0', 'a'), ('gn1', 'a')]
JOBS += [(f'rr{i}', 'v') for i in range(4)] + [('rkv0', 'a'), ('rkv1', 'a'), ('rts', 'a')]
for _h in range(NH):
    JOBS += [(f'rs{_h}', 'v'), (f'ro{_h}', 'a')]
JOBS += [('rst', 'a'), ('rx0', 'v'), ('rx1', 'v'), ('rd0', 'v'), ('rd1', 'v'), ('rn0', 'a'), ('rn1', 'a'),
         ('rms2', 'a')]
JPOS = {n: i for i, (n, _) in enumerate(JOBS)}
NJ = len(JOBS)
NBANK = 6


def job_no(l, name):
    return l * NJ + JPOS[name]


def divmod_job(n):
    return n // NJ, JOBS[n % NJ][0]


STORES_PER_LAYER = 10
NSTORES = L * STORES_PER_LAYER + 1


def read_no(l, name):
    who = JOBS[JPOS[name]][1]
    per = sum(w == who for _, w in JOBS)
    return who, l * per + sum(w == who for _, w in JOBS[:JPOS[name] + 1])


FB = [(j * COLS, min(COLS, DFF - j * COLS)) for j in range(-(-DFF // COLS))]
EB = DE // COLS


def ring_units():
    order = []
    for l in range(L):
        order += [('ada', l, i) for i in range(6 * DM // COLS)]
        order += [('in', l, 0), ('in', l, 1), ('in', l, 2)]
        for b in range(NS):
            order.append(('k', l, b))
            if b < 5:
                order.append(('in', l, 3 + b))
        order += [('v', l, b) for b in range(NS)]
        order += [('out', l, 0), ('out', l, 1)]
        if l % 2 == 0:
            for j in range(len(FB)):
                order += [('w1', l, j), ('w3', l, j), ('w2', l, j)]
    return order


UNITS = ring_units()
UPOS = {u: n for n, u in enumerate(UNITS)}


def host_constants():
    c = np.zeros((P, NC), np.float32)

    def put(name, a):
        o, w = CCOL[name]
        c[:a.shape[0], o:o + w] = a.reshape(a.shape[0], -1)

    f = np.float32
    put('ident', np.eye(P, dtype=f))
    put('ones', np.ones((P, P), f))
    hd = np.arange(P) // HD
    put('heads', (hd[:, None] == hd[None, :]).astype(f))
    half = HD // 2
    swap = np.zeros((P, P), f)
    for m in range(P):
        if m % HD < half:
            swap[m + half, m] = -1.0
        else:
            swap[m - half, m] = 1.0
    put('swap', swap)
    put('later', (np.arange(P)[:, None] > np.arange(P)[None, :]).astype(f))
    inv = f(10000.0) ** (-np.arange(half, dtype=f) / f(half))
    pos = np.concatenate([np.arange(NP, dtype=f), np.full(NS, f(PAGE * NPAGE), f)])
    ang = (pos[None, :] * inv[:, None]).astype(f)
    put('cos', np.tile(np.cos(ang), (P // half, 1)))
    put('sin', np.tile(np.sin(ang), (P // half, 1)))
    put('reset', np.tile((np.arange(NP) % CH != 0).astype(f), (P, 1)))
    put('slot', np.tile(np.arange(P, dtype=f), (P, 1)))
    put('row8', (np.arange(NS)[:, None, None] == np.arange(NS)[None, :, None]).astype(f) * np.ones((1, 1, P), f))
    put('row4', (np.arange(NH)[:, None, None] == np.arange(NH)[None, :, None]).astype(f) * np.ones((1, 1, P), f))
    lg = np.log(1.0 - np.exp2(-5.0 - np.arange(NH)))
    rel = np.arange(NP)[None, :] - np.arange(P)[:, None]
    put('decay', np.stack([np.where(rel >= 0, np.exp(np.maximum(rel, 0) * g), 0.0) for g in lg], 1).astype(f))
    tri = np.where(np.arange(P)[None, :] <= np.arange(P)[:, None], f(0), f(-1e30))
    put('causal', np.concatenate([tri, np.zeros((P, P), f), tri], 1))
    put('chunk', (np.arange(P)[:, None] // CH == np.arange(8)[None, :]).astype(f))
    put('half', (hd[:, None] == np.arange(2)[None, :]).astype(f))
    tok = np.arange(P)[:, None] + P * np.arange(2)[None, :]
    put('dk', np.exp((NP - 1 - tok)[:, :, None] * lg[None, None, :]).astype(f))
    put('gamma', np.exp(lg).astype(f)[2 * np.arange(2)[None, :] + hd[:, None]])
    put('sub', (np.arange(P)[:, None] % SUB + SUB * np.arange(L)[None, :]).astype(f))
    put('eio', np.tile(np.arange(NE, dtype=f), (P, 1)))
    return c


def trunk_kernel(nc, xT, cT, vt, consts, conv_in, gla_in, ret_in, ptr, cache_k, cache_v, cache_logf,
                 w_in, w_out, w_ada, gate2, ffn_w1, ffn_w3, ffn_w2, router, moe_w1, moe_w3, moe_w2,
                 y_out, conv_out, k_out, v_out, logf_out, gla_out, ret_out):
    ctx = ExitStack()
    with ctx:
        def sb(name, shape, dt=F32):
            return ctx.enter_context(nc.sbuf_tensor(name, shape, dt))

        def sem(name):
            return ctx.enter_context(nc.semaphore(name))

        ring = sb("ring", [P, NSLOT + 1, SLOT])
        C = sb("C", [P, NC])
        VT = sb("VT", [P, L, NV])
        X = sb("X", [P, KC, T])
        H = sb("H", [P, KC, T])
        Z = sb("Z", [P, NZ, T])
        MOD = sb("MOD", [P, 6 * KC, NS + 1])
        CT = sb("CT", [P, KC, NS + 1])
        MA = sb("MA", [P, KC, NS + 1])
        R = sb("R", [P, T])
        PR = sb("PR", [P, NH * P])
        UP = sb("UP", [P, 2, KW - 1 + NP])
        UB = sb("UB", [P, 2, NS, KW])
        TMK = sb("TMK", [P, 2, GW])
        TMV = sb("TMV", [P, 2, GW])
        PT = sb("PT", [P, 3 * P])
        BC = sb("BC", [P, 2, NP])
        O = sb("O", [P, 2, T])
        SG = sb("SG", [P, 2, NS * HD])
        SR = sb("SR", [P, 2, NS * HD])
        G2 = sb("G2", [LR, L, GW])
        RW = sb("RW", [P, KC, NE])
        LF = sb("LF", [NH, T])
        SM = sb("SM", [P, 256])
        IDXI = sb("IDXI", [P, NS], I32)
        IDX = sb("IDX", [P, L, NS], I32)
        DEC = sb("DEC", [P, 2, NCH])[:, :, :]
        MI = sb("MI", [P, 3, 8], U32)
        PASSES = sb("PASSES", [P, 1], I32)

        def c_(name, rows=P, a=0, b=None):
            o, w = CCOL[name]
            return C[0:rows, o + a:o + (w if b is None else b)]

        def v_(l, name, i=0, n=1):
            return VT[:, l, VCOL[name] + i:VCOL[name] + i + n]

        ident, ones, heads = c_('ident'), c_('ones'), c_('heads')
        scr = ring[:, NSLOT, :]
        QB = scr[:, 0:2048].rearrange("p (b f) -> p b f", b=NS)
        RN = scr[:, 0:4 * T].rearrange("p (c t) -> p c t", c=4)
        SQ = scr[:, 2048:2048 + 4 * T].rearrange("p (c t) -> p c t", c=4)
        SC = scr[:, 2048:2560].rearrange("p (b h t) -> p b h t", b=NS, h=NH)
        SUF = scr[:, 2560:3072].rearrange("p (b h t) -> p b h t", b=NS, h=NH)
        LP = scr[:, 3072:3584].rearrange("p (b t h) -> p b t h", b=NS, t=TPP)
        PS = scr[:, 0:NH * 3 * P].rearrange("p (h c) -> p h c", h=NH)
        VX = scr[:, 0:2048].rearrange("p (h n v) -> p h n v", h=NH, n=8)
        SH = scr[:, 2048:4096].rearrange("p (c n v) -> p c n v", c=2, n=NCH)
        VE = scr[0:NS, 0:2048].rearrange("p (h b v) -> p h b v", h=NH, b=NS)
        EX = [scr[:, 2048 + 512 * i:2560 + 512 * i] for i in range(2)]
        WX = [scr[:, 3072 + 512 * i:3584 + 512 * i] for i in range(2)]
        TA = [scr[:, 512 * i:512 + 512 * i] for i in range(2)]
        TA2 = scr[:, 1024:1024 + 2 * T].rearrange("p (c t) -> p c t", c=2)
        GM = scr[:, 0:2 * T].rearrange("p (c t) -> p c t", c=2)
        GA = scr[:, 2 * T:4 * T].rearrange("p (c t) -> p c t", c=2)
        BCT, RNG = GM, GA
        GX = Z[:, ZT['cg']:ZT['cg'] + 2, :]
        GQD = Z[:, ZT['fq']:ZT['fq'] + 2, 0:NP]
        GKD = Z[:, ZT['fk']:ZT['fk'] + 2, 0:NP]
        PR4 = PR[:, :].rearrange("p (b h t) -> p b h t", b=NS, h=NH)
        CAT = H
        QS = PT[0:NS, 0:GW]
        KV8 = PR[0:NS, :]
        FX = Z[0:NH, ZT['ff'], :]
        FS = TMK[0:NH].rearrange("p a b -> p (a b)")[:, 0:T]
        SG4 = SG[:, :, :].rearrange("p c (b v) -> p c b v", b=NS)
        SR4 = SR[:, :, :].rearrange("p c (b v) -> p c b v", b=NS)
        AB = Z[:, 8:20, :].rearrange("p (i t) n -> p i t n", i=3)
        Y = Z[:, 20:28, :]
        SA = [SG[:, 0, 0:T], SG[:, 1, 0:T], SR[:, 0, 0:T], SR[:, 1, 0:T]]
        HT = Z[:, 0:12, :].rearrange("p z t -> p (z t)")[:, 0:3 * DM].rearrange("p (a f) -> p a f", a=3)
        HG = Z[:, 12:20, :].rearrange("p z t -> p (z t)")[:, 0:DM].rearrange("p (c s) -> p c s", c=KC)
        SLG = Z[:, 16, 0:2 * 3 * (NE + 1)].rearrange("p (i a e) -> p i a e", i=2, a=3)
        SILU = [SG[:, i, :] for i in range(2)]
        AM = [SR[:, i, :] for i in range(2)]
        AT = [t.rearrange("p (k s) -> p k s", k=4)
              for t in (PR[:, :], TMK[:, :, :].rearrange("p a b -> p (a b)"))]
        YS = H[:, :, :].rearrange("p c t -> p (c t)")[:, 0:DM]
        SEL = PT[:, :].rearrange("p (a s) -> p a s", a=3)
        GSEL = UP[:, :, :].rearrange("p c t -> p (c t)")[:, 0:3 * P].rearrange("p (a s) -> p a s", a=3)
        GST = O[:, :, :].rearrange("p c t -> p (c t)")[:, 0:T]

        def small(a, n=1, rows=P):
            return SM[0:rows, a:a + n]

        EPSB = small(250)
        def RP(h):
            return scr[:, 1024 + 3 * P * (h % 2):1024 + 3 * P * (h % 2 + 1)]

        def MASK(tt, n):
            return small(128 + NE * tt, NE, n)

        psum = [ctx.enter_context(nc.psum_tensor(f"bank{i}", [P, 512], F32)) for i in range(8)]

        slot_full = [sem(f"slot_full{i}") for i in range(NSLOT + 1)]
        pages_full = [sem(f"pages_full{i}") for i in range(NSLOT)]
        consts_in = sem("consts_in")
        states_in = sem("states_in")
        page_idx = sem("page_idx")
        logf_in = sem("logf_in")
        ada_done = sem("ada_done")
        mod_part = sem("mod_part")
        mod_ready = sem("mod_ready")
        z_done = sem("z_done")
        z_ready = sem("z_ready")
        job_done = sem("job_done")
        job_read = {'a': sem("job_read_act"), 'v': sem("job_read_dve")}
        k_used = sem("k_used")
        out_done = sem("out_done")
        out_added = sem("out_added")
        gu_done = sem("gu_done")
        silu_ready = sem("silu_ready")
        a_ready = sem("a_ready")
        y_done = sem("y_done")
        y_added = sem("y_added")
        h_turned, ht_ready = sem("h_turned"), sem("ht_ready")
        router_done, gates_read, masks_ready = sem("router_done"), sem("gates_read"), sem("masks_ready")
        passes_ready, slots_ready = sem("passes_ready"), sem("slots_ready")
        gather_done, gathered = sem("gather_done"), sem("gathered")
        gst_done, gst_ready = sem("gate_turn_done"), sem("gate_turned")
        egu_done, esilu_ready, ea_ready = sem("expert_gu_done"), sem("expert_silu"), sem("expert_act")
        turn_done, turned = sem("act_turn_done"), sem("act_turned")
        down_done, y_copied = sem("down_done"), sem("y_copied")
        sel_ready, slots_moved = sem("sel_ready"), sem("slots_moved")
        scatter_done, scattered = sem("scatter_done"), sem("scattered")
        stored = sem("stored")
        k_stored = sem("k_stored")
        ev_pv = sem("v_used")
        ev_ffln = sem("fox_ln")
        idx_ready = sem("idx_ready")
        dve_chain = sem("dve_chain")
        act_chain = sem("act_chain")
        pool_chain = sem("pool_chain")
        ct_ready = sem("ct_ready")
        ev = {n: sem(n) for n in (
            "squares1", "h1", "fox_squares", "fox_qk", "fox_logf", "k_phase", "probs_max", "probs_exp", "probs",
            "row_terms", "past_totals", "max_part", "max_diag", "dec_shift", "dec_exp", "dec_sum", "dec_probs",
            "glu_gate", "glu", "conv_y", "conv_sq", "conv_rstd", "conv_out", "gla_x", "gla_abs", "gla_ln", "gla_b", "gla_decays",
            "gla_kq", "lag_diff", "lag_exp", "lag_w", "gla_vx", "gla_states", "ve_gla", "s_gla", "o_gla", "gla_sq",
            "gla_rn", "gate_silu", "gla_cat", "rope", "ret_p", "ret_kd", "ve_ret", "s_ret", "o_ret", "ret_sq", "ret_rn", "cat",
            "squares2", "h2", "x_final", "fox_o", "ff_exp")}

        block = ctx.enter_context(nc.Block())

        def unit(u):
            return ring[:, UPOS[u] % NSLOT, :]

        def unit_full(u):
            n, pages = UPOS[u], u[0] in 'kv'
            count = sum((v[0] in 'kv') == pages for v in UNITS[n % NSLOT:n + 1:NSLOT])
            return (pages_full if pages else slot_full)[n % NSLOT], 16 * count

        def wait_unit(eng, u):
            eng.wait_ge(*unit_full(u))

        def z_unit_end(l, i):
            return l * NZ + max(n for n, t in enumerate(ZORDER) if t[1] == i) + 1

        def wait_unit_used(eng, u):
            kind, l, i = u
            if kind == 'ada':
                eng.wait_ge(ada_done, l * 12 + i + 1)
            elif kind == 'in':
                eng.wait_ge(z_done, z_unit_end(l, i))
            elif kind == 'k':
                eng.wait_ge(k_used, l * NS + i + 1)
            elif kind == 'v':
                eng.wait_ge(ev_pv, l * NS + i + 1)
            elif kind == 'out':
                eng.wait_ge(out_done, l * KC + 4 * (i + 1))
            elif kind in ('w1', 'w3'):
                eng.wait_ge(gu_done, sum(w // P for _, w in FB[:i + 1]))
            else:
                eng.wait_ge(y_done, KC * (i + 1))


        def wait_slot_free(eng, u):
            n = UPOS[u]
            if n >= NSLOT:
                wait_unit_used(eng, UNITS[n - NSLOT])

        def bank(l, name):
            return psum[2 + job_no(l, name) % NBANK]

        class Chain:

            def __init__(self, eng, semaphore):
                self.eng, self.sem, self.n = eng, semaphore, 0

            def add(self, ins):
                self.n += 1
                ins.then_inc(self.sem, 1)

            def wait(self):
                self.eng.wait_ge(self.sem, self.n)

            def __call__(self, ins):
                self.add(ins)
                self.wait()

        nstored = [0]

        def store(eng, dst, src):
            nstored[0] += 1
            eng.dma_start(dst, src).then_inc(stored, 16)

        @block.sync
        def _(sp):
            for dst, src in ((C[:, :], consts), (VT[:, :, :], vt), (CT[:, :, :], cT), (X[:, :, :], xT),
                             (G2[:, :, :], gate2.rearrange("l r n -> r l n")),
                             (RW[:, :, :], router.rearrange("(c p) e -> p c e", p=P))):
                sp.dma_start(dst, src).then_inc(consts_in, 16)
            for u in UNITS:
                kind, l, i = u
                if kind in 'kv':
                    continue
                wait_slot_free(sp, u)
                dst, full = unit(u), unit_full(u)[0]
                if kind == 'ada':
                    w, n = w_ada[l, :, i * COLS:(i + 1) * COLS], COLS
                elif kind == 'in':
                    n = sum(ZW[g] for g in ZUNITS[i])
                    w = w_in[l, :, ZCOL[ZUNITS[i][0]]:ZCOL[ZUNITS[i][0]] + n]
                elif kind == 'out':
                    w, n = w_out[l, :, i * COLS:(i + 1) * COLS], COLS
                elif kind in ('w1', 'w3'):
                    a, n = FB[i]
                    w = (ffn_w1 if kind == 'w1' else ffn_w3)[l // 2, :, a:a + n]
                else:
                    a, k = FB[i]
                    sp.dma_start(dst[:, 0:k // P * DM].rearrange("p (c n) -> p c n", n=DM),
                                 ffn_w2[l // 2, a:a + k, :].rearrange("(c p) n -> p c n", p=P)).then_inc(full, 16)
                    continue
                sp.dma_start(dst[:, 0:KC * n].rearrange("p (c n) -> p c n", n=n),
                             w.rearrange("(c p) n -> p c n", p=P)).then_inc(full, 16)

            def expert_unit(e, u):
                kind, j = u % 3, u // 3
                dst = ring[:, u % (NSLOT + 1), :]
                if kind < 2:
                    w = (moe_w1, moe_w3)[kind][0, bass.ds(e, 1), :, j * COLS:(j + 1) * COLS]
                    src, n = w.rearrange("e (c p) n -> p (e c) n", p=P), COLS
                else:
                    w = moe_w2[0, bass.ds(e, 1), j * COLS:(j + 1) * COLS, :]
                    src, n = w.rearrange("e (c p) n -> p (e c) n", p=P), DM
                sp.dma_start(dst.rearrange("p (c n) -> p c n", n=n), src).then_inc(slot_full[u % (NSLOT + 1)], 16)

            def expert_slot_free(p, e, u):
                kind, j = (u - 7) % 3, (u - 7) // 3
                if kind < 2:
                    sp.wait_ge(egu_done, p * (NE * 2 * EB) + e * (2 * EB) + 2 * j + kind + 1)
                else:
                    sp.wait_ge(down_done, p * (NE * 2 * EB) + e * (2 * EB) + 2 * j + 2)

            for s in range(NSLOT):
                wait_unit_used(sp, [u for n, u in enumerate(UNITS) if n % NSLOT == s][-1])
                expert_unit(0, s)
            sp.wait_ge(ev["cat"], L)
            sp.wait_ge(out_added, L * KC)
            sp.wait_ge(stored, 16 * L * STORES_PER_LAYER)
            expert_unit(0, NSLOT)
            sp.wait_ge(passes_ready, 1)
            passes = sp.value_load(PASSES[0:1, 0:1], min_val=1, max_val=NPASS)
            with sp.Fori(0, NPASS) as p:
                with sp.If(p < passes):
                    with sp.Fori(0, NE - 1) as e:
                        for u in range(7, 28):
                            expert_slot_free(p, e, u)
                            expert_unit(e if u < 21 else e + 1, u % 21)
                    for u in range(7, 21):
                        expert_slot_free(p, NE - 1, u)
                        expert_unit(NE - 1, u)
                    with sp.If(p + 1 < passes):
                        for u in range(21, 28):
                            expert_slot_free(p, NE - 1, u)
                            expert_unit(0, u % 21)
            sp.wait_ge(stored, 16 * NSTORES)

        @block.gpsimd
        def _(pool):
            chain = Chain(pool, pool_chain)
            pool.dma_start(IDXI[:, :], ptr).then_inc(page_idx, 16)
            chain(nc.gpsimd.memset(UP[:, :, 0:KW - 1], 0.0))
            pool.wait_ge(idx_ready, L)

            def gather_logf(l):
                pool.wait_ge(ev["fox_qk"], l + 1)
                for b in range(NS):
                    nc.gpsimd.indirect_dma_start(
                        scr[:, 3072 + b * TPP * NH:3072 + (b + 1) * TPP * NH], None,
                        cache_logf.rearrange("n l (s t) h -> (n l s) (t h)", t=TPP),
                        bass.IndirectOffsetOnAxis(ap=IDX[:, l, b:b + 1], axis=0)).then_inc(logf_in, 16)

            for l in range(L):
                if l:
                    pool.wait_ge(ev["cat"], l)
                    pool.wait_ge(stored, 16 * STORES_PER_LAYER * l)
                    pool.wait_ge(a_ready, DFF // P)
                for c in range(2):
                    pool.dma_start(UB[:, c, :, 0:KW - 1], conv_in[l, :, c]).then_inc(states_in, 16)
                pool.dma_start(SG[:, :, :], gla_in[l]).then_inc(states_in, 16)
                pool.dma_start(SR[:, :, :], ret_in[l]).then_inc(states_in, 16)
                for kind, cache in (('k', cache_k), ('v', cache_v)):
                    rows = cache.rearrange("n l (s t) h d -> (n l s) (t h d)", t=TPP)
                    for b in range(NS):
                        u = (kind, l, b)
                        wait_slot_free(pool, u)
                        nc.gpsimd.indirect_dma_start(
                            unit(u), None, rows,
                            bass.IndirectOffsetOnAxis(ap=IDX[:, l, b:b + 1], axis=0)
                        ).then_inc(unit_full(u)[0], 16)
                        if (kind, b) == ('k', 2):
                            gather_logf(l)

        @block.tensor
        def _(pe):
            mm = nc.tensor.matmul

            def open_job(l, name):
                n = job_no(l, name)
                if n >= NBANK:
                    who, count = read_no(*divmod_job(n - NBANK))
                    pe.wait_ge(job_read[who], count)
                return psum[2 + n % NBANK]

            def close(ins):
                ins.then_inc(job_done, 1)

            def one(l, name, lhsT, rhs, rows=P, at=0):
                b = open_job(l, name)
                n = rhs.free_size()
                close(mm(b[at:at + rows, 0:n], lhsT, rhs, start=True, stop=True))

            def norm_sum(l, name, src):
                b = open_job(l, name)
                for c in range(KC):
                    ins = mm(b[:, 0:T], ones, src[:, c, :], start=(c == 0), stop=(c == KC - 1))
                close(ins)

            def project(l, i):
                wait_unit(pe, ('in', l, i))
                n = sum(ZW[g] for g in ZUNITS[i])
                w = unit(('in', l, i))[:, 0:KC * n].rearrange("p (c n) -> p c n", n=n)
                for pos, (z, u, col, m) in enumerate(ZORDER):
                    if u != i:
                        continue
                    if l * NZ + pos >= 2:
                        pe.wait_ge(z_ready, l * NZ + pos - 1)
                    for c in range(KC):
                        ins = mm(psum[pos % 2][0:m, 0:T], w[:, c, col:col + m], H[:, c, :],
                                 start=(c == 0), stop=(c == KC - 1))
                    ins.then_inc(z_done, 1)

            def turn(out, src, rows):
                return nc.tensor.transpose(out, src, ident[0:rows, 0:rows])

            def token_major(l, name, tt, tiles):
                b = open_job(l, name)
                for n, src in enumerate(tiles):
                    ins = turn(b[:, n * P:(n + 1) * P], src[:, tt * P:(tt + 1) * P], P)
                close(ins)

            def sample_outer(l, names, kcol):
                for pr in range(2):
                    b = open_job(l, names[pr])
                    for s in range(2):
                        h = 2 * pr + s
                        ins = mm(b[s * HD:(s + 1) * HD, :], KV8[:, kcol + h * HD:kcol + (h + 1) * HD],
                                 VE[:, h].rearrange("p b v -> p (b v)"), start=True, stop=True)
                    close(ins)

            def sample_read(l, names, S4, q):
                for s in range(2):
                    b = open_job(l, names[s])
                    for pr in range(2):
                        for i in range(NS):
                            ins = mm(b[s * HD:(s + 1) * HD, pr * NS + i:pr * NS + i + 1],
                                     S4[s * HD:(s + 1) * HD, pr, i, :],
                                     q[s * HD:(s + 1) * HD, pr, NP + i:NP + i + 1], start=True, stop=True)
                    close(ins)

            pe.wait_ge(consts_in, 16 * 6)
            for l in range(L):
                pe.wait_ge(ct_ready, 1)
                if l:
                    pe.wait_ge(mod_ready, l)
                for i in range(12):
                    wait_unit(pe, ('ada', l, i))
                    w = unit(('ada', l, i)).rearrange("p (c n) -> p c n", n=COLS)
                    for m in range(4):
                        o = (4 * i + m) * (NS + 1)
                        for c in range(KC):
                            ins = mm(psum[0][:, o:o + NS + 1], w[:, c, m * P:(m + 1) * P], CT[:, c, :],
                                     start=(c == 0), stop=(c == KC - 1))
                    ins.then_inc(ada_done, 1)
                pe.wait_ge(ev["squares1"], l + 1)
                norm_sum(l, 'rms1', H)
                pe.wait_ge(ev["h1"], l + 1)
                pe.wait_ge(mod_ready, l + 1)
                for i in range(3):
                    project(l, i)
                pe.wait_ge(ev["fox_squares"], l + 1)
                for i in range(4):
                    one(l, f'fn{i}', heads, SQ[:, i, :])
                pe.wait_ge(ev["fox_qk"], l + 1)
                fk = Z[:, ZT['fk']:ZT['fk'] + 2, :]
                fq = Z[:, ZT['fq']:ZT['fq'] + 2, :]
                fv = Z[:, ZT['fv']:ZT['fv'] + 2, :]
                for tt in range(2):
                    token_major(l, f'tkv{tt}', tt, (fv[:, 0, :], fv[:, 1, :]))
                b = open_job(l, 'tqs')
                for n in range(2):
                    ins = turn(b[0:NS, n * P:(n + 1) * P], fq[:, n, NP:T], P)
                close(ins)
                for i in range(4):
                    b = open_job(l, f'qb{i}')
                    if i == 0:
                        who, count = read_no(l, 'tqs')
                        pe.wait_ge(job_read[who], count)
                    for n in range(2):
                        ins = mm(b[:, n * GW:(n + 1) * GW], c_('row8', NS, (2 * i + n) * P, (2 * i + n + 1) * P),
                                 QS[:, :], start=True, stop=True)
                    close(ins)
                for i in range(3, 8):
                    project(l, i)
                pe.wait_ge(ev["fox_logf"], l + 1)
                for h in range(NH):
                    c, s = h // 2, (h % 2) * HD
                    b = open_job(l, f's{h}')
                    row = c_('row4', NH, h * P, (h + 1) * P)
                    for at, qt, kt in ((0, 0, 0), (P, 1, 0), (2 * P, 1, 1)):
                        o = b[:, at:at + P]
                        mm(o, fq[s:s + HD, c, qt * P:(qt + 1) * P], fk[s:s + HD, c, kt * P:(kt + 1) * P],
                           start=True, stop=False)
                        mm(o, FS[:, qt * P:(qt + 1) * P], row, start=False, stop=False)
                        ins = mm(o, row, FX[:, kt * P:(kt + 1) * P], start=False, stop=True)
                    close(ins)
                for h in range(NH):
                    c, s = h // 2, (h % 2) * HD
                    pe.wait_ge(ev["probs"], l * NH + h + 1)
                    b = open_job(l, f'pt{h}')
                    for at in range(3):
                        ins = turn(b[:, at * P:(at + 1) * P], PS[:, h, at * P:(at + 1) * P], P)
                    close(ins)
                    b = open_job(l, f'o{h}')
                    who, count = read_no(l, f'pt{h}')
                    pe.wait_ge(job_read[who], count)
                    o = b[s:s + HD, :]
                    mm(o[:, 0:NP], TMV[:, 0, h * HD:(h + 1) * HD], PT[:, 0:NP], start=True, stop=False)
                    close(mm(o[:, P:NP], TMV[:, 1, h * HD:(h + 1) * HD], PT[:, NP:3 * P], start=False, stop=True))
                pe.wait_ge(ev["row_terms"], l + 1)
                one(l, 'snew', ones, small(64, 32))
                pe.wait_ge(ev["past_totals"], l + 1)
                b = open_job(l, 'suf')
                mm(b[:, 0:32], c_('later'), small(96, 32), start=True, stop=False)
                close(mm(b[:, 0:32], c_('ones', NH), small(128, 32, NH), start=False, stop=True))
                pe.wait_ge(ev["max_part"], l + 1)
                b = open_job(l, 'mxt')
                close(turn(b[0:32, 0:P], small(160, 32), P))
                pe.wait_ge(ev["max_diag"], l + 1)
                one(l, 'mxb', c_('ones', 32), small(192, 32, 32))
                pe.wait_ge(ev["dec_sum"], l + 1)
                one(l, 'sumb', ones, small(64, 32))
                pe.wait_ge(ev["dec_probs"], l + 1)
                b = open_job(l, 'pv')
                for i in range(NS):
                    wait_unit(pe, ('v', l, i))
                    v = unit(('v', l, i)).rearrange("p (t f) -> p t f", t=TPP)
                    for c in range(2):
                        o = (2 * i + c) * 2
                        for t in range(TPP):
                            ins = mm(b[:, o:o + 2], v[:, t, c * P:(c + 1) * P], PR4[:, i, 2 * c:2 * c + 2, t],
                                     start=(t == 0), stop=(t == TPP - 1))
                    ins.then_inc(ev_pv, 1)
                close(nc.tensor.matmul(b[:, 64:65], ident, ident[:, 0:1], start=True, stop=True))
                cy = Z[:, ZT['ca']:ZT['ca'] + 2, :]
                pe.wait_ge(ev["conv_y"], l + 1)
                b = open_job(l, 'mean')
                for c in range(2):
                    ins = mm(b[:, 0:T], ones, cy[:, c, :], start=(c == 0), stop=(c == 1))
                close(ins)
                pe.wait_ge(ev["conv_sq"], l + 1)
                b = open_job(l, 'var')
                for c in range(2):
                    ins = mm(b[:, 0:T], ones, TA2[:, c, :], start=(c == 0), stop=(c == 1))
                close(ins)
                gv = Z[:, ZT['gv']:ZT['gv'] + 2, :]
                gq = Z[:, ZT['gq']:ZT['gq'] + 2, :]
                gk = Z[:, ZT['gk']:ZT['gk'] + 2, :]
                for c in range(2):
                    one(l, f'gate{c}', G2[:, l, c * P:(c + 1) * P], Z[0:LR, ZT['glr'], :])
                for lag in range(CH):
                    pe.wait_ge(ev["lag_w"], l * CH + lag + 1)
                    b = open_job(l, f'att{lag}')
                    n = NCH * (CH - lag)
                    for c in range(2):
                        ins = mm(b[:, c * n:(c + 1) * n], heads, WX[lag % 2][:, c * n:(c + 1) * n],
                                 start=True, stop=True)
                    close(ins)
                pe.wait_ge(ev["gla_kq"], l + 1)
                for tt in range(2):
                    token_major(l, f'gkv{tt}', tt, (GKD[:, 0, :], GKD[:, 1, :], gv[:, 0, :], gv[:, 1, :]))
                b = open_job(l, 'gts')
                for n, src in enumerate((gk[:, 0, NP:T], gk[:, 1, NP:T], gv[:, 0, NP:T], gv[:, 1, NP:T])):
                    ins = turn(b[0:NS, n * P:(n + 1) * P], src, P)
                close(ins)
                for tt in range(2):
                    pe.wait_ge(ev["gla_vx"], l * 2 + tt + 1)
                    for pr in range(2):
                        b = open_job(l, f'kv{tt}{pr}')
                        for s in range(2):
                            h = 2 * pr + s
                            ins = mm(b[s * HD:(s + 1) * HD, :], TMK[:, tt, h * HD:(h + 1) * HD],
                                     VX[:, h].rearrange("p n v -> p (n v)"), start=True, stop=True)
                        close(ins)
                pe.wait_ge(ev["gla_states"], l + 1)
                for s in range(2):
                    b = open_job(l, f'gi{s}')
                    for pr in range(2):
                        for n in range(1, NCH):
                            o = pr * NP + n * CH
                            ins = mm(b[s * HD:(s + 1) * HD, o:o + CH], SH[s * HD:(s + 1) * HD, pr, n - 1, :],
                                     GQD[s * HD:(s + 1) * HD, pr, n * CH:(n + 1) * CH], start=True, stop=True)
                    close(ins)
                pe.wait_ge(ev["ve_gla"], l + 1)
                sample_outer(l, ('gx0', 'gx1'), 0)
                pe.wait_ge(ev["s_gla"], l + 1)
                sample_read(l, ('gs0', 'gs1'), SG4, gq)
                pe.wait_ge(ev["gla_sq"], l + 1)
                for c in range(2):
                    one(l, f'gn{c}', heads, BCT[:, c, :])
                rv = Z[:, ZT['rv']:ZT['rv'] + 2, :]
                rq = Z[:, ZT['rq']:ZT['rq'] + 2, :]
                rk = Z[:, ZT['rk']:ZT['rk'] + 2, :]
                for i in range(4):
                    one(l, f'rr{i}', c_('swap'), Z[:, ZT['rq'] + i, :])
                pe.wait_ge(ev["rope"], l + 1)
                for tt in range(2):
                    token_major(l, f'rkv{tt}', tt, (rk[:, 0, :], rk[:, 1, :], rv[:, 0, :], rv[:, 1, :]))
                b = open_job(l, 'rts')
                for n, src in enumerate((rk[:, 0, NP:T], rk[:, 1, NP:T], rv[:, 0, NP:T], rv[:, 1, NP:T])):
                    ins = turn(b[0:NS, n * P:(n + 1) * P], src, P)
                close(ins)
                who, count = read_no(l, 'rts')
                pe.wait_ge(job_read[who], count)
                for h in range(NH):
                    c, s = h // 2, (h % 2) * HD
                    b = open_job(l, f'rs{h}')
                    mm(b[:, 0:NP], rk[s:s + HD, c, 0:P], rq[s:s + HD, c, 0:NP], start=True, stop=True)
                    close(mm(b[:, NP:3 * P], rk[s:s + HD, c, P:NP], rq[s:s + HD, c, P:NP], start=True, stop=True))
                    pe.wait_ge(ev["ret_p"], l * NH + h + 1)
                    b = open_job(l, f'ro{h}')
                    o = b[s:s + HD, :]
                    mm(o[:, 0:NP], TMV[:, 0, h * HD:(h + 1) * HD], RP(h)[:, 0:NP], start=True, stop=False)
                    close(mm(o[:, P:NP], TMV[:, 1, h * HD:(h + 1) * HD], RP(h)[:, NP:3 * P], start=False, stop=True))
                pe.wait_ge(ev["ret_kd"], l + 1)
                b = open_job(l, 'rst')
                for h in range(NH):
                    c, s = h // 2, (h % 2) * HD
                    for tt in range(2):
                        ins = mm(b[s:s + HD, c * HD:(c + 1) * HD], TMK[:, tt, h * HD:(h + 1) * HD],
                                 TMV[:, tt, h * HD:(h + 1) * HD], start=(tt == 0), stop=(tt == 1))
                close(ins)
                pe.wait_ge(ev["ve_ret"], l + 1)
                sample_outer(l, ('rx0', 'rx1'), 0)
                pe.wait_ge(ev["s_ret"], l + 1)
                sample_read(l, ('rd0', 'rd1'), SR4, rq)
                pe.wait_ge(ev["ret_sq"], l + 1)
                for c in range(2):
                    one(l, f'rn{c}', heads, BCT[:, c, :])
                pe.wait_ge(ev["cat"], l + 1)
                for m in range(KC):
                    if m % 4 == 0:
                        wait_unit(pe, ('out', l, m // 4))
                    w = unit(('out', l, m // 4)).rearrange("p (c n) -> p c n", n=COLS)
                    if m >= 2:
                        pe.wait_ge(out_added, l * KC + m - 1)
                    for c in range(KC):
                        ins = mm(psum[m % 2][:, 0:T], w[:, c, (m % 4) * P:(m % 4 + 1) * P], CAT[:, c, :],
                                 start=(c == 0), stop=(c == KC - 1))
                    ins.then_inc(out_done, 1)
                pe.wait_ge(ev["squares2"], l + 1)
                norm_sum(l, 'rms2', Z[:, 0:KC, :])
                pe.wait_ge(ev["h2"], l + 1)
                if l % 2 == 0:
                    tiles = 0
                    for j in range(len(FB) + 1):
                        if j < len(FB):
                            a, n = FB[j]
                            wait_unit(pe, ('w1', l, j))
                            wait_unit(pe, ('w3', l, j))
                            for t in range(n // P):
                                if tiles >= 2:
                                    pe.wait_ge(a_ready, tiles - 1)
                                for k, kind in enumerate(('w1', 'w3')):
                                    w = unit((kind, l, j))[:, 0:KC * n].rearrange("p (c n) -> p c n", n=n)
                                    for c in range(KC):
                                        ins = mm(psum[2 * (tiles % 2) + k][:, 0:T], w[:, c, t * P:(t + 1) * P],
                                                 H[:, c, :], start=(c == 0), stop=(c == KC - 1))
                                ins.then_inc(gu_done, 1)
                                tiles += 1
                        if j >= 1:
                            i = j - 1
                            nk = FB[i][1] // P
                            wait_unit(pe, ('w2', l, i))
                            pe.wait_ge(a_ready, sum(w // P for _, w in FB[:j]))
                            w = unit(('w2', l, i))[:, 0:nk * DM].rearrange("p (c n) -> p c n", n=DM)
                            for m in range(KC):
                                if KC * i + m >= 4:
                                    pe.wait_ge(y_added, KC * i + m - 3)
                                for k in range(nk):
                                    ins = mm(psum[4 + m % 4][:, 0:T], w[:, k, m * P:(m + 1) * P],
                                             AB[:, i % 3, k, :], start=(k == 0), stop=(k == nk - 1))
                                ins.then_inc(y_done, 1)
                else:
                    rows = (P, P, NS)
                    for tt, n in enumerate(rows):
                        for c in range(KC):
                            ins = mm(psum[0][0:n, tt * NE:(tt + 1) * NE], H[:, c, tt * P:tt * P + n], RW[:, c, :],
                                     start=(c == 0), stop=(c == KC - 1))
                    ins.then_inc(router_done, 1)
                    pe.wait_ge(out_added, l * KC + KC)
                    for i in range(6):
                        tt, half = i // 2, i % 2
                        n = rows[tt]
                        for q in range(4):
                            ins = turn(psum[2 + i][0:n, q * P:(q + 1) * P], H[:, 4 * half + q, tt * P:tt * P + n], P)
                        ins.then_inc(h_turned, 1)
                    pe.wait_ge(masks_ready, 3)
                    for tt, n in enumerate(rows):
                        o = psum[1][0:n, tt * NE:(tt + 1) * NE]
                        mm(o, c_('later', n, 0, n), MASK(tt, n), start=True, stop=(tt == 2))
                        for t2 in range(tt + 1, 3):
                            mm(o, c_('ones', rows[t2], 0, n), MASK(t2, rows[t2]), start=False, stop=(t2 == 2))
                    for tt, n in enumerate(rows):
                        ins = mm(psum[1][:, 3 * NE:4 * NE], c_('ones', n), MASK(tt, n), start=(tt == 0), stop=(tt == 2))
                    ins.then_inc(router_done, 1)
                    pe.wait_ge(ht_ready, 6)
                    pe.wait_ge(passes_ready, 1)
                    passes = pe.value_load(PASSES[0:1, 0:1], min_val=1, max_val=NPASS)

                    def expert(p, e):
                        def at(per, n):
                            return p * (NE * per) + e * per + n

                        def full(u):
                            s = u % (NSLOT + 1)
                            before = sum(v[0] not in 'kv' for v in UNITS[s::NSLOT]) if s < NSLOT else 0
                            pe.wait_ge(slot_full[s], at(16 * 3, 16 * (before + u // (NSLOT + 1) + 1)))

                        pe.wait_ge(slots_ready, at(1, 1))
                        for half in range(2):
                            pe.wait_ge(scattered, at(KC, 7 + half))
                            for q in range(4):
                                c = 4 * half + q
                                for tt, n in enumerate(rows):
                                    ins = mm(psum[6 + half][:, q * P:(q + 1) * P], HT[0:n, tt, c * P:(c + 1) * P],
                                             SEL[0:n, tt, :], start=(tt == 0), stop=(tt == 2))
                            ins.then_inc(gather_done, 1)
                        pe.wait_ge(gathered, at(2, 1))
                        for tt, n in enumerate(rows):
                            ins = turn(psum[6][:, tt * P:tt * P + n], GSEL[0:n, tt, :], n)
                        ins.then_inc(gst_done, 1)

                        def down(j):
                            pe.wait_ge(ea_ready, at(EB, j + 2))
                            pe.wait_ge(*((gathered, at(2, 2)), (gst_ready, at(1, 1)))[j] if j < 2
                                       else (turned, at(EB, j - 1)))
                            for k in range(4):
                                ins = turn(psum[6 + (j + 1) % 2][:, k * P:(k + 1) * P], AM[j % 2][:, k * P:(k + 1) * P], P)
                            ins.then_inc(turn_done, 1)
                            full(3 * j + 2)
                            pe.wait_ge(turned, at(EB, j + 1))
                            w = ring[:, (3 * j + 2) % (NSLOT + 1), :].rearrange("p (c n) -> p c n", n=DM)
                            for half in range(2):
                                if j == 0:
                                    pe.wait_ge(y_copied, at(2, 1 + half))
                                for k in range(4):
                                    ins = mm(psum[4 + half][:, :], AT[j % 2][:, k, :], w[:, k, half * 512:(half + 1) * 512],
                                             start=(j == 0 and k == 0), stop=(j == EB - 1 and k == 3))
                                ins.then_inc(down_done, 1)

                        for j in range(EB):
                            if j != 1:
                                pe.wait_ge(ea_ready, at(EB, max(j, 1)))
                            for k in range(2):
                                full(3 * j + k)
                                w = ring[:, (3 * j + k) % (NSLOT + 1), :].rearrange("p (c n) -> p c n", n=COLS)
                                for c in range(KC):
                                    if j == 0 and k == 0 and c == 4:
                                        pe.wait_ge(gathered, at(2, 2))
                                    ins = mm(psum[2 * (j % 2) + k][:, :], HG[:, c, :], w[:, c, :],
                                             start=(c == 0), stop=(c == KC - 1))
                                ins.then_inc(egu_done, 1)
                            if j >= 1:
                                down(j - 1)
                        down(EB - 1)
                        for m in range(KC):
                            if m % 4 == 0:
                                pe.wait_ge(y_copied, at(2, 3 + m // 4))
                            if m < 2:
                                pe.wait_ge(turned, at(EB, EB - 1 + m))
                            else:
                                pe.wait_ge(scattered, at(KC, KC + m - 1))
                            mm(psum[6 + m % 2][:, 0:T], YS[:, m * P:(m + 1) * P], GST, start=True,
                               stop=True).then_inc(scatter_done, 1)

                    with pe.Fori(0, NPASS) as p:
                        with pe.If(p < passes):
                            with pe.Fori(0, NE) as e:
                                expert(p, e)

        @block.scalar
        def _(act):
            chain = Chain(act, act_chain)
            A = nc.scalar.activation
            act.wait_ge(consts_in, 16 * 6)
            A(CT[:, :, :], CT[:, :, :], ACT.Silu).then_inc(ct_ready, 1)

            def job(l, name):
                act.wait_ge(job_done, job_no(l, name) + 1)
                return bank(l, name)

            def read(ins):
                ins.then_inc(job_read['a'], 1)

            def wait_read(l, name):
                act.wait_ge(job_read['a'], read_no(l, name)[1])

            def evacuate(l, i):
                for pos, (z, u, col, m) in enumerate(ZORDER):
                    if u == i:
                        act.wait_ge(z_done, l * NZ + pos + 1)
                        A(Z[0:m, z, :], psum[pos % 2][0:m, 0:T], ACT.Copy).then_inc(z_ready, 1)

            def log_sigmoid(x, e, ready, ready_n, exp_done, done):
                act.wait_ge(ready, ready_n)
                chain(A(e, e, ACT.Exp, scale=-1.0))
                A(e, e, ACT.Ln, bias=1.0).then_inc(done, 1)

            for l in range(L):
                if l:
                    act.wait_ge(stored, 16 * nstored[0])
                A(R[:, :], job(l, 'rms1')[:, 0:T], ACT.Sqrt, bias=EPSB, scale=1.0 / DM).then_inc(job_read['a'], 1)
                for i in range(3):
                    evacuate(l, i)
                for i in range(4):
                    read(A(RN[:, i, :], job(l, f'fn{i}')[:, 0:T], ACT.Sqrt, bias=EPSB, scale=1.0 / HD))
                for tt in range(2):
                    b = job(l, f'tkv{tt}')
                    read(A(TMV[:, tt, :], b[:, 0:GW], ACT.Copy))
                read(A(QS[:, :], job(l, 'tqs')[0:NS, 0:GW], ACT.Copy))
                for i in range(4):
                    read(A(QB[:, 2 * i:2 * i + 2, :].rearrange("p b f -> p (b f)"), job(l, f'qb{i}')[:, :], ACT.Copy))
                act.wait_ge(ev["fox_qk"], l + 1)
                act.dma_start(k_out[l], Z[:, ZT['fk']:ZT['fk'] + 2, :]).then_inc(k_stored, 16)
                act.wait_ge(z_ready, l * NZ + ZPOS[ZT['fv'] + 1] + 1)
                store(act, v_out[l], Z[:, ZT['fv']:ZT['fv'] + 2, :])
                act.wait_ge(ev["ff_exp"], l + 1)
                chain(A(LF[:, :], LF[:, :], ACT.Exp, scale=-1.0))
                A(LF[:, :], LF[:, :], ACT.Ln, bias=1.0).then_inc(ev_ffln, 1)
                act.wait_ge(ev["fox_logf"], l + 1)
                store(act, logf_out[l], LF[:, :])
                for i in range(3, 8):
                    evacuate(l, i)
                for h in range(NH):
                    act.wait_ge(ev["probs_max"], l * NH + h + 1)
                    A(PS[:, h, 0:P], PS[:, h, 0:P], ACT.Exp, bias=small(2 * h), accum_out=small(8 + 2 * h)).then_inc(ev["probs_exp"], 1)
                    A(PS[:, h, P:3 * P], PS[:, h, P:3 * P], ACT.Exp, bias=small(2 * h + 1),
                      accum_out=small(9 + 2 * h)).then_inc(ev["probs_exp"], 1)
                for h in range(NH):
                    c, s = h // 2, (h % 2) * HD
                    read(A(PT[:, :], job(l, f'pt{h}')[:, 0:3 * P], ACT.Copy))
                    read(A(CAT[s:s + HD, 2 + c, 0:NP], job(l, f'o{h}')[s:s + HD, 0:NP], ACT.Copy))
                act.wait_ge(ev["dec_shift"], l + 1)
                chain.add(A(PR[:, :], PR[:, :], ACT.Exp))
                A(small(32, 32), small(32, 32), ACT.Exp).then_inc(ev["dec_exp"], 1)
                act.wait_ge(z_ready, l * NZ + ZPOS[ZT['cg'] + 1] + 1)
                cg = Z[:, ZT['cg']:ZT['cg'] + 2, :]
                A(cg, cg, ACT.Sigmoid).then_inc(ev["glu_gate"], 1)
                act.wait_ge(ev["glu"], l + 1)
                for c in range(2):
                    store(act, conv_out[l, :, c, 0:KW - 1], UP[:, c, NP:NP + KW - 1])
                    store(act, conv_out[l, :, c, KW - 1:(NS + 1) * (KW - 1)].rearrange("p (b k) -> p b k", b=NS),
                          UB[:, c, :, 1:KW])
                read(A(small(96, 32), job(l, 'pv')[:, 0:32], ACT.Copy))
                read(A(R[:, :], job(l, 'var')[:, 0:T], ACT.Sqrt, bias=EPSB, scale=1.0 / GW))
                act.wait_ge(ev["conv_out"], l + 1)
                A(CAT[:, 0:2, :], CAT[:, 0:2, :], ACT.Silu).then_inc(ev["gate_silu"], 1)
                for g in ('go', 'rg'):
                    z = Z[:, ZT[g]:ZT[g] + 2, :]
                    A(z, z, ACT.Silu).then_inc(ev["gate_silu"], 1)
                act.wait_ge(ev["gla_abs"], l + 1)
                chain(A(GA, GA, ACT.Exp, scale=-1.0))
                A(GA, GA, ACT.Ln, bias=1.0).then_inc(ev["gla_ln"], 1)
                act.wait_ge(ev["gla_b"], l + 1)
                chain.add(A(GQD, BC[:, :, :], ACT.Exp))
                chain.add(A(GKD, GKD, ACT.Exp))
                chain.add(A(DEC, DEC, ACT.Exp))
                A(GX, GX, ACT.Exp).then_inc(ev["gla_decays"], 1)
                for lag in range(1, CH):
                    act.wait_ge(ev["lag_diff"], l * (CH - 1) + lag)
                    n = 2 * NCH * (CH - lag)
                    A(EX[lag % 2][:, 0:n], EX[lag % 2][:, 0:n], ACT.Exp).then_inc(ev["lag_exp"], 1)
                for tt in range(2):
                    b = job(l, f'gkv{tt}')
                    chain.add(A(TMK[:, tt, :], b[:, 0:GW], ACT.Copy))
                    read(A(TMV[:, tt, :], b[:, GW:2 * GW], ACT.Copy))
                read(A(KV8[:, :], job(l, 'gts')[0:NS, :], ACT.Copy))
                act.wait_ge(ev["gla_states"], l + 1)
                store(act, gla_out[l, :, :, 0:HD], SH[:, :, NCH - 1, :])
                act.wait_ge(ev["s_gla"], l + 1)
                store(act, gla_out[l, :, :, HD:(NS + 1) * HD], SG[:, :, :])
                for c in range(2):
                    read(A(RNG[:, c, :], job(l, f'gn{c}')[:, 0:T], ACT.Sqrt, bias=EPSB, scale=1.0 / HD))
                for tt in range(2):
                    b = job(l, f'rkv{tt}')
                    chain.add(A(TMK[:, tt, :], b[:, 0:GW], ACT.Copy))
                    read(A(TMV[:, tt, :], b[:, GW:2 * GW], ACT.Copy))
                read(A(KV8[:, :], job(l, 'rts')[0:NS, :], ACT.Copy))
                act.wait_ge(ev["gla_cat"], l + 1)
                for h in range(NH):
                    c, s = h // 2, (h % 2) * HD
                    read(A(O[s:s + HD, c, 0:NP], job(l, f'ro{h}')[s:s + HD, 0:NP], ACT.Copy))
                read(A(PT[:, 0:P], job(l, 'rst')[:, 0:P], ACT.Copy))
                wait_read(l, 'rst')
                store(act, ret_out[l, :, :, 0:HD], PT[:, 0:P].rearrange("p (c v) -> p c v", c=2))
                act.wait_ge(ev["s_ret"], l + 1)
                store(act, ret_out[l, :, :, HD:(NS + 1) * HD], SR[:, :, :])
                for c in range(2):
                    read(A(RNG[:, c, :], job(l, f'rn{c}')[:, 0:T], ACT.Sqrt, bias=EPSB, scale=1.0 / HD))
                read(A(R[:, :], job(l, 'rms2')[:, 0:T], ACT.Sqrt, bias=EPSB, scale=1.0 / DM))
                if l % 2 == 0:
                    n = 0
                    act.wait_ge(stored, 16 * nstored[0])
                    for j in range(len(FB)):
                        for t in range(FB[j][1] // P):
                            act.wait_ge(gu_done, n + 1)
                            if n >= 4:
                                act.wait_ge(a_ready, n - 3)
                            A(SA[n % 4], psum[2 * (n % 2)][:, 0:T], ACT.Silu).then_inc(silu_ready, 1)
                            n += 1
                else:
                    act.wait_ge(stored, 16 * nstored[0])
                    act.wait_ge(gates_read, 1)
                    A(small(40, 3), small(40, 3), ACT.Exp).then_inc(gates_read, 1)
                    for i in range(6):
                        n = P if i < 4 else NS
                        act.wait_ge(h_turned, i + 1)
                        A(HT[0:n, i // 2, (i % 2) * 512:(i % 2 + 1) * 512], psum[2 + i][0:n, :], ACT.Copy).then_inc(ht_ready, 1)
                    chain(A(small(247), EPSB, ACT.Copy))
                    A(small(247), EPSB, ACT.Copy).then_inc(y_copied, 2)
                    act.wait_ge(passes_ready, 1)
                    passes = act.value_load(PASSES[0:1, 0:1], min_val=1, max_val=NPASS)

                    def expert(p, e):
                        def at(per, n):
                            return p * (NE * per) + e * per + n

                        for half in range(2):
                            act.wait_ge(gather_done, at(2, 1 + half))
                            A(HG[:, 4 * half:4 * half + 4, :].rearrange("p c s -> p (c s)"), psum[6 + half][:, :],
                              ACT.Copy).then_inc(gathered, 1)
                        act.wait_ge(gst_done, at(1, 1))
                        A(GST, psum[6][:, 0:T], ACT.Copy).then_inc(gst_ready, 1)

                        def turn_out(j):
                            act.wait_ge(turn_done, at(EB, j + 1))
                            A(AT[j % 2].rearrange("p k s -> p (k s)"), psum[6 + (j + 1) % 2][:, :],
                              ACT.Copy).then_inc(turned, 1)

                        for j in range(EB):
                            act.wait_ge(egu_done, at(2 * EB, 2 * j + 1))
                            if j != 1:
                                act.wait_ge(ea_ready, at(EB, max(j, 1)))
                            A(SILU[j % 2], psum[2 * (j % 2)][:, :], ACT.Silu).then_inc(esilu_ready, 1)
                            if j >= 1:
                                turn_out(j - 1)
                        turn_out(EB - 1)
                        for half in range(2):
                            act.wait_ge(down_done, at(2 * EB, 2 * EB - 1 + half))
                            A(YS[:, half * 512:(half + 1) * 512], psum[4 + half][:, :], ACT.Copy).then_inc(y_copied, 1)

                    with act.Fori(0, NPASS) as p:
                        with act.If(p < passes):
                            with act.Fori(0, NE) as e:
                                expert(p, e)
            act.wait_ge(ev["x_final"], 1)
            store(act, y_out, X[:, :, :])

        @block.vector
        def _(dve):
            d = Chain(dve, dve_chain)
            V = nc.vector
            tt_, ts, stt = V.tensor_tensor, V.tensor_scalar, V.scalar_tensor_tensor

            def job(l, name):
                dve.wait_ge(job_done, job_no(l, name) + 1)
                return bank(l, name)

            def read(l, name, ins):
                ins.then_inc(job_read['v'], 1)
                dve.wait_ge(job_read['v'], read_no(l, name)[1])

            def wait_act_read(l, name):
                dve.wait_ge(job_read['a'], read_no(l, name)[1])

            def wait_z(l, g, i=None):
                dve.wait_ge(z_ready, l * NZ + ZPOS[ZT[g] + (max(ZW[g] // P - 1, 0) if i is None else i)] + 1)

            def signal(ins, name, count):
                ins.then_inc(ev[name], 1)
                dve.wait_ge(ev[name], count)

            def bmid(ap, n):
                return ap[:, None, :].to_broadcast([ap.shape[0], n, ap.shape[1]])

            def bend(ap, n):
                shape = list(ap.shape) + [n]
                return (ap[:, :, None] if len(ap.shape) == 2 else ap[:, :, :, None]).to_broadcast(shape)

            def norm(l, job_name, gain, scale, shift, signal_squares, signal_h, sq):
                signal(tt_(sq, X[:, :, :], X[:, :, :], ALU.mult), signal_squares, l + 1)
                d.add(ts(MA[:, :, :], MOD[:, scale * KC:(scale + 1) * KC, :], 1.0, None, ALU.add))
                d.wait()
                d(tt_(MA[:, :, :], MA[:, :, :], bend(v_(l, gain, 0, KC), NS + 1), ALU.mult))
                wait_act_read(l, job_name)
                d(V.reciprocal(R[:, :], R[:, :]))
                d(tt_(H[:, :, :], X[:, :, :], bmid(R[:, :], KC), ALU.mult))
                d.add(tt_(H[:, :, NP:T], H[:, :, NP:T], MA[:, :, 1:], ALU.mult))
                sh = MOD[:, shift * KC:(shift + 1) * KC, :]
                for c in range(KC):
                    d.add(ts(H[:, c, 0:NP], H[:, c, 0:NP], MA[:, c, 0:1], sh[:, c, 0:1], ALU.mult, ALU.add))
                d.wait()
                signal(tt_(H[:, :, NP:T], H[:, :, NP:T], sh[:, :, 1:], ALU.add), signal_h, l + 1)

            def add_residual(dst, src, m, gate):
                g = MOD[:, gate * KC + m, :]
                d.add(tt_(small(208, NS), src[:, NP:T], g[:, 1:], ALU.mult))
                d.add(stt(dst[:, 0:NP], src[:, 0:NP], g[:, 0:1], dst[:, 0:NP], ALU.mult, ALU.add))
                d.wait()
                return tt_(dst[:, NP:T], dst[:, NP:T], small(208, NS), ALU.add)

            def value_rows(v_off, signal_name, count):
                for h in range(NH):
                    v = KV8[:, v_off + h * HD:v_off + (h + 1) * HD]
                    ins = tt_(VE[:, h], bmid(v, NS), bend(ident[0:NS, 0:NS], HD), ALU.mult)
                    if h < NH - 1:
                        d.add(ins)
                d.wait()
                signal(ins, signal_name, count)

            def head_norm(l, squares, jobs, gain, gate, first, last, cat):
                signal(tt_(BCT, O[:, :, :], O[:, :, :], ALU.mult), squares, l + 1)
                wait_act_read(l, jobs[1])
                d(V.reciprocal(RNG, RNG))
                d(tt_(O[:, :, :], O[:, :, :], RNG, ALU.mult))
                for c in range(2):
                    ins = stt(CAT[:, cat + c, :], O[:, c, :], v_(l, gain, c), Z[:, ZT[gate] + c, :],
                              ALU.mult, ALU.mult)
                    if c == 0:
                        d(ins)
                return ins

            V.memset(EPSB, EPS).then_inc(dve_chain, 1)
            d.n += 1
            dve.wait_ge(consts_in, 16 * 6)
            dve.wait_ge(page_idx, 16)
            for l in range(L):
                ts(IDX[:, l, :], IDXI[:, :], float(L * SUB), c_('sub', P, l, l + 1), ALU.mult,
                   ALU.add).then_inc(idx_ready, 1)
            for l in range(L):
                dve.wait_ge(ada_done, 12 * (l + 1))
                tt_(MOD[:, :, :], psum[0][:, 0:6 * KC * (NS + 1)].rearrange("p (c n) -> p c n", n=NS + 1),
                    bend(v_(l, 'b_ada', 0, 6 * KC), NS + 1), ALU.add).then_inc(mod_ready, 1)
                dve.wait_ge(mod_ready, l + 1)
                norm(l, 'rms1', 'norm1', 1, 0, "squares1", "h1", H[:, :, :])
                wait_z(l, 'fk')
                fqk = Z[:, ZT['fq']:ZT['fq'] + 4, :]
                signal(tt_(SQ, fqk, fqk, ALU.mult), "fox_squares", l + 1)
                wait_z(l, 'ff')
                d(ts(FX[:, :], FX[:, :], VT[0:NH, l, VCOL['fb']:VCOL['fb'] + 1], None, ALU.add))
                d(ts(FS[:, :], FX[:, :], 0.0, None, ALU.min))
                signal(stt(LF[:, :], FS[:, :], -2.0, FX[:, :], ALU.mult, ALU.add), "ff_exp", l + 1)
                wait_act_read(l, 'fn3')
                d(V.reciprocal(RN, RN))
                for i in range(4):
                    d.add(stt(fqk[:, i, :], fqk[:, i, :], v_(l, 'qn' if i < 2 else 'kn'), RN[:, i, :],
                              ALU.mult, ALU.mult))
                d.wait()
                signal(ts(fqk[:, 0:2, :], fqk[:, 0:2, :], HD ** -0.5, None, ALU.mult), "fox_qk", l + 1)
                dve.wait_ge(ev_ffln, l + 1)
                d(tt_(LF[:, :], FS[:, :], LF[:, :], ALU.subtract))
                for i in range(2):
                    a, b = i * P, (i + 1) * P
                    d(V.tensor_tensor_scan(FS[:, a:b], c_('ones', NH), LF[:, a:b],
                                           0.0 if i == 0 else FS[:, a - 1:a], ALU.mult, ALU.add))
                signal(ts(FX[:, 0:NP], FS[:, 0:NP], -1.0, None, ALU.mult), "fox_logf", l + 1)
                wait_act_read(l, 'qb3')
                for b in range(NS):
                    wait_unit(dve, ('k', l, b))
                    k3 = unit(('k', l, b)).rearrange("p (t f) -> p t f", t=TPP)
                    d(tt_(k3, k3, bmid(QB[:, b, :], TPP), ALU.mult))
                    V.tensor_reduce(SC[:, b].rearrange("p h t -> p t h"),
                                    k3.rearrange("p t (h d) -> p t h d", h=NH), AX.X, ALU.add).then_inc(k_used, 1)
                dve.wait_ge(k_used, NS * (l + 1))
                dve.wait_ge(logf_in, 16 * NS * (l + 1))
                LT = LP.rearrange("p b t h -> p b h t")
                d(V.memset(SUF[:, :, :, TPP - 1], 0.0))
                for t in range(TPP - 2, -1, -1):
                    d(tt_(SUF[:, :, :, t], SUF[:, :, :, t + 1], LT[:, :, :, t + 1], ALU.add))
                tot = small(96, 32).rearrange("p (b h) -> p b h", b=NS)
                d(tt_(tot, SUF[:, :, :, 0], LT[:, :, :, 0], ALU.add))
                lf = small(128, 32, NH).rearrange("p (b h) -> p b h", b=NS)
                signal(tt_(lf, bend(LF[:, NP:T], NH), bmid(ident[0:NH, 0:NH], NS), ALU.mult), "past_totals", l + 1)
                qk = small(224, 16).rearrange("p (c b) -> p c b", c=2)
                d(tt_(qk, fqk[:, 0:2, NP:T], fqk[:, 2:4, NP:T], ALU.mult))
                rt = small(64, 32).rearrange("p (b c s) -> p b c s", b=NS, c=2)
                d(tt_(rt[:, :, 0, :], bend(qk[:, 0, :], 2), bmid(c_('half'), NS), ALU.mult))
                signal(tt_(rt[:, :, 1, :], bend(qk[:, 1, :], 2), bmid(c_('half'), NS), ALU.mult), "row_terms", l + 1)
                for h in range(NH):
                    read(l, f's{h}', tt_(PS[:, h, :], job(l, f's{h}')[:, 0:3 * P], c_('causal'), ALU.add))
                    d.add(V.tensor_reduce(small(2 * h), PS[:, h, 0:P], AX.X, ALU.max, negate=True))
                    V.tensor_reduce(small(2 * h + 1), PS[:, h, P:3 * P], AX.X, ALU.max,
                                    negate=True).then_inc(ev["probs_max"], 1)
                for h in range(NH):
                    dve.wait_ge(ev["probs_exp"], 2 * (NH * l + h + 1))
                    d(V.reciprocal(small(8 + 2 * h, 2), small(8 + 2 * h, 2)))
                    d.add(ts(PS[:, h, 0:P], PS[:, h, 0:P], small(8 + 2 * h), None, ALU.mult))
                    ts(PS[:, h, P:3 * P], PS[:, h, P:3 * P], small(9 + 2 * h), None,
                       ALU.mult).then_inc(ev["probs"], 1)
                sn = small(32, 32)
                d(tt_(PR4, SC, SUF, ALU.add))
                read(l, 'snew', V.tensor_copy(sn, job(l, 'snew')[:, 0:32]))
                sf = job(l, 'suf')[:, 0:32].rearrange("p (b h) -> p b h", b=NS)
                read(l, 'suf', tt_(PR4, PR4, bend(sf, TPP), ALU.add))
                mx = small(160, 32)
                pr3 = PR[:, :].rearrange("p (r t) -> p r t", t=TPP)
                d(V.tensor_reduce(mx, pr3, AX.X, ALU.max))
                signal(tt_(mx, mx, sn, ALU.max), "max_part", l + 1)
                read(l, 'mxt', V.tensor_reduce(small(240, 1, 32), job(l, 'mxt')[0:32, 0:P], AX.X, ALU.max))
                signal(ts(small(192, 32, 32), ident[0:32, 0:32], small(240, 1, 32), None, ALU.mult), "max_diag", l + 1)
                mb = job(l, 'mxb')[:, 0:32]
                d(tt_(sn, sn, mb, ALU.subtract))
                read(l, 'mxb', tt_(pr3, pr3, bend(mb, TPP), ALU.subtract))
                signal(V.memset(small(241), 0.0), "dec_shift", l + 1)
                dve.wait_ge(ev["dec_exp"], l + 1)
                signal(V.tensor_reduce(small(64, 32), pr3, AX.X, ALU.add), "dec_sum", l + 1)
                read(l, 'sumb', tt_(small(160, 32), job(l, 'sumb')[:, 0:32], sn, ALU.add))
                d(V.reciprocal(small(160, 32), small(160, 32)))
                d(tt_(sn, sn, small(160, 32), ALU.mult))
                signal(tt_(pr3, pr3, bend(small(160, 32), TPP), ALU.mult), "dec_probs", l + 1)
                ca = Z[:, ZT['ca']:ZT['ca'] + 2, :]
                cg = Z[:, ZT['cg']:ZT['cg'] + 2, :]
                dve.wait_ge(ev["glu_gate"], l + 1)
                dve.wait_ge(states_in, 64 * (l + 1))
                if l == 0:
                    dve.wait_ge(pool_chain, 1)
                d.add(tt_(UB[:, :, :, KW - 1], ca[:, :, NP:T], cg[:, :, NP:T], ALU.mult))
                signal(tt_(UP[:, :, KW - 1:], ca[:, :, 0:NP], cg[:, :, 0:NP], ALU.mult), "glu", l + 1)
                d.wait()
                cw = v_(l, 'conv_w', 0, 2 * KW).rearrange("p (c k) -> p c k", c=2)
                UBW = TA[0][:, 0:2 * NS * KW].rearrange("p (c b k) -> p c b k", c=2, b=NS)
                dve.wait_ge(job_done, job_no(l, 'o3') + 1)
                for c in range(2):
                    d.add(ts(ca[:, c, 0:NP], UP[:, c, 0:NP], cw[:, c, 0:1], v_(l, 'conv_b', c), ALU.mult, ALU.add))
                    d.add(tt_(UBW[:, c], UB[:, c], bmid(cw[:, c, :], NS), ALU.mult))
                d.wait()
                for k in range(1, KW):
                    for c in range(2):
                        dve.wait_ge(dve_chain, d.n - 1)
                        d.add(stt(ca[:, c, 0:NP], UP[:, c, k:k + NP], cw[:, c, k:k + 1], ca[:, c, 0:NP],
                                  ALU.mult, ALU.add))
                for c in range(2):
                    d.add(V.tensor_reduce(ca[:, c, NP:T], UBW[:, c], AX.X, ALU.add))
                d.wait()
                signal(tt_(ca[:, :, NP:T], ca[:, :, NP:T], bend(v_(l, 'conv_b', 0, 2), NS), ALU.add), "conv_y", l + 1)
                b = job(l, 'mean')[:, 0:T]
                read(l, 'mean', ts(R[:, :], b, -1.0 / GW, None, ALU.mult))
                d(tt_(ca, ca, bmid(R[:, :], 2), ALU.add))
                signal(tt_(TA2, ca, ca, ALU.mult), "conv_sq", l + 1)
                wait_act_read(l, 'var')
                d(V.reciprocal(R[:, :], R[:, :]))
                d(tt_(ca, ca, bmid(R[:, :], 2), ALU.mult))
                for c in range(2):
                    d.add(ts(CAT[:, c, :], ca[:, c, :], v_(l, 'ln_g', c), v_(l, 'ln_b', c), ALU.mult, ALU.add))
                d.wait()
                signal(V.memset(small(241), 0.0), "conv_out", l + 1)
                fv = Z[:, ZT['fv']:ZT['fv'] + 2, :]
                wait_act_read(l, 'pv')
                pv4 = small(96, 32).rearrange("p (b c s) -> p c s b", b=NS, c=2)
                sn4 = sn.rearrange("p (b c s) -> p c s b", b=NS, c=2)
                for s in range(2):
                    r = slice(s * HD, (s + 1) * HD)
                    d(tt_(CAT[r, 2:4, NP:T], sn4[r, :, s, :], fv[r, :, NP:T], ALU.mult))
                    d(tt_(CAT[r, 2:4, NP:T], CAT[r, 2:4, NP:T], pv4[r, :, s, :], ALU.add))
                for c in range(2):
                    read(l, f'gate{c}', ts(GX[:, c, :], job(l, f'gate{c}')[:, 0:T], v_(l, 'b_gate', c), None, ALU.add))
                d(ts(GM, GX, 0.0, None, ALU.min))
                signal(stt(GA, GM, -2.0, GX, ALU.mult, ALU.add), "gla_abs", l + 1)
                dve.wait_ge(ev["gla_ln"], l + 1)
                d(tt_(GX, GM, GA, ALU.subtract))
                d(ts(GX, GX, 1.0 / 16.0, None, ALU.mult))
                for c in range(2):
                    d.add(V.tensor_tensor_scan(BC[:, c, :], c_('reset'), GX[:, c, 0:NP], 0.0, ALU.mult, ALU.add))
                d.wait()
                bc4 = BC[:, :, :].rearrange("p c (n i) -> p c n i", i=CH)
                kd4 = GKD.rearrange("p c (n i) -> p c n i", i=CH)
                last = bc4[:, :, :, CH - 1]
                d.add(V.tensor_copy(DEC, last))
                dve.wait_ge(k_stored, 16 * (l + 1))
                for c in range(2):
                    ins = tt_(kd4[:, c], bend(last[:, c, :], CH), bc4[:, c], ALU.subtract)
                    if c == 0:
                        d.add(ins)
                d.wait()
                signal(ins, "gla_b", l + 1)
                gq = Z[:, ZT['gq']:ZT['gq'] + 2, :]
                gk = Z[:, ZT['gk']:ZT['gk'] + 2, :]
                gv = Z[:, ZT['gv']:ZT['gv'] + 2, :]
                wait_z(l, 'gv')
                d(ts(gq, gq, HD ** -0.5, None, ALU.mult))
                dve.wait_ge(ev["gla_decays"], l + 1)
                d.add(tt_(GQD, GQD, gq[:, :, 0:NP], ALU.mult))
                signal(tt_(GKD, GKD, gk[:, :, 0:NP], ALU.mult), "gla_kq", l + 1)
                q4, k4, v4 = (t[:, :, 0:NP].rearrange("p c (n i) -> p c n i", i=CH) for t in (gq, gk, gv))
                o4 = O[:, :, 0:NP].rearrange("p c (n i) -> p c n i", i=CH)

                def lag_view(t, lag):
                    return t[:, 0:2 * NCH * (CH - lag)].rearrange("p (c n i) -> p c n i", c=2, n=NCH)

                def difference(lag):
                    if lag >= 1:
                        tt_(lag_view(EX[lag % 2], lag), bc4[:, :, :, lag:], bc4[:, :, :, 0:CH - lag],
                            ALU.subtract).then_inc(ev["lag_diff"], 1)

                def weights(lag):
                    w = lag_view(WX[lag % 2], lag)
                    if lag >= 2:
                        dve.wait_ge(job_done, job_no(l, f'att{lag - 2}') + 1)
                    ins = tt_(w, q4[:, :, :, lag:], k4[:, :, :, 0:CH - lag], ALU.mult)
                    if lag >= 1:
                        d(ins)
                        dve.wait_ge(ev["lag_exp"], l * (CH - 1) + lag)
                        ins = tt_(w, w, lag_view(EX[lag % 2], lag), ALU.mult)
                    signal(ins, "lag_w", l * CH + lag + 1)

                def gather_lag(lag):
                    b = lag_view(job(l, f'att{lag}'), lag)
                    if lag == 0:
                        read(l, 'att0', tt_(o4, b, v4, ALU.mult))
                        return
                    t = lag_view(TA[lag % 2], lag)
                    read(l, f'att{lag}', tt_(t, b, v4[:, :, :, 0:CH - lag], ALU.mult))
                    d(tt_(o4[:, :, :, lag:], o4[:, :, :, lag:], t, ALU.add))

                for lag in range(CH + 1):
                    if lag < CH:
                        difference(lag)
                        weights(lag)
                    if lag >= 1:
                        gather_lag(lag - 1)
                for tt in range(2):
                    wait_act_read(l, 'gkv1')
                    if tt:
                        dve.wait_ge(job_done, job_no(l, 'kv01') + 1)
                    for h in range(NH):
                        ins = tt_(VX[:, h], bmid(TMV[:, tt, h * HD:(h + 1) * HD], 8), bend(c_('chunk'), HD), ALU.mult)
                        if h < NH - 1:
                            d.add(ins)
                    d.wait()
                    signal(ins, "gla_vx", 2 * l + tt + 1)
                    for pr in range(2):
                        b = job(l, f'kv{tt}{pr}')[:, :].rearrange("p (n v) -> p n v", n=8)
                        for n in range(8):
                            g = 8 * tt + n
                            if g == 0:
                                ins = V.tensor_copy(SH[:, pr, 0, :], b[:, 0, :])
                            else:
                                ins = stt(SH[:, pr, g, :], SH[:, pr, g - 1, :], DEC[:, pr, g:g + 1], b[:, n, :],
                                          ALU.mult, ALU.add)
                            if n < 7:
                                d(ins)
                        read(l, f'kv{tt}{pr}', ins)
                signal(V.memset(small(241), 0.0), "gla_states", l + 1)
                for s in range(2):
                    r = slice(s * HD, (s + 1) * HD)
                    b = job(l, f'gi{s}')[r, :].rearrange("p (c t) -> p c t", c=2)
                    read(l, f'gi{s}', tt_(O[r, :, CH:NP], O[r, :, CH:NP], b[:, :, CH:NP], ALU.add))
                wait_act_read(l, 'gts')
                dve.wait_ge(job_done, job_no(l, 'kv11') + 1)
                value_rows(GW, "ve_gla", l + 1)
                for c in range(2):
                    d.add(tt_(SG4[:, c], SG4[:, c], bend(GX[:, c, NP:T], HD), ALU.mult))
                d.wait()
                for c in range(2):
                    read(l, f'gx{c}', tt_(SG[:, c, :], SG[:, c, :], job(l, f'gx{c}')[:, :], ALU.add))
                signal(V.memset(small(241), 0.0), "s_gla", l + 1)
                for s in range(2):
                    r = slice(s * HD, (s + 1) * HD)
                    b = job(l, f'gs{s}')[r, 0:2 * NS].rearrange("p (c b) -> p c b", c=2)
                    read(l, f'gs{s}', V.tensor_copy(O[r, :, NP:T], b))
                dve.wait_ge(ev["gate_silu"], 3 * (l + 1))
                signal(head_norm(l, "gla_sq", ('gn0', 'gn1'), 'gla_g', 'go', None, None, 4), "gla_cat", l + 1)
                for i in range(4):
                    z, t = Z[:, ZT['rq'] + i, :], TA[i % 2][:, 0:T]
                    sc = 1.0 if i < 2 else HD ** -0.5
                    read(l, f'rr{i}', stt(t, job(l, f'rr{i}')[:, 0:T], sc, c_('sin'), ALU.mult, ALU.mult))
                    d(stt(z, z, sc, c_('cos'), ALU.mult, ALU.mult))
                    d(tt_(z, z, t, ALU.add))
                signal(V.memset(small(241), 0.0), "rope", l + 1)
                dec = c_('decay').rearrange("p (h t) -> p h t", h=NH)
                for h in range(NH):
                    b = job(l, f'rs{h}')
                    d(tt_(RP(h)[:, 0:NP], b[:, 0:NP], dec[:, h, :], ALU.mult))
                    read(l, f'rs{h}', tt_(RP(h)[:, NP:3 * P], b[:, NP:3 * P], dec[:, h, 0:P], ALU.mult))
                    V.memset(small(241), 0.0).then_inc(ev["ret_p"], 1)
                    dve.wait_ge(ev["ret_p"], NH * l + h + 1)
                wait_act_read(l, 'rkv1')
                dk = c_('dk').rearrange("p (t h) -> p t h", h=NH)
                for tt in range(2):
                    ins = tt_(TMK[:, tt, :].rearrange("p (h d) -> p h d", h=NH),
                              TMK[:, tt, :].rearrange("p (h d) -> p h d", h=NH), bend(dk[:, tt, :], HD), ALU.mult)
                    if tt == 0:
                        d(ins)
                signal(ins, "ret_kd", l + 1)
                dve.wait_ge(job_done, job_no(l, 'ro3') + 1)
                value_rows(GW, "ve_ret", l + 1)
                for c in range(2):
                    d(ts(SR[:, c, :], SR[:, c, :], c_('gamma', P, c, c + 1), None, ALU.mult))
                for c in range(2):
                    read(l, f'rx{c}', tt_(SR[:, c, :], SR[:, c, :], job(l, f'rx{c}')[:, :], ALU.add))
                signal(V.memset(small(241), 0.0), "s_ret", l + 1)
                for s in range(2):
                    r = slice(s * HD, (s + 1) * HD)
                    b = job(l, f'rd{s}')[r, 0:2 * NS].rearrange("p (c b) -> p c b", c=2)
                    read(l, f'rd{s}', V.tensor_copy(O[r, :, NP:T], b))
                wait_act_read(l, 'ro3')
                signal(head_norm(l, "ret_sq", ('rn0', 'rn1'), 'ret_g', 'rg', None, None, 6), "cat", l + 1)
                for m in range(KC):
                    dve.wait_ge(out_done, l * KC + m + 1)
                    add_residual(X[:, m, :], psum[m % 2], m, 2).then_inc(out_added, 1)
                    dve.wait_ge(out_added, l * KC + m + 1)
                dve.wait_ge(stored, 16 * STORES_PER_LAYER * (l + 1))
                if l % 2 == 0:
                    norm(l, 'rms2', 'norm2', 4, 3, "squares2", "h2", Z[:, 0:KC, :])
                    n = 0
                    for j in range(len(FB) + 1):
                        if j < len(FB):
                            for t in range(FB[j][1] // P):
                                if j >= 3:
                                    dve.wait_ge(y_done, KC * (j - 2))
                                dve.wait_ge(silu_ready, n + 1)
                                tt_(AB[:, j % 3, t, :], SA[n % 4], psum[2 * (n % 2) + 1][:, 0:T],
                                    ALU.mult).then_inc(a_ready, 1)
                                n += 1
                        if j >= 1:
                            for m in range(KC):
                                q = KC * (j - 1) + m
                                dve.wait_ge(y_done, q + 1)
                                b = psum[4 + m % 4][:, 0:T]
                                if j == 1:
                                    V.tensor_copy(Y[:, m, :], b).then_inc(y_added, 1)
                                else:
                                    tt_(Y[:, m, :], Y[:, m, :], b, ALU.add).then_inc(y_added, 1)
                                dve.wait_ge(y_added, q + 1)
                    for m in range(KC):
                        d(add_residual(X[:, m, :], Y[:, m, :], m, 5))
                else:
                    norm(l, 'rms2', 'norm2', 4, 3, "squares2", "h2", Z[:, 0:KC, :])
                    dve.wait_ge(router_done, 1)
                    for tt in range(3):
                        n = P if tt < 2 else NS
                        lg = small(56, NE, n)
                        d(V.tensor_copy(lg, psum[0][0:n, tt * NE:(tt + 1) * NE]))
                        d(V.max(small(16 * tt + 64, 8, n), lg))
                        d(V.max_index(MI[0:n, tt, :], small(16 * tt + 64, 8, n), lg))
                        d(V.tensor_copy(small(16 * tt + 72, 2, n), MI[0:n, tt, 0:2]))
                        d(tt_(small(40 + tt, 1, n), small(16 * tt + 65, 1, n), small(16 * tt + 64, 1, n), ALU.subtract))
                    signal_n = V.memset(small(241), 0.0)
                    signal_n.then_inc(gates_read, 1)
                    dve.wait_ge(gates_read, 2)
                    d(ts(small(44, 3), small(40, 3), 1.0, None, ALU.add))
                    d(V.reciprocal(small(44, 3), small(44, 3)))
                    d(tt_(small(48, 3), small(44, 3), small(40, 3), ALU.mult))
                    SLOTS, GATES = SLG[:, 0], SLG[:, 1]
                    d(V.memset(SLG[:, :, :, :], 0.0))
                    for tt in range(3):
                        n = P if tt < 2 else NS
                        i1, i2 = small(16 * tt + 72, 1, n), small(16 * tt + 73, 1, n)
                        m1, m2 = small(56, NE, n), small(8, NE, n)
                        d.add(ts(m1, c_('eio', n), i1, None, ALU.is_equal))
                        d(ts(m2, c_('eio', n), i2, None, ALU.is_equal))
                        tt_(MASK(tt, n), m1, m2, ALU.add).then_inc(masks_ready, 1)
                        d(ts(m1, m1, small(44 + tt, 1, n), None, ALU.mult))
                        d(stt(GATES[0:n, tt, 0:NE], m2, small(48 + tt, 1, n), m1, ALU.mult, ALU.add))
                    dve.wait_ge(masks_ready, 3)
                    dve.wait_ge(router_done, 2)
                    for tt in range(3):
                        n = P if tt < 2 else NS
                        d(stt(SLOTS[0:n, tt, 0:NE], psum[1][0:n, tt * NE:(tt + 1) * NE], 1.0, MASK(tt, n),
                              ALU.add, ALU.mult))
                    d(ts(SLOTS[:, :, 0:NE], SLOTS[:, :, 0:NE], -1.0, None, ALU.add))
                    d.add(ts(SLOTS[:, :, NE:], SLOTS[:, :, 0:1], -float(CAP), None, ALU.add))
                    d.add(V.tensor_copy(GATES[:, :, NE:], GATES[:, :, 0:1]))
                    d.add(V.memset(Y, 0.0))
                    d(V.tensor_reduce(small(16), psum[1][:, 3 * NE:4 * NE], AX.X, ALU.max))
                    d(ts(small(17), small(16), CAP + 0.5, None, ALU.is_gt))
                    d(stt(small(18), small(16), 2 * CAP + 0.5, small(17), ALU.is_gt, ALU.add))
                    signal_passes = ts(PASSES[:, :], small(18), 1.0, 1.0, ALU.mult, ALU.add)
                    signal_passes.then_inc(passes_ready, 1)

                    def select(column):
                        s, g = SLG[:, 0, :, column], SLG[:, 1, :, column]
                        d(tt_(SEL, bmid(c_('slot'), 3), s.to_broadcast([P, 3, P]), ALU.is_equal))
                        return tt_(GSEL, SEL, g.to_broadcast([P, 3, P]), ALU.mult)

                    select(slice(0, 1)).then_inc(slots_ready, 1)
                    V.memset(small(241), 0.0).then_inc(ea_ready, 1)
                    V.memset(small(242), 0.0).then_inc(scattered, KC)
                    dve.wait_ge(passes_ready, 1)
                    passes = dve.value_load(PASSES[0:1, 0:1], min_val=1, max_val=NPASS)

                    def expert(p, e):
                        def at(per, n):
                            return p * (NE * per) + e * per + n

                        for j in range(EB):
                            dve.wait_ge(egu_done, at(2 * EB, 2 * j + 2))
                            dve.wait_ge(esilu_ready, at(EB, j + 1))
                            tt_(AM[j % 2], SILU[j % 2], psum[2 * (j % 2) + 1][:, :], ALU.mult).then_inc(ea_ready, 1)
                            if j == 3:
                                s, g = SLG[:, 0, :, bass.ds(e + 1, 1)], SLG[:, 1, :, bass.ds(e + 1, 1)]
                                tt_(SEL, bmid(c_('slot'), 3), s.to_broadcast([P, 3, P]),
                                    ALU.is_equal).then_inc(sel_ready, 1)
                                dve.wait_ge(sel_ready, at(1, 1))
                                tt_(GSEL, SEL, g.to_broadcast([P, 3, P]), ALU.mult).then_inc(slots_ready, 1)
                        for m in range(KC):
                            dve.wait_ge(scatter_done, at(KC, m + 1))
                            dve.wait_ge(scattered, at(KC, m + 1))
                            tt_(Y[:, m, :], Y[:, m, :], psum[6 + m % 2][:, 0:T], ALU.add).then_inc(scattered, 1)

                    with dve.Fori(0, NPASS) as p:
                        with dve.If(p < passes):
                            with dve.Fori(0, NE) as e:
                                expert(p, e)
                            ts(SLOTS, SLOTS, -float(CAP), None, ALU.add).then_inc(slots_moved, 1)
                            dve.wait_ge(slots_moved, p + 1)
                            V.memset(small(241), 0.0)
                    dve.wait_ge(scattered, passes * (NE * KC) + KC)
                    for m in range(KC):
                        ins = add_residual(X[:, m, :], Y[:, m, :], m, 5)
                        if m < KC - 1:
                            d(ins)
                    ins.then_inc(ev["x_final"], 1)


def kernel(**inputs):
    import numpy as np
    import concourse.bacc as bacc
    from concourse.bass_utils import run_bass_kernel_spmd

    a = {k: np.asarray(v) for k, v in inputs.items()}

    def features(x):
        return np.ascontiguousarray(x.T.reshape(-1, P, x.shape[0]).transpose(1, 0, 2))

    def columns(v):
        return v.reshape(-1, P).T

    x = np.concatenate([a['x_prompt'][0], a['x_sample'][:, 0]])
    c = np.concatenate([a['c_prompt'], a['c_sample']])
    vt = []
    for l in range(L):
        parts = [columns(a['norm1_g'][l]), columns(a['norm2_g'][l]), columns(a['b_ada'][l]), columns(a['conv_b'][l]),
                 columns(a['conv_ln_g'][l]), columns(a['conv_ln_b'][l]), columns(a['gla_b_gate'][l]),
                 columns(a['gla_norm_g'][l]), columns(a['ret_norm_g'][l]), np.tile(a['fox_qn_g'][l], 2)[:, None],
                 np.tile(a['fox_kn_g'][l], 2)[:, None], np.tile(a['fox_fb'][l], P // NH)[:, None],
                 a['conv_w'][l].T.reshape(2, P, KW).transpose(1, 0, 2).reshape(P, 2 * KW)]
        vt.append(np.concatenate(parts, 1))

    def states(s):
        return np.ascontiguousarray(
            s.reshape(L, NS, 2, 2, HD, HD).transpose(0, 3, 4, 2, 1, 5).reshape(L, P, 2, NS * HD))

    arrays = {
        'xT': features(x), 'cT': features(c), 'vt': np.ascontiguousarray(np.stack(vt, 1)),
        'consts': host_constants(),
        'conv_in': np.ascontiguousarray(
            a['state_conv'].reshape(L, NS, KW - 1, 2, P).transpose(0, 4, 3, 1, 2)),
        'gla_in': states(a['state_gla']), 'ret_in': states(a['state_ret']),
        'ptr': np.ascontiguousarray(np.repeat(a['page_table'].T, SUB, axis=0)),
        'cache_k': a['cache_k'], 'cache_v': a['cache_v'], 'cache_logf': a['cache_logf'],
        'w_in': a['w_in'], 'w_out': a['w_out'], 'w_ada': a['w_ada'], 'gate2': a['gla_w_gate2'],
        'ffn_w1': a['ffn_w1'], 'ffn_w3': a['ffn_w3'], 'ffn_w2': a['ffn_w2'],
        'router': a['moe_router'][0], 'moe_w1': a['moe_w1'], 'moe_w3': a['moe_w3'], 'moe_w2': a['moe_w2'],
    }
    outs = {'y_out': (P, KC, T), 'conv_out': (L, P, 2, (NS + 1) * (KW - 1)), 'k_out': (L, P, 2, T),
            'v_out': (L, P, 2, T), 'logf_out': (L, NH, T), 'gla_out': (L, P, 2, (NS + 1) * HD),
            'ret_out': (L, P, 2, (NS + 1) * HD)}
    nc = bacc.Bacc("TRN2", target_bir_lowering=False, num_devices=1)
    args = [nc.dram_tensor(k, v.shape, mybir.dt.from_np(v.dtype), kind="ExternalInput").ap()
            for k, v in arrays.items()]
    args += [nc.dram_tensor(k, v, F32, kind="ExternalOutput").ap() for k, v in outs.items()]
    trunk_kernel(nc, *args)
    r = run_bass_kernel_spmd(nc, [arrays], core_ids=[0]).results[0]

    def tokens(y):
        y = np.moveaxis(y, -1, -3)
        return np.swapaxes(y, -1, -2).reshape(*y.shape[:-2], -1)

    y = tokens(r['y_out'])
    conv = np.asarray(r['conv_out']).reshape(L, P, 2, NS + 1, KW - 1).transpose(0, 3, 4, 2, 1)
    conv = conv.reshape(L, NS + 1, KW - 1, GW)
    k, v = (tokens(r[n]).reshape(L, T, NH, HD) for n in ('k_out', 'v_out'))
    logf = np.asarray(r['logf_out']).transpose(0, 2, 1)

    def split(s):
        s = np.asarray(s).reshape(L, 2, HD, 2, NS + 1, HD).transpose(0, 4, 3, 1, 2, 5)
        s = s.reshape(L, NS + 1, NH, HD, HD)
        return s[:, :1], s[:, 1:]

    def by_sample(t):
        return t[:, NP:].swapaxes(0, 1)[:, :, None]

    gla, ret = split(r['gla_out']), split(r['ret_out'])
    result = (y[None, :NP], y[NP:, None], conv[:, :1], conv[:, 1:], k[None, :, :NP], by_sample(k),
              v[None, :, :NP], by_sample(v), logf[None, :, :NP], by_sample(logf), gla[0], gla[1], ret[0], ret[1])
    return tuple(np.ascontiguousarray(t) for t in result)
```

```python
from contextlib import ExitStack

import concourse.bass as bass
import numpy as np
from concourse import mybir

F32 = mybir.dt.float32
F32R = mybir.dt.float32r
I32 = mybir.dt.int32
U32 = mybir.dt.uint32
ALU = mybir.AluOpType
ACT = mybir.ActivationFunctionType
AX = mybir.AxisListType

P = 128
DM = 1024
KC = DM // P
NP = 256
NS = 8
T = NP + NS
L = 2
NH, HD = 4, 64
GW = NH * HD
KW = 31
LR = 16
CH = 16
NCH = NP // CH
PAGE, NPAGE, NPHYS = 128, 16, 160
TPP = PAGE * NPAGE // P
SUB = PAGE // TPP
DFF = 2816
NE, DE = 8, 3584
CAP = P
NPASS = -(-T // CAP)
EPS = 1e-6
SLOT = 4096
NSLOT = 6
NLOW = 4
COLS = 512

ZT = {'ca': 0, 'cg': 2, 'fq': 4, 'fk': 6, 'fv': 8, 'ff': 10, 'gq': 11, 'gk': 13, 'gv': 15,
      'glr': 17, 'go': 18, 'rq': 20, 'rk': 22, 'rv': 24, 'rg': 26}
NZ = 28
ZCOL = {'ca': 0, 'cg': 256, 'fq': 512, 'fk': 768, 'fv': 1024, 'ff': 1280, 'gq': 1284, 'gk': 1540,
        'gv': 1796, 'glr': 2052, 'go': 2068, 'rq': 2324, 'rk': 2580, 'rv': 2836, 'rg': 3092}
ZW = {k: GW for k in ZT} | {'ff': NH, 'glr': LR}
ZUNITS = [('fq', 'fk'), ('fv', 'ff'), ('ca', 'cg'), ('gq', 'gk'), ('gv', 'glr'), ('go', 'rq'),
          ('rk', 'rv'), ('rg',)]
ZORDER = []
for _u, _gs in enumerate(ZUNITS):
    for _g in _gs:
        for _c in range(0, ZW[_g], P):
            ZORDER.append((ZT[_g] + _c // P, _u, ZCOL[_g] - ZCOL[_gs[0]] + _c, min(P, ZW[_g] - _c)))
ZPOS = {t[0]: n for n, t in enumerate(ZORDER)}

VCOL, _n = {}, 0
for _k, _w in (('norm1', KC), ('norm2', KC), ('b_ada', 6 * KC), ('conv_b', 2), ('ln_g', 2), ('ln_b', 2),
               ('b_gate', 2), ('gla_g', 2), ('ret_g', 2), ('qn', 1), ('kn', 1), ('fb', 1),
               ('conv_w', 2 * KW)):
    VCOL[_k] = _n
    _n += _w
NV = _n

CCOL, _n = {}, 0
for _k, _w in (('ident', P), ('ones', P), ('heads', P), ('swap', P), ('later', P), ('cos', T), ('sin', T),
               ('reset', NP), ('slot', P), ('decay', NH * NP), ('causal', 3 * P),
               ('chunk', 8), ('half', 2), ('dk', 2 * NH), ('gamma', 2), ('eio', NE), ('sub', L)):
    CCOL[_k] = (_n, _w)
    _n += _w
NC = _n

EB = DE // COLS
PIECE = SLOT // 2
STREAM = [(k, 0, i) for k in range(2) for i in range(2)]
for _j in range(1, EB):
    STREAM += [(k, _j, i) for k in range(2) for i in range(2)] + [(2, _j - 1, i) for i in range(2)]
STREAM += [(2, EB - 1, i) for i in range(2)]
NPC = len(STREAM)
SPOS = {p: n for n, p in enumerate(STREAM)}
NRAW = 7
NSPLIT = 3
assert NPC % NRAW == 0 and NPC % NSPLIT == 0

JOBS = [('rms1', 'a')] + [(f'fn{i}', 'a') for i in range(4)]
JOBS += [('tkv0', 'a'), ('tkv1', 'a'), ('tqs', 'a')] + [(f'qb{i}', 'a') for i in range(4)]
JOBS += [(f's{h}', 'v') for h in range(NH)]
for _h in range(NH):
    JOBS += [(f'pt{_h}', 'a'), (f'o{_h}', 'a')]
JOBS += [('snew', 'v'), ('suf', 'v'), ('mxt', 'v'), ('mxb', 'v'), ('sumb', 'v')]
JOBS += [('mean', 'v'), ('var', 'a')]
JOBS += [('gate0', 'v'), ('gate1', 'v')] + [(f'att{i}', 'v') for i in range(CH)]
JOBS += [('gkv0', 'a'), ('gkv1', 'a'), ('gts', 'a')]
JOBS += [(f'kv{_tt}{_pr}', 'v') for _tt in range(2) for _pr in range(2)]
JOBS += [('gi0', 'v'), ('gi1', 'v'), ('gx0', 'v'), ('gx1', 'v'), ('gs0', 'v'), ('gs1', 'v'),
         ('gn0', 'a'), ('gn1', 'a')]
JOBS += [(f'rr{i}', 'v') for i in range(4)] + [('rkv0', 'a'), ('rkv1', 'a'), ('rts', 'a')]
for _h in range(NH):
    JOBS += [(f'rs{_h}', 'v'), (f'ro{_h}', 'a')]
JOBS += [('rst', 'a'), ('rx0', 'v'), ('rx1', 'v'), ('rd0', 'v'), ('rd1', 'v'), ('rn0', 'a'), ('rn1', 'a'),
         ('rms2', 'a')]
JPOS = {n: i for i, (n, _) in enumerate(JOBS)}
NJ = len(JOBS)
NBANK = 6


def job_no(l, name):
    return l * NJ + JPOS[name]


def divmod_job(n):
    return n // NJ, JOBS[n % NJ][0]


STORES_PER_LAYER = 10
NSTORES = L * STORES_PER_LAYER + 1


def read_no(l, name):
    who = JOBS[JPOS[name]][1]
    per = sum(w == who for _, w in JOBS)
    return who, l * per + sum(w == who for _, w in JOBS[:JPOS[name] + 1])


ADA1 = 4
NADA = 6 * DM // COLS
ROWS_FIRST = [('ada', 0, i) for i in range(ADA1)]
ROWS_OF = []
for _l in range(L):
    ROWS_OF.append([('ada', _l, i) for i in range(ADA1, NADA)])
    ROWS_OF[_l] += [('pv', _l, i) for i in range(NS // 2)]
    if _l + 1 < L:
        ROWS_OF[_l] += [('ada', _l + 1, i) for i in range(ADA1)]
LAG_BG, REST_BG = (7, 4), (8, 8)
ROWJOBS = ROWS_FIRST + sum(ROWS_OF, [])
RPOS = {j: n for n, j in enumerate(ROWJOBS)}


def row_units(j):
    return [j] if j[0] == 'ada' else [('v', j[1], 2 * j[2]), ('v', j[1], 2 * j[2] + 1)]


FB = [(j * COLS, min(COLS, DFF - j * COLS)) for j in range(-(-DFF // COLS))]


def ring_units():
    order = list(ROWS_FIRST)
    for l in range(L):
        order += [('in', l, 0), ('in', l, 1), ('in', l, 2)]
        for b in range(NS):
            order.append(('k', l, b))
            if b < 5:
                order.append(('in', l, 3 + b))
        for j in ROWS_OF[l]:
            order += row_units(j)
        order += [('out', l, 0), ('out', l, 1)]
        if l % 2 == 0:
            for j in range(len(FB)):
                order += [('w1', l, j), ('w3', l, j), ('w2', l, j)]
    return order


UNITS = ring_units()
UPOS = {u: n for n, u in enumerate(UNITS)}


def host_constants():
    c = np.zeros((P, NC), np.float32)

    def put(name, a):
        o, w = CCOL[name]
        c[:a.shape[0], o:o + w] = a.reshape(a.shape[0], -1)

    f = np.float32
    put('ident', np.eye(P, dtype=f))
    put('ones', np.ones((P, P), f))
    hd = np.arange(P) // HD
    put('heads', (hd[:, None] == hd[None, :]).astype(f))
    half = HD // 2
    swap = np.zeros((P, P), f)
    for m in range(P):
        if m % HD < half:
            swap[m + half, m] = -1.0
        else:
            swap[m - half, m] = 1.0
    put('swap', swap)
    put('later', (np.arange(P)[:, None] > np.arange(P)[None, :]).astype(f))
    inv = f(10000.0) ** (-np.arange(half, dtype=f) / f(half))
    pos = np.concatenate([np.arange(NP, dtype=f), np.full(NS, f(PAGE * NPAGE), f)])
    ang = (pos[None, :] * inv[:, None]).astype(f)
    put('cos', np.tile(np.cos(ang), (P // half, 1)))
    put('sin', np.tile(np.sin(ang), (P // half, 1)))
    put('reset', np.tile((np.arange(NP) % CH != 0).astype(f), (P, 1)))
    put('slot', np.tile(np.arange(P, dtype=f), (P, 1)))
    lg = np.log(1.0 - np.exp2(-5.0 - np.arange(NH)))
    rel = np.arange(NP)[None, :] - np.arange(P)[:, None]
    put('decay', np.stack([np.where(rel >= 0, np.exp(np.maximum(rel, 0) * g), 0.0) for g in lg], 1).astype(f))
    tri = np.where(np.arange(P)[None, :] <= np.arange(P)[:, None], f(0), f(-1e30))
    put('causal', np.concatenate([tri, np.zeros((P, P), f), tri], 1))
    put('chunk', (np.arange(P)[:, None] // CH == np.arange(8)[None, :]).astype(f))
    put('half', (hd[:, None] == np.arange(2)[None, :]).astype(f))
    tok = np.arange(P)[:, None] + P * np.arange(2)[None, :]
    put('dk', np.exp((NP - 1 - tok)[:, :, None] * lg[None, None, :]).astype(f))
    put('gamma', np.exp(lg).astype(f)[2 * np.arange(2)[None, :] + hd[:, None]])
    put('sub', (np.arange(P)[:, None] % SUB + SUB * np.arange(L)[None, :]).astype(f))
    put('eio', np.tile(np.arange(NE, dtype=f), (P, 1)))
    return c


def trunk_kernel(nc, xT, cT, vt, consts, conv_in, gla_in, ret_in, ptr, cache_k, cache_v, cache_logf,
                 w_in, w_out, w_ada, gate2, ffn_w1, ffn_w3, ffn_w2, router, moe_w1, moe_w3, moe_w2,
                 y_out, conv_out, k_out, v_out, logf_out, gla_out, ret_out):
    ctx = ExitStack()
    with ctx:
        def sb(name, shape, dt=F32):
            return ctx.enter_context(nc.sbuf_tensor(name, shape, dt))

        def sem(name):
            return ctx.enter_context(nc.semaphore(name))

        early = ExitStack()

        def sbe(name, shape, dt=F32):
            return early.enter_context(nc.sbuf_tensor(name, shape, dt))

        ring_low = sb("ring_low", [P, NLOW, SLOT])
        C = sb("C", [P, NC])
        VT = sb("VT", [P, L, NV])
        X = sb("X", [P, KC, T])
        H = sb("H", [P, KC, T])
        MOD = sb("MOD", [P, L, 6 * KC, NS + 1])
        CT = sb("CT", [P, KC, NS + 1])
        MA = sb("MA", [P, KC, NS + 1])
        R = sb("R", [P, T])
        G2 = sb("G2", [LR, L, GW])
        RW = sb("RW", [P, KC, NE])
        LF = sb("LF", [NH, T])
        SM = sb("SM", [P, 256])
        IDXI = sb("IDXI", [P, NS], I32)
        IDX = sb("IDX", [P, L, NS], I32)
        DEC = sb("DEC", [P, 2, NCH])[:, :, :]
        MI = sb("MI", [P, 3, 8], U32)
        PASSES = sb("PASSES", [P, 1], I32)
        ring_high = sbe("ring_high", [P, NSLOT + 1 - NLOW, SLOT])
        Z = sbe("Z", [P, NZ, T])
        ROWS = sbe("ROWS", [NS + 1, 2, COLS])
        PR = sbe("PR", [P, NH * P])
        UP = sbe("UP", [P, 2, KW - 1 + NP])
        UB = sbe("UB", [P, 2, NS, KW])
        TMK = sbe("TMK", [P, 2, GW])
        TMV = sbe("TMV", [P, 2, GW])
        PT = sbe("PT", [P, 3 * P])
        BC = sbe("BC", [P, 2, NP])
        O = sbe("O", [P, 2, T])
        SG = sbe("SG", [P, 2, NS * HD])
        SR = sbe("SR", [P, 2, NS * HD])

        def c_(name, rows=P, a=0, b=None):
            o, w = CCOL[name]
            return C[0:rows, o + a:o + (w if b is None else b)]

        def v_(l, name, i=0, n=1):
            return VT[:, l, VCOL[name] + i:VCOL[name] + i + n]

        ident, ones, heads = c_('ident'), c_('ones'), c_('heads')

        def slot(n):
            return ring_low[:, n, :] if n < NLOW else ring_high[:, n - NLOW, :]

        scr = slot(NSLOT)
        QB = scr[:, 0:2048].rearrange("p (b f) -> p b f", b=NS)
        RN = scr[:, 0:4 * T].rearrange("p (c t) -> p c t", c=4)
        SQ = scr[:, 2048:2048 + 4 * T].rearrange("p (c t) -> p c t", c=4)
        SC = scr[:, 2048:2560].rearrange("p (b h t) -> p b h t", b=NS, h=NH)
        SUF = scr[:, 2560:3072].rearrange("p (b h t) -> p b h t", b=NS, h=NH)
        LP = scr[:, 3072:3584].rearrange("p (b t h) -> p b t h", b=NS, t=TPP)
        PS = scr[:, 0:NH * 3 * P].rearrange("p (h c) -> p h c", h=NH)
        VX = scr[:, 0:2048].rearrange("p (h n v) -> p h n v", h=NH, n=8)
        SH = scr[:, 2048:4096].rearrange("p (c n v) -> p c n v", c=2, n=NCH)
        VE = scr[0:NS, 0:2048].rearrange("p (h b v) -> p h b v", h=NH, b=NS)
        EX = [scr[:, 2048 + 512 * i:2560 + 512 * i] for i in range(2)]
        WX = [scr[:, 3072 + 512 * i:3584 + 512 * i] for i in range(2)]
        TA = [scr[:, 512 * i:512 + 512 * i] for i in range(2)]
        TA2 = scr[:, 1024:1024 + 2 * T].rearrange("p (c t) -> p c t", c=2)
        GM = scr[:, 0:2 * T].rearrange("p (c t) -> p c t", c=2)
        GA = scr[:, 2 * T:4 * T].rearrange("p (c t) -> p c t", c=2)
        BCT, RNG = GM, GA
        GX = Z[:, ZT['cg']:ZT['cg'] + 2, :]
        GQD = Z[:, ZT['fq']:ZT['fq'] + 2, 0:NP]
        GKD = Z[:, ZT['fk']:ZT['fk'] + 2, 0:NP]
        PR4 = PR[:, :].rearrange("p (b h t) -> p b h t", b=NS, h=NH)
        CAT = H
        QS = PT[0:NS, 0:GW]
        KV8 = Z[0:NS, ZT['ca']:ZT['ca'] + 2, :].rearrange("p c t -> p (c t)")[:, 0:2 * GW]
        FX = Z[0:NH, ZT['ff'], :]
        FS = TMK[0:NH].rearrange("p a b -> p (a b)")[:, 0:T]
        SG4 = SG[:, :, :].rearrange("p c (b v) -> p c b v", b=NS)
        SR4 = SR[:, :, :].rearrange("p c (b v) -> p c b v", b=NS)
        AB = Z[:, 8:20, :].rearrange("p (i t) n -> p i t n", i=3)
        YF = Z[:, 20:28, :]
        SA = [SG[:, 0, 0:T], SG[:, 1, 0:T], SR[:, 0, 0:T], SR[:, 1, 0:T]]
        early.close()
        WH = sb("WH", [P, NSPLIT, PIECE], F32R)
        WL = sb("WL", [P, NSPLIT, PIECE], F32R)
        HT = sb("HT", [P, 3, DM])
        Y = sb("Y", [P, KC, T])
        HGH = sb("HGH", [P, KC, P], F32R)
        HGL = sb("HGL", [P, KC, P], F32R)
        SILU = sb("SILU", [P, COLS])
        AM = sb("AM", [P, COLS])
        ATH = sb("ATH", [P, 4, P], F32R)
        ATL = sb("ATL", [P, 4, P], F32R)
        SEL = sb("SEL", [P, 3, P])
        GSEL = sb("GSEL", [P, 3, P])
        GST = sb("GST", [P, T])
        SLG = sb("SLG", [P, 2, 3, NE + 1])
        YS = H[:, :, :].rearrange("p c t -> p (c t)")[:, 0:DM]
        raw = [ring_low[:, i // 2, (i % 2) * PIECE:(i % 2 + 1) * PIECE] for i in range(NRAW)]

        def small(a, n=1, rows=P):
            return SM[0:rows, a:a + n]

        EPSB = small(250)
        def RP(h):
            return scr[:, 1024 + 3 * P * (h % 2):1024 + 3 * P * (h % 2 + 1)]

        def MASK(tt, n):
            return small(128 + NE * tt, NE, n)

        psum = [ctx.enter_context(nc.psum_tensor(f"bank{i}", [P, 512], F32)) for i in range(8)]

        slot_full = [sem(f"slot_full{i}") for i in range(NSLOT)]
        raw_full = [sem(f"raw_full{i}") for i in range(NRAW)]
        pages_full = [sem(f"pages_full{i}") for i in range(NSLOT)]
        consts_in = sem("consts_in")
        states_in = sem("states_in")
        page_idx = sem("page_idx")
        logf_in = sem("logf_in")
        row_done, row_copied = sem("row_done"), sem("row_copied")
        row_turned, row_used = sem("row_turned"), sem("row_used")
        z_done = sem("z_done")
        z_ready = sem("z_ready")
        job_done = sem("job_done")
        job_read = {'a': sem("job_read_act"), 'v': sem("job_read_dve")}
        k_used = sem("k_used")
        out_done = sem("out_done")
        out_added = sem("out_added")
        gu_done = sem("gu_done")
        silu_ready = sem("silu_ready")
        a_ready = sem("a_ready")
        y_done = sem("y_done")
        y_added = sem("y_added")
        h_turned, ht_ready = sem("h_turned"), sem("ht_ready")
        router_done, gates_read, masks_ready = sem("router_done"), sem("gates_read"), sem("masks_ready")
        passes_ready, slots_ready = sem("passes_ready"), sem("slots_ready")
        gather_done, gathered_high, gathered = sem("gather_done"), sem("gathered_high"), sem("gathered")
        gst_done, gst_ready = sem("gate_turn_done"), sem("gate_turned")
        esilu_ready, ea_ready = sem("expert_silu"), sem("expert_act")
        high_ready, low_ready, piece_used = sem("high_ready"), sem("low_ready"), sem("piece_used")
        turn_done, turned_high, turned = sem("act_turn_done"), sem("act_turned_high"), sem("act_turned")
        down_done, y_copied = sem("down_done"), sem("y_copied")
        sel_ready, slots_moved = sem("sel_ready"), sem("slots_moved")
        scatter_done, scattered = sem("scatter_done"), sem("scattered")
        stored = sem("stored")
        k_stored = sem("k_stored")
        ev_ffln = sem("fox_ln")
        idx_ready = sem("idx_ready")
        dve_chain = sem("dve_chain")
        act_chain = sem("act_chain")
        pool_chain = sem("pool_chain")
        ct_ready = sem("ct_ready")
        ev = {n: sem(n) for n in (
            "squares1", "h1", "fox_squares", "fox_qk", "fox_logf", "k_phase", "probs_max", "probs_exp", "probs",
            "row_terms", "past_totals", "max_part", "max_diag", "dec_shift", "dec_exp", "dec_sum", "dec_probs",
            "glu_gate", "glu", "conv_taps", "conv_y", "conv_sq", "conv_rstd", "conv_out", "gla_x", "gla_abs", "gla_ln", "gla_b", "gla_decays",
            "gla_kq", "lag_diff", "lag_exp", "lag_w", "gla_vx", "gla_states", "ve_gla", "s_gla", "o_gla", "gla_sq",
            "gla_rn", "gate_silu", "gla_cat", "rope", "ret_p", "ret_kd", "ve_ret", "s_ret", "o_ret", "ret_sq", "ret_rn", "cat",
            "squares2", "h2", "x_final", "fox_o", "ff_exp")}

        block = ctx.enter_context(nc.Block())

        def unit(u):
            return slot(UPOS[u] % NSLOT)

        def unit_full(u):
            n, pages = UPOS[u], u[0] in 'kv'
            count = sum((v[0] in 'kv') == pages for v in UNITS[n % NSLOT:n + 1:NSLOT])
            return (pages_full if pages else slot_full)[n % NSLOT], 16 * count

        def wait_unit(eng, u):
            eng.wait_ge(*unit_full(u))

        def z_unit_end(l, i):
            return l * NZ + max(n for n, t in enumerate(ZORDER) if t[1] == i) + 1

        def wait_unit_used(eng, u):
            kind, l, i = u
            if kind == 'ada':
                eng.wait_ge(row_done, RPOS[u] + 1)
            elif kind == 'in':
                eng.wait_ge(z_done, z_unit_end(l, i))
            elif kind == 'k':
                eng.wait_ge(k_used, l * NS + i + 1)
            elif kind == 'v':
                eng.wait_ge(row_done, RPOS[('pv', l, i // 2)] + 1)
            elif kind == 'out':
                eng.wait_ge(out_done, l * KC + 4 * (i + 1))
            elif kind in ('w1', 'w3'):
                eng.wait_ge(gu_done, sum(w // P for _, w in FB[:i + 1]))
            else:
                eng.wait_ge(y_done, KC * (i + 1))


        def wait_slot_free(eng, u):
            n = UPOS[u]
            if n >= NSLOT:
                wait_unit_used(eng, UNITS[n - NSLOT])

        def bank(l, name):
            return psum[2 + job_no(l, name) % NBANK]

        class Chain:

            def __init__(self, eng, semaphore):
                self.eng, self.sem, self.n = eng, semaphore, 0

            def add(self, ins):
                self.n += 1
                ins.then_inc(self.sem, 1)

            def wait(self):
                self.eng.wait_ge(self.sem, self.n)

            def __call__(self, ins):
                self.add(ins)
                self.wait()

        row_place, turn_place = {}, {}

        nstored = [0]

        def store(eng, dst, src):
            nstored[0] += 1
            eng.dma_start(dst, src).then_inc(stored, 16)

        @block.sync
        def _(sp):
            for dst, src in ((C[:, :], consts), (VT[:, :, :], vt), (CT[:, :, :], cT), (X[:, :, :], xT),
                             (G2[:, :, :], gate2.rearrange("l r n -> r l n")),
                             (RW[:, :, :], router.rearrange("(c p) e -> p c e", p=P))):
                sp.dma_start(dst, src).then_inc(consts_in, 16)
            for u in UNITS:
                kind, l, i = u
                if kind in 'kv':
                    continue
                wait_slot_free(sp, u)
                dst, full = unit(u), unit_full(u)[0]
                if kind == 'ada':
                    w, n = w_ada[l, :, i * COLS:(i + 1) * COLS], COLS
                elif kind == 'in':
                    n = sum(ZW[g] for g in ZUNITS[i])
                    w = w_in[l, :, ZCOL[ZUNITS[i][0]]:ZCOL[ZUNITS[i][0]] + n]
                elif kind == 'out':
                    w, n = w_out[l, :, i * COLS:(i + 1) * COLS], COLS
                elif kind in ('w1', 'w3'):
                    a, n = FB[i]
                    w = (ffn_w1 if kind == 'w1' else ffn_w3)[l // 2, :, a:a + n]
                else:
                    a, k = FB[i]
                    sp.dma_start(dst[:, 0:k // P * DM].rearrange("p (c n) -> p c n", n=DM),
                                 ffn_w2[l // 2, a:a + k, :].rearrange("(c p) n -> p c n", p=P)).then_inc(full, 16)
                    continue
                sp.dma_start(dst[:, 0:KC * n].rearrange("p (c n) -> p c n", n=n),
                             w.rearrange("(c p) n -> p c n", p=P)).then_inc(full, 16)

            def load_piece(e, q):
                kind, j, half = STREAM[q]
                if kind < 2:
                    w = (moe_w1, moe_w3)[kind][0, bass.ds(e, 1), half * 512:(half + 1) * 512, j * COLS:(j + 1) * COLS]
                    n = COLS
                else:
                    w = moe_w2[0, bass.ds(e, 1), j * COLS + half * 256:j * COLS + (half + 1) * 256, :]
                    n = DM
                sp.dma_start(raw[q % NRAW].rearrange("p (c n) -> p c n", n=n),
                             w.rearrange("e (c p) n -> p (e c) n", p=P)).then_inc(raw_full[q % NRAW], 16)

            def raw_free(p, e, q):
                if q == SPOS[(2, 0, 0)]:
                    return
                if q == SPOS[(2, 0, 0)] - 1:
                    q += 1
                sp.wait_ge(low_ready, p * (NE * NPC) + e * NPC + q - NRAW + 1)

            for q in range(NRAW):
                if q % 2 == 0:
                    wait_unit_used(sp, [u for n, u in enumerate(UNITS) if n % NSLOT == q // 2][-1])
                load_piece(0, q)
            sp.wait_ge(passes_ready, 1)
            passes = sp.value_load(PASSES[0:1, 0:1], min_val=1, max_val=NPASS)
            with sp.Fori(0, NPASS) as p:
                with sp.If(p < passes):
                    with sp.Fori(0, NE - 1) as e:
                        for q in range(NRAW, NPC + NRAW):
                            raw_free(p, e, q)
                            load_piece(e if q < NPC else e + 1, q % NPC)
                    for q in range(NRAW, NPC):
                        raw_free(p, NE - 1, q)
                        load_piece(NE - 1, q)
                    with sp.If(p + 1 < passes):
                        for q in range(NPC, NPC + NRAW):
                            raw_free(p, NE - 1, q)
                            load_piece(0, q % NPC)
            sp.wait_ge(stored, 16 * NSTORES)

        @block.gpsimd
        def _(pool):
            chain = Chain(pool, pool_chain)
            pool.dma_start(IDXI[:, :], ptr).then_inc(page_idx, 16)
            chain(nc.gpsimd.memset(UP[:, :, 0:KW - 1], 0.0))
            G = nc.gpsimd

            def glu(l):
                ca = Z[:, ZT['ca']:ZT['ca'] + 2, :]
                cg = Z[:, ZT['cg']:ZT['cg'] + 2, :]
                pool.wait_ge(ev["glu_gate"], l + 1)
                pool.wait_ge(states_in, 64 * (l + 1))
                chain.add(G.tensor_tensor(UB[:, :, :, KW - 1], ca[:, :, NP:T], cg[:, :, NP:T], ALU.mult))
                G.tensor_tensor(UP[:, :, KW - 1:], ca[:, :, 0:NP], cg[:, :, 0:NP], ALU.mult).then_inc(ev["glu"], 1)
                chain.wait()
                pool.wait_ge(ev["glu"], l + 1)

            def taps(l, first, last):
                y = Z[:, ZT['ca']:ZT['ca'] + 2, 0:NP]
                cw = v_(l, 'conv_w', 0, 2 * KW).rearrange("p (c k) -> p c k", c=2)
                t = O[:, :, 0:NP]
                for k in range(first, last):
                    w = cw[:, :, k:k + 1].to_broadcast([P, 2, NP])
                    chain(G.tensor_tensor(y if k == 0 else t, UP[:, :, k:k + NP], w, ALU.mult))
                    if k:
                        chain(G.tensor_tensor(y, y, t, ALU.add))
                if last == KW:
                    G.memset(small(249), 0.0).then_inc(ev["conv_taps"], 1)
                    pool.wait_ge(ev["conv_taps"], l + 1)

            pool.wait_ge(idx_ready, L)

            def gather_logf(l):
                pool.wait_ge(ev["fox_qk"], l + 1)
                for b in range(NS):
                    nc.gpsimd.indirect_dma_start(
                        scr[:, 3072 + b * TPP * NH:3072 + (b + 1) * TPP * NH], None,
                        cache_logf.rearrange("n l (s t) h -> (n l s) (t h)", t=TPP),
                        bass.IndirectOffsetOnAxis(ap=IDX[:, l, b:b + 1], axis=0)).then_inc(logf_in, 16)

            for l in range(L):
                if l:
                    pool.wait_ge(ev["cat"], l)
                    pool.wait_ge(stored, 16 * STORES_PER_LAYER * l)
                    pool.wait_ge(a_ready, DFF // P)
                for c in range(2):
                    pool.dma_start(UB[:, c, :, 0:KW - 1], conv_in[l, :, c]).then_inc(states_in, 16)
                pool.dma_start(SG[:, :, :], gla_in[l]).then_inc(states_in, 16)
                pool.dma_start(SR[:, :, :], ret_in[l]).then_inc(states_in, 16)
                for kind, cache in (('k', cache_k), ('v', cache_v)):
                    rows = cache.rearrange("n l (s t) h d -> (n l s) (t h d)", t=TPP)
                    for b in range(NS):
                        u = (kind, l, b)
                        if (kind, b) == ('k', 3):
                            glu(l)
                            taps(l, 0, 12)
                        elif kind == 'k' and b > 3:
                            taps(l, 12 + 3 * (b - 4), 15 + 3 * (b - 4))
                        elif (kind, b) == ('v', 0):
                            taps(l, 24, KW)
                        wait_slot_free(pool, u)
                        nc.gpsimd.indirect_dma_start(
                            unit(u), None, rows,
                            bass.IndirectOffsetOnAxis(ap=IDX[:, l, b:b + 1], axis=0)
                        ).then_inc(unit_full(u)[0], 16)
                        if (kind, b) == ('k', 2):
                            gather_logf(l)

        @block.tensor
        def _(pe):
            mm = nc.tensor.matmul
            emitted = {'job': 0, 'step': 0, 'closed': 0}

            def open_job(l, name):
                n = job_no(l, name)
                if n >= NBANK:
                    who, count = read_no(*divmod_job(n - NBANK))
                    pe.wait_ge(job_read[who], count)
                return psum[2 + n % NBANK]

            def close(ins):
                emitted['closed'] += 1
                ins.then_inc(job_done, 1)

            def one(l, name, lhsT, rhs, rows=P, at=0):
                b = open_job(l, name)
                n = rhs.free_size()
                close(mm(b[at:at + rows, 0:n], lhsT, rhs, start=True, stop=True))

            def norm_sum(l, name, src):
                b = open_job(l, name)
                for c in range(KC):
                    ins = mm(b[:, 0:T], ones, src[:, c, :], start=(c == 0), stop=(c == KC - 1))
                close(ins)

            def project(l, i):
                wait_unit(pe, ('in', l, i))
                n = sum(ZW[g] for g in ZUNITS[i])
                w = unit(('in', l, i))[:, 0:KC * n].rearrange("p (c n) -> p c n", n=n)
                for pos, (z, u, col, m) in enumerate(ZORDER):
                    if u != i:
                        continue
                    if l * NZ + pos >= 2:
                        pe.wait_ge(z_ready, l * NZ + pos - 1)
                    for c in range(KC):
                        ins = mm(psum[pos % 2][0:m, 0:T], w[:, c, col:col + m], H[:, c, :],
                                 start=(c == 0), stop=(c == KC - 1))
                    ins.then_inc(z_done, 1)

            def turn(out, src, rows):
                return nc.tensor.transpose(out, src, ident[0:rows, 0:rows])

            def token_major(l, name, tt, tiles):
                b = open_job(l, name)
                for n, src in enumerate(tiles):
                    ins = turn(b[:, n * P:(n + 1) * P], src[:, tt * P:(tt + 1) * P], P)
                close(ins)

            def sample_outer(l, names, kcol):
                for pr in range(2):
                    b = open_job(l, names[pr])
                    for s in range(2):
                        h = 2 * pr + s
                        ins = mm(b[s * HD:(s + 1) * HD, :], KV8[:, kcol + h * HD:kcol + (h + 1) * HD],
                                 VE[:, h].rearrange("p b v -> p (b v)"), start=True, stop=True)
                    close(ins)

            def sample_read(l, names, S4, q):
                for s in range(2):
                    b = open_job(l, names[s])
                    for pr in range(2):
                        for i in range(NS):
                            ins = mm(b[s * HD:(s + 1) * HD, pr * NS + i:pr * NS + i + 1],
                                     S4[s * HD:(s + 1) * HD, pr, i, :],
                                     q[s * HD:(s + 1) * HD, pr, NP + i:NP + i + 1], start=True, stop=True)
                    close(ins)

            def row_product(job, step):
                kind, l, i = job
                n = RPOS[job]
                if step == 0:
                    if n >= 1:
                        pe.wait_ge(row_copied, n)
                    if kind == 'pv' and i == 0:
                        pe.wait_ge(ev["dec_probs"], l + 1)
                if kind == 'ada':
                    if step == 0:
                        wait_unit(pe, job)
                    w = unit(job).rearrange("p (c n) -> p c n", n=COLS)
                    ins = mm(psum[0][0:NS + 1, :], CT[:, step, :], w[:, step, :],
                             start=(step == 0), stop=(step == KC - 1))
                else:
                    half, t = step // TPP, step % TPP
                    v = ('v', l, 2 * i + half)
                    if t == 0:
                        wait_unit(pe, v)
                    ins = mm(psum[0][0:NH, half * GW:(half + 1) * GW], PR4[:, v[2], :, t],
                             unit(v)[:, t * GW:(t + 1) * GW], start=(t == 0), stop=(t == TPP - 1))
                if step == row_steps(job) - 1:
                    ins.then_inc(row_done, 1)
                    row_place[n] = emitted['closed']

            def turn_rows(job):
                n = RPOS[job]
                pe.wait_ge(row_copied, n + 1)
                if n >= 1:
                    pe.wait_ge(row_used, n)
                r = ROWS[:, n % 2, :]
                if job[0] == 'ada':
                    for q in range(4):
                        ins = mm(psum[1][:, q * (NS + 1):(q + 1) * (NS + 1)], r[:, q * P:(q + 1) * P],
                                 ident[0:NS + 1, 0:NS + 1], start=True, stop=True)
                else:
                    for q in range(4):
                        ins = mm(psum[1][:, 2 * q:2 * q + 2], r[0:NH, q * P:(q + 1) * P],
                                 ident[0:NH, 2 * (q % 2):2 * (q % 2) + 2], start=True, stop=True)
                ins.then_inc(row_turned, 1)
                turn_place[n] = emitted['closed']

            def row_steps(job):
                return KC if job[0] == 'ada' else 2 * TPP


            def background(jobs, count):
                for _ in range(count):
                    if emitted['job'] >= RPOS[jobs[-1]] + 1:
                        return
                    job, step = ROWJOBS[emitted['job']], emitted['step']
                    row_product(job, step)
                    if step == row_steps(job) // 2 - 1 and job != jobs[0]:
                        turn_rows(ROWJOBS[emitted['job'] - 1])
                    emitted['step'] += 1
                    if emitted['step'] == row_steps(job):
                        emitted['job'] += 1
                        emitted['step'] = 0

            def finish_background(jobs):
                background(jobs, 1000)
                turn_rows(jobs[-1])

            pe.wait_ge(consts_in, 16 * 6)
            for l in range(L):
                def bg(count):
                    background(ROWS_OF[l], count)

                if l == 0:
                    pe.wait_ge(ct_ready, 1)
                    background(ROWS_FIRST, KC * len(ROWS_FIRST))
                    turn_rows(ROWS_FIRST[-1])
                pe.wait_ge(ev["squares1"], l + 1)
                norm_sum(l, 'rms1', H)
                pe.wait_ge(ev["h1"], l + 1)
                if l == 0:
                    pe.wait_ge(row_used, len(ROWS_FIRST))
                for i in range(3):
                    project(l, i)
                pe.wait_ge(ev["fox_squares"], l + 1)
                for i in range(4):
                    one(l, f'fn{i}', heads, SQ[:, i, :])
                pe.wait_ge(ev["fox_qk"], l + 1)
                fk = Z[:, ZT['fk']:ZT['fk'] + 2, :]
                fq = Z[:, ZT['fq']:ZT['fq'] + 2, :]
                fv = Z[:, ZT['fv']:ZT['fv'] + 2, :]
                for tt in range(2):
                    token_major(l, f'tkv{tt}', tt, (fv[:, 0, :], fv[:, 1, :]))
                b = open_job(l, 'tqs')
                for n in range(2):
                    ins = turn(b[0:NS, n * P:(n + 1) * P], fq[:, n, NP:T], P)
                close(ins)
                for i in range(4):
                    b = open_job(l, f'qb{i}')
                    if i == 0:
                        who, count = read_no(l, 'tqs')
                        pe.wait_ge(job_read[who], count)
                    for n in range(2):
                        ins = mm(b[:, n * GW:(n + 1) * GW], ident[0:NS, 2 * i + n:2 * i + n + 1].to_broadcast([NS, P]),
                                 QS[:, :], start=True, stop=True)
                    close(ins)
                for i in range(3, 8):
                    project(l, i)
                pe.wait_ge(z_ready, (l + 1) * NZ)
                pe.wait_ge(ev["fox_logf"], l + 1)
                for h in range(NH):
                    c, s = h // 2, (h % 2) * HD
                    b = open_job(l, f's{h}')
                    row = ident[0:NH, h:h + 1].to_broadcast([NH, P])
                    for at, qt, kt in ((0, 0, 0), (P, 1, 0), (2 * P, 1, 1)):
                        o = b[:, at:at + P]
                        mm(o, fq[s:s + HD, c, qt * P:(qt + 1) * P], fk[s:s + HD, c, kt * P:(kt + 1) * P],
                           start=True, stop=False)
                        mm(o, FS[:, qt * P:(qt + 1) * P], row, start=False, stop=False)
                        ins = mm(o, row, FX[:, kt * P:(kt + 1) * P], start=False, stop=True)
                    close(ins)
                bg(16)
                for h in range(NH):
                    c, s = h // 2, (h % 2) * HD
                    bg(1)
                    pe.wait_ge(ev["probs"], l * NH + h + 1)
                    b = open_job(l, f'pt{h}')
                    for at in range(3):
                        ins = turn(b[:, at * P:(at + 1) * P], PS[:, h, at * P:(at + 1) * P], P)
                    close(ins)
                    b = open_job(l, f'o{h}')
                    who, count = read_no(l, f'pt{h}')
                    pe.wait_ge(job_read[who], count)
                    o = b[s:s + HD, :]
                    mm(o[:, 0:NP], TMV[:, 0, h * HD:(h + 1) * HD], PT[:, 0:NP], start=True, stop=False)
                    close(mm(o[:, P:NP], TMV[:, 1, h * HD:(h + 1) * HD], PT[:, NP:3 * P], start=False, stop=True))
                pe.wait_ge(ev["row_terms"], l + 1)
                one(l, 'snew', ones, small(64, 32))
                pe.wait_ge(ev["past_totals"], l + 1)
                b = open_job(l, 'suf')
                mm(b[:, 0:32], c_('later'), small(96, 32), start=True, stop=False)
                close(mm(b[:, 0:32], c_('ones', NH), small(128, 32, NH), start=False, stop=True))
                pe.wait_ge(ev["max_part"], l + 1)
                b = open_job(l, 'mxt')
                close(turn(b[0:32, 0:P], small(160, 32), P))
                pe.wait_ge(ev["max_diag"], l + 1)
                one(l, 'mxb', c_('ones', 32), small(192, 32, 32))
                pe.wait_ge(ev["dec_sum"], l + 1)
                one(l, 'sumb', ones, small(64, 32))
                pe.wait_ge(ev["dec_probs"], l + 1)
                cy = Z[:, ZT['ca']:ZT['ca'] + 2, :]
                pe.wait_ge(ev["conv_y"], l + 1)
                b = open_job(l, 'mean')
                for c in range(2):
                    ins = mm(b[:, 0:T], ones, cy[:, c, :], start=(c == 0), stop=(c == 1))
                close(ins)
                pe.wait_ge(ev["conv_sq"], l + 1)
                b = open_job(l, 'var')
                for c in range(2):
                    ins = mm(b[:, 0:T], ones, TA2[:, c, :], start=(c == 0), stop=(c == 1))
                close(ins)
                gv = Z[:, ZT['gv']:ZT['gv'] + 2, :]
                gq = Z[:, ZT['gq']:ZT['gq'] + 2, :]
                gk = Z[:, ZT['gk']:ZT['gk'] + 2, :]
                for c in range(2):
                    one(l, f'gate{c}', G2[:, l, c * P:(c + 1) * P], Z[0:LR, ZT['glr'], :])
                for lag in range(CH):
                    bg(LAG_BG[l])
                    pe.wait_ge(ev["lag_w"], l * CH + lag + 1)
                    b = open_job(l, f'att{lag}')
                    n = NCH * (CH - lag)
                    for c in range(2):
                        ins = mm(b[:, c * n:(c + 1) * n], heads, WX[lag % 2][:, c * n:(c + 1) * n],
                                 start=True, stop=True)
                    close(ins)
                bg(REST_BG[l])
                pe.wait_ge(ev["gla_kq"], l + 1)
                for tt in range(2):
                    token_major(l, f'gkv{tt}', tt, (GKD[:, 0, :], GKD[:, 1, :], gv[:, 0, :], gv[:, 1, :]))
                b = open_job(l, 'gts')
                for n, src in enumerate((gk[:, 0, NP:T], gk[:, 1, NP:T], gv[:, 0, NP:T], gv[:, 1, NP:T])):
                    ins = turn(b[0:NS, n * P:(n + 1) * P], src, P)
                close(ins)
                for tt in range(2):
                    bg(REST_BG[l])
                    pe.wait_ge(ev["gla_vx"], l * 2 + tt + 1)
                    for pr in range(2):
                        b = open_job(l, f'kv{tt}{pr}')
                        for s in range(2):
                            h = 2 * pr + s
                            ins = mm(b[s * HD:(s + 1) * HD, :], TMK[:, tt, h * HD:(h + 1) * HD],
                                     VX[:, h].rearrange("p n v -> p (n v)"), start=True, stop=True)
                        close(ins)
                bg(REST_BG[l])
                pe.wait_ge(ev["gla_states"], l + 1)
                for s in range(2):
                    b = open_job(l, f'gi{s}')
                    for pr in range(2):
                        for n in range(1, NCH):
                            o = pr * NP + n * CH
                            ins = mm(b[s * HD:(s + 1) * HD, o:o + CH], SH[s * HD:(s + 1) * HD, pr, n - 1, :],
                                     GQD[s * HD:(s + 1) * HD, pr, n * CH:(n + 1) * CH], start=True, stop=True)
                    close(ins)
                pe.wait_ge(ev["ve_gla"], l + 1)
                sample_outer(l, ('gx0', 'gx1'), 0)
                pe.wait_ge(ev["s_gla"], l + 1)
                sample_read(l, ('gs0', 'gs1'), SG4, gq)
                pe.wait_ge(ev["gla_sq"], l + 1)
                for c in range(2):
                    one(l, f'gn{c}', heads, BCT[:, c, :])
                rv = Z[:, ZT['rv']:ZT['rv'] + 2, :]
                rq = Z[:, ZT['rq']:ZT['rq'] + 2, :]
                rk = Z[:, ZT['rk']:ZT['rk'] + 2, :]
                bg(REST_BG[l])
                for i in range(4):
                    one(l, f'rr{i}', c_('swap'), Z[:, ZT['rq'] + i, :])
                bg(REST_BG[l])
                pe.wait_ge(ev["rope"], l + 1)
                for tt in range(2):
                    token_major(l, f'rkv{tt}', tt, (rk[:, 0, :], rk[:, 1, :], rv[:, 0, :], rv[:, 1, :]))
                b = open_job(l, 'rts')
                for n, src in enumerate((rk[:, 0, NP:T], rk[:, 1, NP:T], rv[:, 0, NP:T], rv[:, 1, NP:T])):
                    ins = turn(b[0:NS, n * P:(n + 1) * P], src, P)
                close(ins)
                who, count = read_no(l, 'rts')
                pe.wait_ge(job_read[who], count)
                for h in range(NH):
                    c, s = h // 2, (h % 2) * HD
                    b = open_job(l, f'rs{h}')
                    mm(b[:, 0:NP], rk[s:s + HD, c, 0:P], rq[s:s + HD, c, 0:NP], start=True, stop=True)
                    close(mm(b[:, NP:3 * P], rk[s:s + HD, c, P:NP], rq[s:s + HD, c, P:NP], start=True, stop=True))
                    pe.wait_ge(ev["ret_p"], l * NH + h + 1)
                    b = open_job(l, f'ro{h}')
                    o = b[s:s + HD, :]
                    mm(o[:, 0:NP], TMV[:, 0, h * HD:(h + 1) * HD], RP(h)[:, 0:NP], start=True, stop=False)
                    close(mm(o[:, P:NP], TMV[:, 1, h * HD:(h + 1) * HD], RP(h)[:, NP:3 * P], start=False, stop=True))
                bg(REST_BG[l])
                pe.wait_ge(ev["ret_kd"], l + 1)
                b = open_job(l, 'rst')
                for h in range(NH):
                    c, s = h // 2, (h % 2) * HD
                    for tt in range(2):
                        ins = mm(b[s:s + HD, c * HD:(c + 1) * HD], TMK[:, tt, h * HD:(h + 1) * HD],
                                 TMV[:, tt, h * HD:(h + 1) * HD], start=(tt == 0), stop=(tt == 1))
                close(ins)
                bg(REST_BG[l])
                pe.wait_ge(ev["ve_ret"], l + 1)
                sample_outer(l, ('rx0', 'rx1'), 0)
                pe.wait_ge(ev["s_ret"], l + 1)
                sample_read(l, ('rd0', 'rd1'), SR4, rq)
                finish_background(ROWS_OF[l])
                pe.wait_ge(ev["ret_sq"], l + 1)
                for c in range(2):
                    one(l, f'rn{c}', heads, BCT[:, c, :])
                pe.wait_ge(row_used, RPOS[ROWS_OF[l][-1]] + 1)
                pe.wait_ge(ev["cat"], l + 1)
                for m in range(KC):
                    if m % 4 == 0:
                        wait_unit(pe, ('out', l, m // 4))
                    w = unit(('out', l, m // 4)).rearrange("p (c n) -> p c n", n=COLS)
                    if m >= 2:
                        pe.wait_ge(out_added, l * KC + m - 1)
                    for c in range(KC):
                        ins = mm(psum[m % 2][:, 0:T], w[:, c, (m % 4) * P:(m % 4 + 1) * P], CAT[:, c, :],
                                 start=(c == 0), stop=(c == KC - 1))
                    ins.then_inc(out_done, 1)
                pe.wait_ge(ev["squares2"], l + 1)
                norm_sum(l, 'rms2', Z[:, 0:KC, :])
                pe.wait_ge(ev["h2"], l + 1)
                if l % 2 == 0:
                    tiles = 0
                    for j in range(len(FB) + 1):
                        if j < len(FB):
                            a, n = FB[j]
                            wait_unit(pe, ('w1', l, j))
                            wait_unit(pe, ('w3', l, j))
                            for t in range(n // P):
                                if tiles >= 2:
                                    pe.wait_ge(a_ready, tiles - 1)
                                for k, kind in enumerate(('w1', 'w3')):
                                    w = unit((kind, l, j))[:, 0:KC * n].rearrange("p (c n) -> p c n", n=n)
                                    for c in range(KC):
                                        ins = mm(psum[2 * (tiles % 2) + k][:, 0:T], w[:, c, t * P:(t + 1) * P],
                                                 H[:, c, :], start=(c == 0), stop=(c == KC - 1))
                                ins.then_inc(gu_done, 1)
                                tiles += 1
                        if j >= 1:
                            i = j - 1
                            nk = FB[i][1] // P
                            wait_unit(pe, ('w2', l, i))
                            pe.wait_ge(a_ready, sum(w // P for _, w in FB[:j]))
                            w = unit(('w2', l, i))[:, 0:nk * DM].rearrange("p (c n) -> p c n", n=DM)
                            for m in range(KC):
                                if KC * i + m >= 4:
                                    pe.wait_ge(y_added, KC * i + m - 3)
                                for k in range(nk):
                                    ins = mm(psum[4 + m % 4][:, 0:T], w[:, k, m * P:(m + 1) * P],
                                             AB[:, i % 3, k, :], start=(k == 0), stop=(k == nk - 1))
                                ins.then_inc(y_done, 1)
                else:
                    rows = (P, P, NS)
                    for tt, n in enumerate(rows):
                        for c in range(KC):
                            ins = mm(psum[0][0:n, tt * NE:(tt + 1) * NE], H[:, c, tt * P:tt * P + n], RW[:, c, :],
                                     start=(c == 0), stop=(c == KC - 1))
                    ins.then_inc(router_done, 1)
                    pe.wait_ge(out_added, l * KC + KC)
                    for i in range(6):
                        tt, half = i // 2, i % 2
                        n = rows[tt]
                        for q in range(4):
                            ins = turn(psum[2 + i][0:n, q * P:(q + 1) * P], H[:, 4 * half + q, tt * P:tt * P + n], P)
                        ins.then_inc(h_turned, 1)
                    pe.wait_ge(masks_ready, 3)
                    for tt, n in enumerate(rows):
                        o = psum[1][0:n, tt * NE:(tt + 1) * NE]
                        mm(o, c_('later', n, 0, n), MASK(tt, n), start=True, stop=(tt == 2))
                        for t2 in range(tt + 1, 3):
                            mm(o, c_('ones', rows[t2], 0, n), MASK(t2, rows[t2]), start=False, stop=(t2 == 2))
                    for tt, n in enumerate(rows):
                        ins = mm(psum[1][:, 3 * NE:4 * NE], c_('ones', n), MASK(tt, n), start=(tt == 0), stop=(tt == 2))
                    ins.then_inc(router_done, 1)
                    pe.wait_ge(ht_ready, 6)
                    pe.wait_ge(passes_ready, 1)
                    passes = pe.value_load(PASSES[0:1, 0:1], min_val=1, max_val=NPASS)

                    def gather(slots, free):
                        pe.wait_ge(slots_ready, slots)
                        for half in range(2):
                            if free:
                                pe.wait_ge(*free[half])
                            for q in range(4):
                                c = 4 * half + q
                                for tt, n in enumerate(rows):
                                    ins = mm(psum[6 + half][:, q * P:(q + 1) * P], HT[0:n, tt, c * P:(c + 1) * P],
                                             SEL[0:n, tt, :], start=(tt == 0), stop=(tt == 2))
                            ins.then_inc(gather_done, 1)

                    def three(out, high, low, wh, wl, start, stop):
                        mm(out, high, wh, start=start, stop=False)
                        mm(out, high, wl, start=False, stop=False)
                        return mm(out, low, wh, start=False, stop=stop)

                    def expert(p, e):
                        def at(per, n):
                            return p * (NE * per) + e * per + n

                        def piece(kind, j, half):
                            q = SPOS[(kind, j, half)]
                            pe.wait_ge(low_ready, at(NPC, q + 1))
                            n = DM if kind == 2 else COLS
                            return [t[:, q % NSPLIT, :].rearrange("p (c n) -> p c n", n=n) for t in (WH, WL)]

                        def up(kind, j):
                            for half in range(2):
                                wh, wl = piece(kind, j, half)
                                for i in range(4):
                                    c = 4 * half + i
                                    ins = three(psum[2 * (j % 2) + kind][:, :], HGH[:, c, :], HGL[:, c, :],
                                                wh[:, i, :], wl[:, i, :], c == 0, c == KC - 1)
                                ins.then_inc(piece_used, 1)

                        def turn_block(j):
                            pe.wait_ge(ea_ready, at(EB, j + 2))
                            pe.wait_ge(*((scattered, at(KC, 7)), (turned, at(EB, 1)), (gst_ready, at(1, 1)))[j] if j < 3
                                       else (turned, at(EB, j - 1)))
                            b = 6 + (j > 0) * (j + 1) % 2
                            for k in range(4):
                                ins = turn(psum[b][:, k * P:(k + 1) * P], AM[:, k * P:(k + 1) * P], P)
                            ins.then_inc(turn_done, 1)

                        def down(j):
                            pe.wait_ge(turned, at(EB, j + 1))
                            for i in range(2):
                                wh, wl = piece(2, j, i)
                                for half in range(2):
                                    if j == 0 and i == 0:
                                        pe.wait_ge(y_copied, at(2, 1 + half))
                                    for k in range(2):
                                        cols = slice(half * 512, (half + 1) * 512)
                                        ins = three(psum[4 + half][:, :], ATH[:, 2 * i + k, :], ATL[:, 2 * i + k, :],
                                                    wh[:, k, cols], wl[:, k, cols], j == 0 and i == 0 and k == 0,
                                                    j == EB - 1 and i == 1 and k == 1)
                                    if half == 0 and i == 1:
                                        ins.then_inc(down_done, 1)
                                ins.then_inc(piece_used, 1)

                        for j in range(EB):
                            if j == 0:
                                pe.wait_ge(gathered, at(2, 2))
                            if j != 1:
                                pe.wait_ge(ea_ready, at(EB, max(j, 1)))
                            up(0, j)
                            if j >= 1:
                                turn_block(j - 1)
                            if j == 1:
                                pe.wait_ge(scattered, at(KC, 8))
                                for tt, n in enumerate(rows):
                                    ins = turn(psum[7][:, tt * P:tt * P + n], GSEL[0:n, tt, :], n)
                                ins.then_inc(gst_done, 1)
                            up(1, j)
                            if j >= 1:
                                down(j - 1)
                        turn_block(EB - 1)
                        gather(at(1, 2), [(turned, at(EB, EB - 1)), (turned, at(EB, EB))])
                        down(EB - 1)
                        for m in range(KC):
                            if m % 4 == 0:
                                pe.wait_ge(y_copied, at(2, 3 + m // 4))
                            if m < 2:
                                pe.wait_ge(gathered, at(2, 3 + m))
                            else:
                                pe.wait_ge(scattered, at(KC, KC + m - 1))
                            mm(psum[6 + m % 2][:, 0:T], YS[:, m * P:(m + 1) * P], GST[:, :], start=True,
                               stop=True).then_inc(scatter_done, 1)

                    gather(1, None)
                    with pe.Fori(0, NPASS) as p:
                        with pe.If(p < passes):
                            with pe.Fori(0, NE) as e:
                                expert(p, e)

        @block.scalar
        def _(act):
            chain = Chain(act, act_chain)
            A = nc.scalar.activation
            act.wait_ge(consts_in, 16 * 6)
            A(CT[:, :, :], CT[:, :, :], ACT.Silu).then_inc(ct_ready, 1)

            def rows(l, name):
                n = job_no(l, name)
                while True:
                    if turned[0] in turn_place and turned[0] < copied[0] and turn_place[turned[0]] <= n and (
                            copied[0] not in row_place or turn_place[turned[0]] <= row_place[copied[0]]):
                        use_rows(ROWJOBS[turned[0]])
                        turned[0] += 1
                    elif copied[0] in row_place and row_place[copied[0]] <= n:
                        copy_rows(ROWJOBS[copied[0]])
                        copied[0] += 1
                    else:
                        return

            copied, turned = [0], [0]

            def copy_rows(job):
                n, kind = RPOS[job], job[0]
                act.wait_ge(row_done, n + 1)
                if n >= 2:
                    act.wait_ge(row_turned, n - 1)
                r = NS + 1 if kind == 'ada' else NH
                A(ROWS[0:r, n % 2, :], psum[0][0:r, :], ACT.Copy).then_inc(row_copied, 1)

            def use_rows(job):
                kind, l, i = job
                act.wait_ge(row_turned, RPOS[job] + 1)
                if kind == 'ada':
                    for q in range(4):
                        ins = A(MOD[:, l, 4 * i + q, :], psum[1][:, q * (NS + 1):(q + 1) * (NS + 1)], ACT.Identity,
                                bias=v_(l, 'b_ada', 4 * i + q))
                        if q < 3:
                            chain.add(ins)
                    chain.wait()
                else:
                    ins = A(small(96 + 8 * i, 8), psum[1][:, 0:8], ACT.Copy)
                ins.then_inc(row_used, 1)

            def job(l, name):
                rows(l, name)
                act.wait_ge(job_done, job_no(l, name) + 1)
                return bank(l, name)

            def read(ins):
                ins.then_inc(job_read['a'], 1)

            def wait_read(l, name):
                act.wait_ge(job_read['a'], read_no(l, name)[1])

            def evacuate(l, i):
                for pos, (z, u, col, m) in enumerate(ZORDER):
                    if u == i:
                        act.wait_ge(z_done, l * NZ + pos + 1)
                        A(Z[0:m, z, :], psum[pos % 2][0:m, 0:T], ACT.Copy).then_inc(z_ready, 1)

            def log_sigmoid(x, e, ready, ready_n, exp_done, done):
                act.wait_ge(ready, ready_n)
                chain(A(e, e, ACT.Exp, scale=-1.0))
                A(e, e, ACT.Ln, bias=1.0).then_inc(done, 1)

            for l in range(L):
                if l:
                    act.wait_ge(stored, 16 * nstored[0])
                A(R[:, :], job(l, 'rms1')[:, 0:T], ACT.Sqrt, bias=EPSB, scale=1.0 / DM).then_inc(job_read['a'], 1)
                for i in range(3):
                    evacuate(l, i)
                act.wait_ge(z_ready, l * NZ + ZPOS[ZT['cg'] + 1] + 1)
                cg = Z[:, ZT['cg']:ZT['cg'] + 2, :]
                A(cg, cg, ACT.Sigmoid).then_inc(ev["glu_gate"], 1)
                for i in range(4):
                    read(A(RN[:, i, :], job(l, f'fn{i}')[:, 0:T], ACT.Sqrt, bias=EPSB, scale=1.0 / HD))
                for tt in range(2):
                    b = job(l, f'tkv{tt}')
                    read(A(TMV[:, tt, :], b[:, 0:GW], ACT.Copy))
                read(A(QS[:, :], job(l, 'tqs')[0:NS, 0:GW], ACT.Copy))
                for i in range(4):
                    read(A(QB[:, 2 * i:2 * i + 2, :].rearrange("p b f -> p (b f)"), job(l, f'qb{i}')[:, :], ACT.Copy))
                act.wait_ge(ev["fox_qk"], l + 1)
                act.dma_start(k_out[l], Z[:, ZT['fk']:ZT['fk'] + 2, :]).then_inc(k_stored, 16)
                act.wait_ge(z_ready, l * NZ + ZPOS[ZT['fv'] + 1] + 1)
                store(act, v_out[l], Z[:, ZT['fv']:ZT['fv'] + 2, :])
                act.wait_ge(ev["ff_exp"], l + 1)
                chain(A(LF[:, :], LF[:, :], ACT.Exp, scale=-1.0))
                A(LF[:, :], LF[:, :], ACT.Ln, bias=1.0).then_inc(ev_ffln, 1)
                act.wait_ge(ev["fox_logf"], l + 1)
                store(act, logf_out[l], LF[:, :])
                for i in range(3, 8):
                    evacuate(l, i)
                act.wait_ge(ev["glu"], l + 1)
                for c in range(2):
                    store(act, conv_out[l, :, c, 0:KW - 1], UP[:, c, NP:NP + KW - 1])
                    store(act, conv_out[l, :, c, KW - 1:(NS + 1) * (KW - 1)].rearrange("p (b k) -> p b k", b=NS),
                          UB[:, c, :, 1:KW])
                rows(l, 'pt0')
                for h in range(NH):
                    act.wait_ge(ev["probs_max"], l * NH + h + 1)
                    A(PS[:, h, 0:P], PS[:, h, 0:P], ACT.Exp, bias=small(2 * h), accum_out=small(8 + 2 * h)).then_inc(ev["probs_exp"], 1)
                    A(PS[:, h, P:3 * P], PS[:, h, P:3 * P], ACT.Exp, bias=small(2 * h + 1),
                      accum_out=small(9 + 2 * h)).then_inc(ev["probs_exp"], 1)
                for h in range(NH):
                    c, s = h // 2, (h % 2) * HD
                    read(A(PT[:, :], job(l, f'pt{h}')[:, 0:3 * P], ACT.Copy))
                    read(A(CAT[s:s + HD, 2 + c, 0:NP], job(l, f'o{h}')[s:s + HD, 0:NP], ACT.Copy))
                rows(l, 'mxb')
                act.wait_ge(ev["dec_shift"], l + 1)
                chain.add(A(PR[:, :], PR[:, :], ACT.Exp))
                A(small(32, 32), small(32, 32), ACT.Exp).then_inc(ev["dec_exp"], 1)
                read(A(R[:, :], job(l, 'var')[:, 0:T], ACT.Sqrt, bias=EPSB, scale=1.0 / GW))
                act.wait_ge(ev["conv_out"], l + 1)
                A(CAT[:, 0:2, :], CAT[:, 0:2, :], ACT.Silu).then_inc(ev["gate_silu"], 1)
                for g in ('go', 'rg'):
                    z = Z[:, ZT[g]:ZT[g] + 2, :]
                    A(z, z, ACT.Silu).then_inc(ev["gate_silu"], 1)
                act.wait_ge(ev["gla_abs"], l + 1)
                chain(A(GA, GA, ACT.Exp, scale=-1.0))
                A(GA, GA, ACT.Ln, bias=1.0).then_inc(ev["gla_ln"], 1)
                act.wait_ge(ev["gla_b"], l + 1)
                chain.add(A(GQD, BC[:, :, :], ACT.Exp))
                chain.add(A(GKD, GKD, ACT.Exp))
                chain.add(A(DEC, DEC, ACT.Exp))
                A(GX, GX, ACT.Exp).then_inc(ev["gla_decays"], 1)
                for lag in range(1, CH):
                    rows(l, f'att{lag}')
                    act.wait_ge(ev["lag_diff"], l * (CH - 1) + lag)
                    n = 2 * NCH * (CH - lag)
                    A(EX[lag % 2][:, 0:n], EX[lag % 2][:, 0:n], ACT.Exp).then_inc(ev["lag_exp"], 1)
                for tt in range(2):
                    b = job(l, f'gkv{tt}')
                    chain.add(A(TMK[:, tt, :], b[:, 0:GW], ACT.Copy))
                    read(A(TMV[:, tt, :], b[:, GW:2 * GW], ACT.Copy))
                read(A(KV8[:, :], job(l, 'gts')[0:NS, :], ACT.Copy))
                rows(l, 'kv11')
                act.wait_ge(ev["gla_states"], l + 1)
                store(act, gla_out[l, :, :, 0:HD], SH[:, :, NCH - 1, :])
                rows(l, 'gx1')
                act.wait_ge(ev["s_gla"], l + 1)
                store(act, gla_out[l, :, :, HD:(NS + 1) * HD], SG[:, :, :])
                for c in range(2):
                    read(A(RNG[:, c, :], job(l, f'gn{c}')[:, 0:T], ACT.Sqrt, bias=EPSB, scale=1.0 / HD))
                for tt in range(2):
                    b = job(l, f'rkv{tt}')
                    chain.add(A(TMK[:, tt, :], b[:, 0:GW], ACT.Copy))
                    read(A(TMV[:, tt, :], b[:, GW:2 * GW], ACT.Copy))
                read(A(KV8[:, :], job(l, 'rts')[0:NS, :], ACT.Copy))
                act.wait_ge(ev["gla_cat"], l + 1)
                for h in range(NH):
                    c, s = h // 2, (h % 2) * HD
                    read(A(O[s:s + HD, c, 0:NP], job(l, f'ro{h}')[s:s + HD, 0:NP], ACT.Copy))
                read(A(PT[:, 0:P], job(l, 'rst')[:, 0:P], ACT.Copy))
                wait_read(l, 'rst')
                store(act, ret_out[l, :, :, 0:HD], PT[:, 0:P].rearrange("p (c v) -> p c v", c=2))
                rows(l, 'rx1')
                act.wait_ge(ev["s_ret"], l + 1)
                store(act, ret_out[l, :, :, HD:(NS + 1) * HD], SR[:, :, :])
                for c in range(2):
                    read(A(RNG[:, c, :], job(l, f'rn{c}')[:, 0:T], ACT.Sqrt, bias=EPSB, scale=1.0 / HD))
                read(A(R[:, :], job(l, 'rms2')[:, 0:T], ACT.Sqrt, bias=EPSB, scale=1.0 / DM))
                if l % 2 == 0:
                    n = 0
                    act.wait_ge(stored, 16 * nstored[0])
                    for j in range(len(FB)):
                        for t in range(FB[j][1] // P):
                            act.wait_ge(gu_done, n + 1)
                            if n >= 4:
                                act.wait_ge(a_ready, n - 3)
                            A(SA[n % 4], psum[2 * (n % 2)][:, 0:T], ACT.Silu).then_inc(silu_ready, 1)
                            n += 1
                else:
                    act.wait_ge(stored, 16 * nstored[0])
                    act.wait_ge(gates_read, 1)
                    A(small(40, 3), small(40, 3), ACT.Exp).then_inc(gates_read, 1)
                    for i in range(6):
                        n = P if i < 4 else NS
                        act.wait_ge(h_turned, i + 1)
                        A(HT[0:n, i // 2, (i % 2) * 512:(i % 2 + 1) * 512], psum[2 + i][0:n, :], ACT.Copy).then_inc(ht_ready, 1)
                    chain(A(small(247), EPSB, ACT.Copy))
                    A(small(247), EPSB, ACT.Copy).then_inc(y_copied, 2)
                    act.wait_ge(passes_ready, 1)
                    passes = act.value_load(PASSES[0:1, 0:1], min_val=1, max_val=NPASS)

                    def round_gathered(half, count):
                        act.wait_ge(gather_done, count)
                        A(HGH[:, 4 * half:4 * half + 4, :].rearrange("p c s -> p (c s)"), psum[6 + half][:, :],
                          ACT.Copy).then_inc(gathered_high, 1)

                    for n in range(NLOW, NSLOT):
                        wait_unit_used(act, [u for i, u in enumerate(UNITS) if i % NSLOT == n][-1])
                    for half in range(2):
                        round_gathered(half, half + 1)

                    def expert(p, e):
                        def at(per, n):
                            return p * (NE * per) + e * per + n

                        def round_piece(q):
                            act.wait_ge(raw_full[q % NRAW], at(16 * (NPC // NRAW), 16 * (q // NRAW + 1)))
                            act.wait_ge(piece_used, at(NPC, q + 1))
                            A(WH[:, q % NSPLIT, :], raw[q % NRAW], ACT.Copy).then_inc(high_ready, 1)

                        def round_turned(j):
                            act.wait_ge(turn_done, at(EB, j + 1))
                            A(ATH[:, :, :].rearrange("p k s -> p (k s)"), psum[6 + (j > 0) * (j + 1) % 2][:, :],
                              ACT.Copy).then_inc(turned_high, 1)

                        for q in range(NPC):
                            round_piece(q)
                            for j in range(EB):
                                if q == SPOS[(0, j, 0)] + 3:
                                    if j >= 1:
                                        round_turned(j - 1)
                                    if j == 1:
                                        act.wait_ge(gst_done, at(1, 1))
                                        A(GST[:, :], psum[7][:, 0:T], ACT.Copy).then_inc(gst_ready, 1)
                                    act.wait_ge(piece_used, at(NPC, SPOS[(0, j, 1)] + 1 + NSPLIT))
                                    act.wait_ge(ea_ready, at(EB, j + 1))
                                    A(SILU[:, :], psum[2 * (j % 2)][:, :], ACT.Silu).then_inc(esilu_ready, 1)
                        round_turned(EB - 1)
                        for half in range(2):
                            round_gathered(half, at(2, 3 + half))
                        for half in range(2):
                            if half == 0:
                                act.wait_ge(down_done, at(EB, EB))
                            else:
                                act.wait_ge(piece_used, at(NPC, NPC + NSPLIT))
                            A(YS[:, half * 512:(half + 1) * 512], psum[4 + half][:, :], ACT.Copy).then_inc(y_copied, 1)

                    with act.Fori(0, NPASS) as p:
                        with act.If(p < passes):
                            with act.Fori(0, NE) as e:
                                expert(p, e)
            act.wait_ge(ev["x_final"], 1)
            store(act, y_out, X[:, :, :])

        @block.vector
        def _(dve):
            d = Chain(dve, dve_chain)
            V = nc.vector
            tt_, ts, stt = V.tensor_tensor, V.tensor_scalar, V.scalar_tensor_tensor

            def job(l, name):
                dve.wait_ge(job_done, job_no(l, name) + 1)
                return bank(l, name)

            def read(l, name, ins):
                ins.then_inc(job_read['v'], 1)
                dve.wait_ge(job_read['v'], read_no(l, name)[1])

            def wait_act_read(l, name):
                dve.wait_ge(job_read['a'], read_no(l, name)[1])

            def wait_z(l, g, i=None):
                dve.wait_ge(z_ready, l * NZ + ZPOS[ZT[g] + (max(ZW[g] // P - 1, 0) if i is None else i)] + 1)

            def signal(ins, name, count):
                ins.then_inc(ev[name], 1)
                dve.wait_ge(ev[name], count)

            def bmid(ap, n):
                return ap[:, None, :].to_broadcast([ap.shape[0], n, ap.shape[1]])

            def bend(ap, n):
                shape = list(ap.shape) + [n]
                return (ap[:, :, None] if len(ap.shape) == 2 else ap[:, :, :, None]).to_broadcast(shape)

            def norm(l, job_name, gain, scale, shift, signal_squares, signal_h, sq):
                signal(tt_(sq, X[:, :, :], X[:, :, :], ALU.mult), signal_squares, l + 1)
                d.add(ts(MA[:, :, :], MOD[:, l, scale * KC:(scale + 1) * KC, :], 1.0, None, ALU.add))
                d.wait()
                d(tt_(MA[:, :, :], MA[:, :, :], bend(v_(l, gain, 0, KC), NS + 1), ALU.mult))
                wait_act_read(l, job_name)
                d(V.reciprocal(R[:, :], R[:, :]))
                d(tt_(H[:, :, :], X[:, :, :], bmid(R[:, :], KC), ALU.mult))
                d.add(tt_(H[:, :, NP:T], H[:, :, NP:T], MA[:, :, 1:], ALU.mult))
                sh = MOD[:, l, shift * KC:(shift + 1) * KC, :]
                for c in range(KC):
                    d.add(ts(H[:, c, 0:NP], H[:, c, 0:NP], MA[:, c, 0:1], sh[:, c, 0:1], ALU.mult, ALU.add))
                d.wait()
                signal(tt_(H[:, :, NP:T], H[:, :, NP:T], sh[:, :, 1:], ALU.add), signal_h, l + 1)

            def add_residual(l, dst, src, m, gate):
                g = MOD[:, l, gate * KC + m, :]
                d.add(tt_(small(208, NS), src[:, NP:T], g[:, 1:], ALU.mult))
                d.add(stt(dst[:, 0:NP], src[:, 0:NP], g[:, 0:1], dst[:, 0:NP], ALU.mult, ALU.add))
                d.wait()
                return tt_(dst[:, NP:T], dst[:, NP:T], small(208, NS), ALU.add)

            def value_rows(v_off, signal_name, count):
                for h in range(NH):
                    v = KV8[:, v_off + h * HD:v_off + (h + 1) * HD]
                    ins = tt_(VE[:, h], bmid(v, NS), bend(ident[0:NS, 0:NS], HD), ALU.mult)
                    if h < NH - 1:
                        d.add(ins)
                d.wait()
                signal(ins, signal_name, count)

            def head_norm(l, squares, jobs, gain, gate, first, last, cat):
                signal(tt_(BCT, O[:, :, :], O[:, :, :], ALU.mult), squares, l + 1)
                wait_act_read(l, jobs[1])
                d(V.reciprocal(RNG, RNG))
                d(tt_(O[:, :, :], O[:, :, :], RNG, ALU.mult))
                for c in range(2):
                    ins = stt(CAT[:, cat + c, :], O[:, c, :], v_(l, gain, c), Z[:, ZT[gate] + c, :],
                              ALU.mult, ALU.mult)
                    if c == 0:
                        d(ins)
                return ins

            V.memset(EPSB, EPS).then_inc(dve_chain, 1)
            d.n += 1
            dve.wait_ge(consts_in, 16 * 6)
            dve.wait_ge(page_idx, 16)
            for l in range(L):
                ts(IDX[:, l, :], IDXI[:, :], float(L * SUB), c_('sub', P, l, l + 1), ALU.mult,
                   ALU.add).then_inc(idx_ready, 1)
            for l in range(L):
                dve.wait_ge(row_used, RPOS[('ada', l, ADA1 - 1)] + 1)
                norm(l, 'rms1', 'norm1', 1, 0, "squares1", "h1", H[:, :, :])
                wait_z(l, 'fk')
                fqk = Z[:, ZT['fq']:ZT['fq'] + 4, :]
                signal(tt_(SQ, fqk, fqk, ALU.mult), "fox_squares", l + 1)
                wait_z(l, 'ff')
                d(ts(FX[:, :], FX[:, :], VT[0:NH, l, VCOL['fb']:VCOL['fb'] + 1], None, ALU.add))
                d(ts(FS[:, :], FX[:, :], 0.0, None, ALU.min))
                signal(stt(LF[:, :], FS[:, :], -2.0, FX[:, :], ALU.mult, ALU.add), "ff_exp", l + 1)
                wait_act_read(l, 'fn3')
                d(V.reciprocal(RN, RN))
                for i in range(4):
                    d.add(stt(fqk[:, i, :], fqk[:, i, :], v_(l, 'qn' if i < 2 else 'kn'), RN[:, i, :],
                              ALU.mult, ALU.mult))
                d.wait()
                signal(ts(fqk[:, 0:2, :], fqk[:, 0:2, :], HD ** -0.5, None, ALU.mult), "fox_qk", l + 1)
                dve.wait_ge(ev_ffln, l + 1)
                d(tt_(LF[:, :], FS[:, :], LF[:, :], ALU.subtract))
                for i in range(2):
                    a, b = i * P, (i + 1) * P
                    d(V.tensor_tensor_scan(FS[:, a:b], c_('ones', NH), LF[:, a:b],
                                           0.0 if i == 0 else FS[:, a - 1:a], ALU.mult, ALU.add))
                signal(ts(FX[:, 0:NP], FS[:, 0:NP], -1.0, None, ALU.mult), "fox_logf", l + 1)
                wait_act_read(l, 'qb3')
                for b in range(NS):
                    wait_unit(dve, ('k', l, b))
                    k3 = unit(('k', l, b)).rearrange("p (t f) -> p t f", t=TPP)
                    d(tt_(k3, k3, bmid(QB[:, b, :], TPP), ALU.mult))
                    V.tensor_reduce(SC[:, b].rearrange("p h t -> p t h"),
                                    k3.rearrange("p t (h d) -> p t h d", h=NH), AX.X, ALU.add).then_inc(k_used, 1)
                dve.wait_ge(k_used, NS * (l + 1))
                dve.wait_ge(logf_in, 16 * NS * (l + 1))
                LT = LP.rearrange("p b t h -> p b h t")
                d(V.memset(SUF[:, :, :, TPP - 1], 0.0))
                for t in range(TPP - 2, -1, -1):
                    d(tt_(SUF[:, :, :, t], SUF[:, :, :, t + 1], LT[:, :, :, t + 1], ALU.add))
                tot = small(96, 32).rearrange("p (b h) -> p b h", b=NS)
                d(tt_(tot, SUF[:, :, :, 0], LT[:, :, :, 0], ALU.add))
                lf = small(128, 32, NH).rearrange("p (b h) -> p b h", b=NS)
                signal(tt_(lf, bend(LF[:, NP:T], NH), bmid(ident[0:NH, 0:NH], NS), ALU.mult), "past_totals", l + 1)
                qk = small(224, 16).rearrange("p (c b) -> p c b", c=2)
                d(tt_(qk, fqk[:, 0:2, NP:T], fqk[:, 2:4, NP:T], ALU.mult))
                rt = small(64, 32).rearrange("p (b c s) -> p b c s", b=NS, c=2)
                d(tt_(rt[:, :, 0, :], bend(qk[:, 0, :], 2), bmid(c_('half'), NS), ALU.mult))
                signal(tt_(rt[:, :, 1, :], bend(qk[:, 1, :], 2), bmid(c_('half'), NS), ALU.mult), "row_terms", l + 1)
                for h in range(NH):
                    read(l, f's{h}', tt_(PS[:, h, :], job(l, f's{h}')[:, 0:3 * P], c_('causal'), ALU.add))
                    d.add(V.tensor_reduce(small(2 * h), PS[:, h, 0:P], AX.X, ALU.max, negate=True))
                    V.tensor_reduce(small(2 * h + 1), PS[:, h, P:3 * P], AX.X, ALU.max,
                                    negate=True).then_inc(ev["probs_max"], 1)
                for h in range(NH):
                    dve.wait_ge(ev["probs_exp"], 2 * (NH * l + h + 1))
                    d(V.reciprocal(small(8 + 2 * h, 2), small(8 + 2 * h, 2)))
                    d.add(ts(PS[:, h, 0:P], PS[:, h, 0:P], small(8 + 2 * h), None, ALU.mult))
                    ts(PS[:, h, P:3 * P], PS[:, h, P:3 * P], small(9 + 2 * h), None,
                       ALU.mult).then_inc(ev["probs"], 1)
                sn = small(32, 32)
                d(tt_(PR4, SC, SUF, ALU.add))
                read(l, 'snew', V.tensor_copy(sn, job(l, 'snew')[:, 0:32]))
                sf = job(l, 'suf')[:, 0:32].rearrange("p (b h) -> p b h", b=NS)
                read(l, 'suf', tt_(PR4, PR4, bend(sf, TPP), ALU.add))
                mx = small(160, 32)
                pr3 = PR[:, :].rearrange("p (r t) -> p r t", t=TPP)
                d(V.tensor_reduce(mx, pr3, AX.X, ALU.max))
                signal(tt_(mx, mx, sn, ALU.max), "max_part", l + 1)
                read(l, 'mxt', V.tensor_reduce(small(240, 1, 32), job(l, 'mxt')[0:32, 0:P], AX.X, ALU.max))
                signal(ts(small(192, 32, 32), ident[0:32, 0:32], small(240, 1, 32), None, ALU.mult), "max_diag", l + 1)
                mb = job(l, 'mxb')[:, 0:32]
                d(tt_(sn, sn, mb, ALU.subtract))
                read(l, 'mxb', tt_(pr3, pr3, bend(mb, TPP), ALU.subtract))
                signal(V.memset(small(241), 0.0), "dec_shift", l + 1)
                dve.wait_ge(ev["dec_exp"], l + 1)
                signal(V.tensor_reduce(small(64, 32), pr3, AX.X, ALU.add), "dec_sum", l + 1)
                read(l, 'sumb', tt_(small(160, 32), job(l, 'sumb')[:, 0:32], sn, ALU.add))
                d(V.reciprocal(small(160, 32), small(160, 32)))
                d(tt_(sn, sn, small(160, 32), ALU.mult))
                signal(tt_(pr3, pr3, bend(small(160, 32), TPP), ALU.mult), "dec_probs", l + 1)
                ca = Z[:, ZT['ca']:ZT['ca'] + 2, :]
                dve.wait_ge(job_done, job_no(l, 'o3') + 1)
                cw = v_(l, 'conv_w', 0, 2 * KW).rearrange("p (c k) -> p c k", c=2)
                UBW = TA[0][:, 0:2 * NS * KW].rearrange("p (c b k) -> p c b k", c=2, b=NS)
                dve.wait_ge(ev["conv_taps"], l + 1)
                for c in range(2):
                    d.add(tt_(UBW[:, c], UB[:, c], bmid(cw[:, c, :], NS), ALU.mult))
                d.wait()
                for c in range(2):
                    d.add(V.tensor_reduce(ca[:, c, NP:T], UBW[:, c], AX.X, ALU.add))
                d.wait()
                signal(tt_(ca, ca, bend(v_(l, 'conv_b', 0, 2), T), ALU.add), "conv_y", l + 1)
                b = job(l, 'mean')[:, 0:T]
                read(l, 'mean', ts(R[:, :], b, -1.0 / GW, None, ALU.mult))
                d(tt_(ca, ca, bmid(R[:, :], 2), ALU.add))
                signal(tt_(TA2, ca, ca, ALU.mult), "conv_sq", l + 1)
                wait_act_read(l, 'var')
                d(V.reciprocal(R[:, :], R[:, :]))
                d(tt_(ca, ca, bmid(R[:, :], 2), ALU.mult))
                for c in range(2):
                    d.add(ts(CAT[:, c, :], ca[:, c, :], v_(l, 'ln_g', c), v_(l, 'ln_b', c), ALU.mult, ALU.add))
                d.wait()
                signal(V.memset(small(241), 0.0), "conv_out", l + 1)
                for c in range(2):
                    read(l, f'gate{c}', ts(GX[:, c, :], job(l, f'gate{c}')[:, 0:T], v_(l, 'b_gate', c), None, ALU.add))
                d(ts(GM, GX, 0.0, None, ALU.min))
                signal(stt(GA, GM, -2.0, GX, ALU.mult, ALU.add), "gla_abs", l + 1)
                dve.wait_ge(ev["gla_ln"], l + 1)
                d(tt_(GX, GM, GA, ALU.subtract))
                d(ts(GX, GX, 1.0 / 16.0, None, ALU.mult))
                for c in range(2):
                    d.add(V.tensor_tensor_scan(BC[:, c, :], c_('reset'), GX[:, c, 0:NP], 0.0, ALU.mult, ALU.add))
                d.wait()
                bc4 = BC[:, :, :].rearrange("p c (n i) -> p c n i", i=CH)
                kd4 = GKD.rearrange("p c (n i) -> p c n i", i=CH)
                last = bc4[:, :, :, CH - 1]
                d.add(V.tensor_copy(DEC, last))
                dve.wait_ge(k_stored, 16 * (l + 1))
                for c in range(2):
                    ins = tt_(kd4[:, c], bend(last[:, c, :], CH), bc4[:, c], ALU.subtract)
                    if c == 0:
                        d.add(ins)
                d.wait()
                signal(ins, "gla_b", l + 1)
                gq = Z[:, ZT['gq']:ZT['gq'] + 2, :]
                gk = Z[:, ZT['gk']:ZT['gk'] + 2, :]
                gv = Z[:, ZT['gv']:ZT['gv'] + 2, :]
                wait_z(l, 'gv')
                d(ts(gq, gq, HD ** -0.5, None, ALU.mult))
                dve.wait_ge(ev["gla_decays"], l + 1)
                d.add(tt_(GQD, GQD, gq[:, :, 0:NP], ALU.mult))
                signal(tt_(GKD, GKD, gk[:, :, 0:NP], ALU.mult), "gla_kq", l + 1)
                q4, k4, v4 = (t[:, :, 0:NP].rearrange("p c (n i) -> p c n i", i=CH) for t in (gq, gk, gv))
                o4 = O[:, :, 0:NP].rearrange("p c (n i) -> p c n i", i=CH)

                def lag_view(t, lag):
                    return t[:, 0:2 * NCH * (CH - lag)].rearrange("p (c n i) -> p c n i", c=2, n=NCH)

                def difference(lag):
                    if lag >= 1:
                        tt_(lag_view(EX[lag % 2], lag), bc4[:, :, :, lag:], bc4[:, :, :, 0:CH - lag],
                            ALU.subtract).then_inc(ev["lag_diff"], 1)

                def weights(lag):
                    w = lag_view(WX[lag % 2], lag)
                    if lag >= 2:
                        dve.wait_ge(job_done, job_no(l, f'att{lag - 2}') + 1)
                    ins = tt_(w, q4[:, :, :, lag:], k4[:, :, :, 0:CH - lag], ALU.mult)
                    if lag >= 1:
                        d(ins)
                        dve.wait_ge(ev["lag_exp"], l * (CH - 1) + lag)
                        ins = tt_(w, w, lag_view(EX[lag % 2], lag), ALU.mult)
                    signal(ins, "lag_w", l * CH + lag + 1)

                def gather_lag(lag):
                    b = lag_view(job(l, f'att{lag}'), lag)
                    if lag == 0:
                        read(l, 'att0', tt_(o4, b, v4, ALU.mult))
                        return
                    t = lag_view(TA[lag % 2], lag)
                    read(l, f'att{lag}', tt_(t, b, v4[:, :, :, 0:CH - lag], ALU.mult))
                    d(tt_(o4[:, :, :, lag:], o4[:, :, :, lag:], t, ALU.add))

                for lag in range(CH + 1):
                    if lag < CH:
                        difference(lag)
                        weights(lag)
                    if lag >= 1:
                        gather_lag(lag - 1)
                for tt in range(2):
                    wait_act_read(l, 'gkv1')
                    if tt:
                        dve.wait_ge(job_done, job_no(l, 'kv01') + 1)
                    for h in range(NH):
                        ins = tt_(VX[:, h], bmid(TMV[:, tt, h * HD:(h + 1) * HD], 8), bend(c_('chunk'), HD), ALU.mult)
                        if h < NH - 1:
                            d.add(ins)
                    d.wait()
                    signal(ins, "gla_vx", 2 * l + tt + 1)
                    for pr in range(2):
                        b = job(l, f'kv{tt}{pr}')[:, :].rearrange("p (n v) -> p n v", n=8)
                        for n in range(8):
                            g = 8 * tt + n
                            if g == 0:
                                ins = V.tensor_copy(SH[:, pr, 0, :], b[:, 0, :])
                            else:
                                ins = stt(SH[:, pr, g, :], SH[:, pr, g - 1, :], DEC[:, pr, g:g + 1], b[:, n, :],
                                          ALU.mult, ALU.add)
                            if n < 7:
                                d(ins)
                        read(l, f'kv{tt}{pr}', ins)
                signal(V.memset(small(241), 0.0), "gla_states", l + 1)
                for s in range(2):
                    r = slice(s * HD, (s + 1) * HD)
                    b = job(l, f'gi{s}')[r, :].rearrange("p (c t) -> p c t", c=2)
                    read(l, f'gi{s}', tt_(O[r, :, CH:NP], O[r, :, CH:NP], b[:, :, CH:NP], ALU.add))
                wait_act_read(l, 'gts')
                dve.wait_ge(job_done, job_no(l, 'kv11') + 1)
                value_rows(GW, "ve_gla", l + 1)
                for c in range(2):
                    d.add(tt_(SG4[:, c], SG4[:, c], bend(GX[:, c, NP:T], HD), ALU.mult))
                d.wait()
                for c in range(2):
                    read(l, f'gx{c}', tt_(SG[:, c, :], SG[:, c, :], job(l, f'gx{c}')[:, :], ALU.add))
                signal(V.memset(small(241), 0.0), "s_gla", l + 1)
                for s in range(2):
                    r = slice(s * HD, (s + 1) * HD)
                    b = job(l, f'gs{s}')[r, 0:2 * NS].rearrange("p (c b) -> p c b", c=2)
                    read(l, f'gs{s}', V.tensor_copy(O[r, :, NP:T], b))
                dve.wait_ge(ev["gate_silu"], 3 * (l + 1))
                signal(head_norm(l, "gla_sq", ('gn0', 'gn1'), 'gla_g', 'go', None, None, 4), "gla_cat", l + 1)
                for i in range(4):
                    z, t = Z[:, ZT['rq'] + i, :], TA[i % 2][:, 0:T]
                    sc = 1.0 if i < 2 else HD ** -0.5
                    read(l, f'rr{i}', stt(t, job(l, f'rr{i}')[:, 0:T], sc, c_('sin'), ALU.mult, ALU.mult))
                    d(stt(z, z, sc, c_('cos'), ALU.mult, ALU.mult))
                    d(tt_(z, z, t, ALU.add))
                signal(V.memset(small(241), 0.0), "rope", l + 1)
                dec = c_('decay').rearrange("p (h t) -> p h t", h=NH)
                for h in range(NH):
                    b = job(l, f'rs{h}')
                    d(tt_(RP(h)[:, 0:NP], b[:, 0:NP], dec[:, h, :], ALU.mult))
                    read(l, f'rs{h}', tt_(RP(h)[:, NP:3 * P], b[:, NP:3 * P], dec[:, h, 0:P], ALU.mult))
                    V.memset(small(241), 0.0).then_inc(ev["ret_p"], 1)
                    dve.wait_ge(ev["ret_p"], NH * l + h + 1)
                wait_act_read(l, 'rkv1')
                dk = c_('dk').rearrange("p (t h) -> p t h", h=NH)
                for tt in range(2):
                    ins = tt_(TMK[:, tt, :].rearrange("p (h d) -> p h d", h=NH),
                              TMK[:, tt, :].rearrange("p (h d) -> p h d", h=NH), bend(dk[:, tt, :], HD), ALU.mult)
                    if tt == 0:
                        d(ins)
                signal(ins, "ret_kd", l + 1)
                dve.wait_ge(job_done, job_no(l, 'ro3') + 1)
                value_rows(GW, "ve_ret", l + 1)
                for c in range(2):
                    d(ts(SR[:, c, :], SR[:, c, :], c_('gamma', P, c, c + 1), None, ALU.mult))
                for c in range(2):
                    read(l, f'rx{c}', tt_(SR[:, c, :], SR[:, c, :], job(l, f'rx{c}')[:, :], ALU.add))
                signal(V.memset(small(241), 0.0), "s_ret", l + 1)
                for s in range(2):
                    r = slice(s * HD, (s + 1) * HD)
                    b = job(l, f'rd{s}')[r, 0:2 * NS].rearrange("p (c b) -> p c b", c=2)
                    read(l, f'rd{s}', V.tensor_copy(O[r, :, NP:T], b))
                wait_act_read(l, 'ro3')
                fv = Z[:, ZT['fv']:ZT['fv'] + 2, :]
                dve.wait_ge(row_used, RPOS[('pv', l, NS // 2 - 1)] + 1)
                pv4 = small(96, 32).rearrange("p (b c s) -> p c s b", b=NS, c=2)
                sn4 = sn.rearrange("p (b c s) -> p c s b", b=NS, c=2)
                for s in range(2):
                    r = slice(s * HD, (s + 1) * HD)
                    d(tt_(CAT[r, 2:4, NP:T], sn4[r, :, s, :], fv[r, :, NP:T], ALU.mult))
                    d(tt_(CAT[r, 2:4, NP:T], CAT[r, 2:4, NP:T], pv4[r, :, s, :], ALU.add))
                signal(head_norm(l, "ret_sq", ('rn0', 'rn1'), 'ret_g', 'rg', None, None, 6), "cat", l + 1)
                dve.wait_ge(row_used, RPOS[('ada', l, NADA - 1)] + 1)
                for m in range(KC):
                    dve.wait_ge(out_done, l * KC + m + 1)
                    add_residual(l, X[:, m, :], psum[m % 2], m, 2).then_inc(out_added, 1)
                    dve.wait_ge(out_added, l * KC + m + 1)
                dve.wait_ge(stored, 16 * STORES_PER_LAYER * (l + 1))
                if l % 2 == 0:
                    norm(l, 'rms2', 'norm2', 4, 3, "squares2", "h2", Z[:, 0:KC, :])
                    n = 0
                    for j in range(len(FB) + 1):
                        if j < len(FB):
                            for t in range(FB[j][1] // P):
                                if j >= 3:
                                    dve.wait_ge(y_done, KC * (j - 2))
                                dve.wait_ge(silu_ready, n + 1)
                                tt_(AB[:, j % 3, t, :], SA[n % 4], psum[2 * (n % 2) + 1][:, 0:T],
                                    ALU.mult).then_inc(a_ready, 1)
                                n += 1
                        if j >= 1:
                            for m in range(KC):
                                q = KC * (j - 1) + m
                                dve.wait_ge(y_done, q + 1)
                                b = psum[4 + m % 4][:, 0:T]
                                if j == 1:
                                    V.tensor_copy(YF[:, m, :], b).then_inc(y_added, 1)
                                else:
                                    tt_(YF[:, m, :], YF[:, m, :], b, ALU.add).then_inc(y_added, 1)
                                dve.wait_ge(y_added, q + 1)
                    for m in range(KC):
                        d(add_residual(l, X[:, m, :], YF[:, m, :], m, 5))
                else:
                    norm(l, 'rms2', 'norm2', 4, 3, "squares2", "h2", Z[:, 0:KC, :])
                    dve.wait_ge(router_done, 1)
                    for tt in range(3):
                        n = P if tt < 2 else NS
                        lg = small(56, NE, n)
                        d(V.tensor_copy(lg, psum[0][0:n, tt * NE:(tt + 1) * NE]))
                        d(V.max(small(16 * tt + 64, 8, n), lg))
                        d(V.max_index(MI[0:n, tt, :], small(16 * tt + 64, 8, n), lg))
                        d(V.tensor_copy(small(16 * tt + 72, 2, n), MI[0:n, tt, 0:2]))
                        d(tt_(small(40 + tt, 1, n), small(16 * tt + 65, 1, n), small(16 * tt + 64, 1, n), ALU.subtract))
                    signal_n = V.memset(small(241), 0.0)
                    signal_n.then_inc(gates_read, 1)
                    dve.wait_ge(gates_read, 2)
                    d(ts(small(44, 3), small(40, 3), 1.0, None, ALU.add))
                    d(V.reciprocal(small(44, 3), small(44, 3)))
                    d(tt_(small(48, 3), small(44, 3), small(40, 3), ALU.mult))
                    SLOTS, GATES = SLG[:, 0], SLG[:, 1]
                    d(V.memset(SLG[:, :, :, :], 0.0))
                    for tt in range(3):
                        n = P if tt < 2 else NS
                        i1, i2 = small(16 * tt + 72, 1, n), small(16 * tt + 73, 1, n)
                        m1, m2 = small(56, NE, n), small(8, NE, n)
                        d.add(ts(m1, c_('eio', n), i1, None, ALU.is_equal))
                        d(ts(m2, c_('eio', n), i2, None, ALU.is_equal))
                        tt_(MASK(tt, n), m1, m2, ALU.add).then_inc(masks_ready, 1)
                        d(ts(m1, m1, small(44 + tt, 1, n), None, ALU.mult))
                        d(stt(GATES[0:n, tt, 0:NE], m2, small(48 + tt, 1, n), m1, ALU.mult, ALU.add))
                    dve.wait_ge(masks_ready, 3)
                    dve.wait_ge(router_done, 2)
                    for tt in range(3):
                        n = P if tt < 2 else NS
                        d(stt(SLOTS[0:n, tt, 0:NE], psum[1][0:n, tt * NE:(tt + 1) * NE], 1.0, MASK(tt, n),
                              ALU.add, ALU.mult))
                    d(ts(SLOTS[:, :, 0:NE], SLOTS[:, :, 0:NE], -1.0, None, ALU.add))
                    d.add(ts(SLOTS[:, :, NE:], SLOTS[:, :, 0:1], -float(CAP), None, ALU.add))
                    d.add(V.tensor_copy(GATES[:, :, NE:], GATES[:, :, 0:1]))
                    d.add(V.memset(Y[:, :, :], 0.0))
                    d(V.tensor_reduce(small(16), psum[1][:, 3 * NE:4 * NE], AX.X, ALU.max))
                    d(ts(small(17), small(16), CAP + 0.5, None, ALU.is_gt))
                    d(stt(small(18), small(16), 2 * CAP + 0.5, small(17), ALU.is_gt, ALU.add))
                    signal_passes = ts(PASSES[:, :], small(18), 1.0, 1.0, ALU.mult, ALU.add)
                    signal_passes.then_inc(passes_ready, 1)

                    def select(column):
                        s, g = SLG[:, 0, :, column], SLG[:, 1, :, column]
                        d(tt_(SEL[:, :, :], bmid(c_('slot'), 3), s.to_broadcast([P, 3, P]), ALU.is_equal))
                        return tt_(GSEL[:, :, :], SEL[:, :, :], g.to_broadcast([P, 3, P]), ALU.mult)

                    select(slice(0, 1)).then_inc(slots_ready, 1)
                    V.memset(small(241), 0.0).then_inc(ea_ready, 1)
                    V.memset(small(242), 0.0).then_inc(scattered, KC)
                    V.memset(small(243), 0.0).then_inc(piece_used, NSPLIT)
                    dve.wait_ge(passes_ready, 1)
                    passes = dve.value_load(PASSES[0:1, 0:1], min_val=1, max_val=NPASS)

                    def rest(out, full, high):
                        return tt_(out, full, high.bitcast(F32), ALU.subtract)

                    def low_gathered(half, count):
                        dve.wait_ge(gathered_high, count)
                        c = slice(4 * half, 4 * half + 4)
                        rest(HGL[:, c, :].rearrange("p c s -> p (c s)"), psum[6 + half][:, :],
                             HGH[:, c, :].rearrange("p c s -> p (c s)")).then_inc(gathered, 1)

                    for half in range(2):
                        low_gathered(half, half + 1)

                    def expert(p, e):
                        def at(per, n):
                            return p * (NE * per) + e * per + n

                        def low_turned(j):
                            dve.wait_ge(turned_high, at(EB, j + 1))
                            rest(ATL[:, :, :].rearrange("p k s -> p (k s)"), psum[6 + (j > 0) * (j + 1) % 2][:, :],
                                 ATH[:, :, :].rearrange("p k s -> p (k s)")).then_inc(turned, 1)

                        for q in range(NPC):
                            dve.wait_ge(high_ready, at(NPC, q + 1))
                            rest(WL[:, q % NSPLIT, :], raw[q % NRAW], WH[:, q % NSPLIT, :]).then_inc(low_ready, 1)
                            for j in range(EB):
                                if q == SPOS[(0, j, 0)] + 3 and j >= 1:
                                    low_turned(j - 1)
                                if q == SPOS[(0, j, 0)] + 5:
                                    dve.wait_ge(piece_used, at(NPC, SPOS[(1, j, 1)] + 1 + NSPLIT))
                                    dve.wait_ge(esilu_ready, at(EB, j + 1))
                                    tt_(AM[:, :], SILU[:, :], psum[2 * (j % 2) + 1][:, :], ALU.mult).then_inc(ea_ready, 1)
                                if q == SPOS[(0, j, 0)] + 5 and j == 3:
                                    s, g = SLG[:, 0, :, bass.ds(e + 1, 1)], SLG[:, 1, :, bass.ds(e + 1, 1)]
                                    tt_(SEL[:, :, :], bmid(c_('slot'), 3), s.to_broadcast([P, 3, P]),
                                        ALU.is_equal).then_inc(sel_ready, 1)
                                    dve.wait_ge(sel_ready, at(1, 1))
                                    tt_(GSEL[:, :, :], SEL[:, :, :], g.to_broadcast([P, 3, P]),
                                        ALU.mult).then_inc(slots_ready, 1)
                        low_turned(EB - 1)
                        for half in range(2):
                            low_gathered(half, at(2, 3 + half))
                        for m in range(KC):
                            dve.wait_ge(scatter_done, at(KC, m + 1))
                            dve.wait_ge(scattered, at(KC, m + 1))
                            tt_(Y[:, m, :], Y[:, m, :], psum[6 + m % 2][:, 0:T], ALU.add).then_inc(scattered, 1)

                    with dve.Fori(0, NPASS) as p:
                        with dve.If(p < passes):
                            with dve.Fori(0, NE) as e:
                                expert(p, e)
                            ts(SLOTS, SLOTS, -float(CAP), None, ALU.add).then_inc(slots_moved, 1)
                            dve.wait_ge(slots_moved, p + 1)
                            V.memset(small(241), 0.0)
                    dve.wait_ge(scattered, passes * (NE * KC) + KC)
                    for m in range(KC):
                        ins = add_residual(l, X[:, m, :], Y[:, m, :], m, 5)
                        if m < KC - 1:
                            d(ins)
                    ins.then_inc(ev["x_final"], 1)


def kernel(**inputs):
    import numpy as np
    import concourse.bacc as bacc
    from concourse.bass_utils import run_bass_kernel_spmd

    a = {k: np.asarray(v) for k, v in inputs.items()}

    def features(x):
        return np.ascontiguousarray(x.T.reshape(-1, P, x.shape[0]).transpose(1, 0, 2))

    def columns(v):
        return v.reshape(-1, P).T

    x = np.concatenate([a['x_prompt'][0], a['x_sample'][:, 0]])
    c = np.concatenate([a['c_prompt'], a['c_sample']])
    vt = []
    for l in range(L):
        parts = [columns(a['norm1_g'][l]), columns(a['norm2_g'][l]), columns(a['b_ada'][l]), columns(a['conv_b'][l]),
                 columns(a['conv_ln_g'][l]), columns(a['conv_ln_b'][l]), columns(a['gla_b_gate'][l]),
                 columns(a['gla_norm_g'][l]), columns(a['ret_norm_g'][l]), np.tile(a['fox_qn_g'][l], 2)[:, None],
                 np.tile(a['fox_kn_g'][l], 2)[:, None], np.tile(a['fox_fb'][l], P // NH)[:, None],
                 a['conv_w'][l].T.reshape(2, P, KW).transpose(1, 0, 2).reshape(P, 2 * KW)]
        vt.append(np.concatenate(parts, 1))

    def states(s):
        return np.ascontiguousarray(
            s.reshape(L, NS, 2, 2, HD, HD).transpose(0, 3, 4, 2, 1, 5).reshape(L, P, 2, NS * HD))

    arrays = {
        'xT': features(x), 'cT': features(c), 'vt': np.ascontiguousarray(np.stack(vt, 1)),
        'consts': host_constants(),
        'conv_in': np.ascontiguousarray(
            a['state_conv'].reshape(L, NS, KW - 1, 2, P).transpose(0, 4, 3, 1, 2)),
        'gla_in': states(a['state_gla']), 'ret_in': states(a['state_ret']),
        'ptr': np.ascontiguousarray(np.repeat(a['page_table'].T, SUB, axis=0)),
        'cache_k': a['cache_k'], 'cache_v': a['cache_v'], 'cache_logf': a['cache_logf'],
        'w_in': a['w_in'], 'w_out': a['w_out'], 'w_ada': a['w_ada'], 'gate2': a['gla_w_gate2'],
        'ffn_w1': a['ffn_w1'], 'ffn_w3': a['ffn_w3'], 'ffn_w2': a['ffn_w2'],
        'router': a['moe_router'][0], 'moe_w1': a['moe_w1'], 'moe_w3': a['moe_w3'], 'moe_w2': a['moe_w2'],
    }
    outs = {'y_out': (P, KC, T), 'conv_out': (L, P, 2, (NS + 1) * (KW - 1)), 'k_out': (L, P, 2, T),
            'v_out': (L, P, 2, T), 'logf_out': (L, NH, T), 'gla_out': (L, P, 2, (NS + 1) * HD),
            'ret_out': (L, P, 2, (NS + 1) * HD)}
    nc = bacc.Bacc("TRN2", target_bir_lowering=False, num_devices=1)
    args = [nc.dram_tensor(k, v.shape, mybir.dt.from_np(v.dtype), kind="ExternalInput").ap()
            for k, v in arrays.items()]
    args += [nc.dram_tensor(k, v, F32, kind="ExternalOutput").ap() for k, v in outs.items()]
    trunk_kernel(nc, *args)
    r = run_bass_kernel_spmd(nc, [arrays], core_ids=[0]).results[0]

    def tokens(y):
        y = np.moveaxis(y, -1, -3)
        return np.swapaxes(y, -1, -2).reshape(*y.shape[:-2], -1)

    y = tokens(r['y_out'])
    conv = np.asarray(r['conv_out']).reshape(L, P, 2, NS + 1, KW - 1).transpose(0, 3, 4, 2, 1)
    conv = conv.reshape(L, NS + 1, KW - 1, GW)
    k, v = (tokens(r[n]).reshape(L, T, NH, HD) for n in ('k_out', 'v_out'))
    logf = np.asarray(r['logf_out']).transpose(0, 2, 1)

    def split(s):
        s = np.asarray(s).reshape(L, 2, HD, 2, NS + 1, HD).transpose(0, 4, 3, 1, 2, 5)
        s = s.reshape(L, NS + 1, NH, HD, HD)
        return s[:, :1], s[:, 1:]

    def by_sample(t):
        return t[:, NP:].swapaxes(0, 1)[:, :, None]

    gla, ret = split(r['gla_out']), split(r['ret_out'])
    result = (y[None, :NP], y[NP:, None], conv[:, :1], conv[:, 1:], k[None, :, :NP], by_sample(k),
              v[None, :, :NP], by_sample(v), logf[None, :, :NP], by_sample(logf), gla[0], gla[1], ret[0], ret[1])
    return tuple(np.ascontiguousarray(t) for t in result)
```

```python
from contextlib import ExitStack

import concourse.bass as bass
import numpy as np
from concourse import mybir

F32 = mybir.dt.float32
F32R = mybir.dt.float32r
I32 = mybir.dt.int32
U32 = mybir.dt.uint32
ALU = mybir.AluOpType
ACT = mybir.ActivationFunctionType
AX = mybir.AxisListType

P = 128
DM = 1024
KC = DM // P
NP = 256
NS = 8
T = NP + NS
L = 2
NH, HD = 4, 64
GW = NH * HD
KW = 31
LR = 16
CH = 16
NCH = NP // CH
PAGE, NPAGE, NPHYS = 128, 16, 160
TPP = PAGE * NPAGE // P
SUB = PAGE // TPP
DFF = 2816
NE, DE = 8, 3584
CAP = P
NPASS = -(-T // CAP)
EPS = 1e-6
SLOT = 4096
NSLOT = 6
SHIFT = 4
NLOW = 4
COLS = 512

ZT = {'ca': 0, 'cg': 2, 'fq': 4, 'fk': 6, 'fv': 8, 'ff': 10, 'gq': 11, 'gk': 13, 'gv': 15,
      'glr': 17, 'go': 18, 'rq': 20, 'rk': 22, 'rv': 24, 'rg': 26}
NZ = 28
ZCOL = {'ca': 0, 'cg': 256, 'fq': 512, 'fk': 768, 'fv': 1024, 'ff': 1280, 'gq': 1284, 'gk': 1540,
        'gv': 1796, 'glr': 2052, 'go': 2068, 'rq': 2324, 'rk': 2580, 'rv': 2836, 'rg': 3092}
ZW = {k: GW for k in ZT} | {'ff': NH, 'glr': LR}
ZUNITS = [('fq', 'fk'), ('fv', 'ff'), ('ca', 'cg'), ('gq', 'gk'), ('gv', 'glr'), ('go', 'rq'),
          ('rk', 'rv'), ('rg',)]
ZORDER = []
for _u, _gs in enumerate(ZUNITS):
    for _g in _gs:
        for _c in range(0, ZW[_g], P):
            ZORDER.append((ZT[_g] + _c // P, _u, ZCOL[_g] - ZCOL[_gs[0]] + _c, min(P, ZW[_g] - _c)))
ZPOS = {t[0]: n for n, t in enumerate(ZORDER)}

VCOL, _n = {}, 0
for _k, _w in (('norm1', KC), ('norm2', KC), ('b_ada', 6 * KC), ('conv_b', 2), ('ln_g', 2), ('ln_b', 2),
               ('b_gate', 2), ('gla_g', 2), ('ret_g', 2), ('qn', 1), ('kn', 1), ('fb', 1),
               ('conv_w', 2 * KW)):
    VCOL[_k] = _n
    _n += _w
NV = _n

CCOL, _n = {}, 0
for _k, _w in (('ident', P), ('ones', P), ('heads', P), ('swap', P), ('later', P), ('sub', L), ('cos', T), ('sin', T),
               ('reset', NP), ('slot', P), ('decay', NH * NP), ('causal', 3 * P),
               ('chunk', 8), ('half', 2), ('dk', 2 * NH), ('gamma', 2), ('eio', NE)):
    CCOL[_k] = (_n, _w)
    _n += _w
NC = _n

EB = DE // COLS
PIECE = SLOT // 2
STREAM = [(k, 0, i) for k in range(2) for i in range(2)]
for _j in range(1, EB):
    STREAM += [(k, _j, i) for k in range(2) for i in range(2)] + [(2, _j - 1, i) for i in range(2)]
STREAM += [(2, EB - 1, i) for i in range(2)]
NPC = len(STREAM)
SPOS = {p: n for n, p in enumerate(STREAM)}
NRAW = 7
NSPLIT = 3
assert NPC % NRAW == 0 and NPC % NSPLIT == 0

FB = [(j * COLS, min(COLS, DFF - j * COLS)) for j in range(-(-DFF // COLS))]
NFB = len(FB)
PW = PIECE // KC
FSTREAM = []
for _j in range(NFB + 1):
    if _j < NFB:
        for _i in range(FB[_j][1] // PW):
            FSTREAM += [('w1', _j, _i), ('w3', _j, _i)]
    if _j >= 1:
        FSTREAM += [('w2', _j - 1, _i) for _i in range(FB[_j - 1][1] // PW)]
NFP = len(FSTREAM)
FPOS = {p: n for n, p in enumerate(FSTREAM)}
PAIRS = [p for p in FSTREAM if p[0] == 'w1']

JOBS = [('rms1', 'a')] + [(f'fn{i}', 'a') for i in range(4)]
JOBS += [('tkv0', 'a'), ('tkv1', 'a'), ('tqs', 'a')] + [(f'qb{i}', 'a') for i in range(4)]
JOBS += [(f's{h}', 'v') for h in range(NH)]
for _h in range(NH):
    JOBS += [(f'pt{_h}', 'a'), (f'o{_h}', 'a')]
JOBS += [('snew', 'v'), ('suf', 'v'), ('mxt', 'v'), ('mxb', 'v'), ('sumb', 'v')]
JOBS += [('mean', 'v'), ('var', 'a')]
JOBS += [('gate0', 'v'), ('gate1', 'v')] + [(f'att{i}', 'v') for i in range(CH)]
JOBS += [('gkv0', 'a'), ('gkv1', 'a'), ('gts', 'a')]
JOBS += [(f'kv{_tt}{_pr}', 'v') for _tt in range(2) for _pr in range(2)]
JOBS += [('gi0', 'v'), ('gi1', 'v'), ('gx0', 'v'), ('gx1', 'v'), ('gs0', 'v'), ('gs1', 'v'),
         ('gn0', 'a'), ('gn1', 'a')]
JOBS += [(f'rr{i}', 'v') for i in range(4)] + [('rkv0', 'a'), ('rkv1', 'a'), ('rts', 'a')]
for _h in range(NH):
    JOBS += [(f'rs{_h}', 'v'), (f'ro{_h}', 'a')]
JOBS += [('rst', 'a'), ('rx0', 'v'), ('rx1', 'v'), ('rd0', 'v'), ('rd1', 'v'), ('rn0', 'a'), ('rn1', 'a'),
         ('rms2', 'a')]
JPOS = {n: i for i, (n, _) in enumerate(JOBS)}
NJ = len(JOBS)
NBANK = 6


def job_no(l, name):
    return l * NJ + JPOS[name]


def divmod_job(n):
    return n // NJ, JOBS[n % NJ][0]


STORES_PER_LAYER = 10
NSTORES = L * STORES_PER_LAYER + 2


def read_no(l, name):
    who = JOBS[JPOS[name]][1]
    per = sum(w == who for _, w in JOBS)
    return who, l * per + sum(w == who for _, w in JOBS[:JPOS[name] + 1])


ADA1 = 4
NADA = 6 * DM // COLS
ROWS_FIRST = [('ada', 0, i) for i in range(ADA1)]
ROWS_OF = []
for _l in range(L):
    ROWS_OF.append([('ada', _l, i) for i in range(ADA1, NADA)])
    ROWS_OF[_l] += [('pv', _l, i) for i in range(NS // 2)]
    if _l + 1 < L:
        ROWS_OF[_l] += [('ada', _l + 1, i) for i in range(ADA1)]
FILL = {'s': (16, 16), 'pt': (1, 1), 'snew': (4, 0), 'suf': (8, 1), 'mxt': (0, 6), 'mxb': (0, 0),
        'sumb': (8, 0), 'mean': (8, 0), 'var': (0, 0), 'gate': (4, 0), 'lag': (7, 4), 'kq': (3, 7),
        'vx': (8, 16), 'states': (8, 8), 'gx': (5, 8), 'gs': (4, 0), 'gn': (8, 9), 'rr': (0, 16),
        'rope': (8, 12), 'rp': (2, 8), 'rst': (8, 8), 'rx': (8, 16), 'rd': (8, 0)}
ROWJOBS = ROWS_FIRST + sum(ROWS_OF, [])
RPOS = {j: n for n, j in enumerate(ROWJOBS)}


def row_units(j):
    return [j] if j[0] == 'ada' else [('v', j[1], 2 * j[2]), ('v', j[1], 2 * j[2] + 1)]



def ring_units():
    order = list(ROWS_FIRST)
    for l in range(L):
        order += [('in', l, 0), ('in', l, 1), ('in', l, 2)]
        for b in range(NS):
            order.append(('k', l, b))
            if b < 5:
                order.append(('in', l, 3 + b))
        for j in ROWS_OF[l]:
            order += row_units(j)
        order += [('out', l, 0), ('out', l, 1)]
    return order


UNITS = ring_units()
UPOS = {u: n for n, u in enumerate(UNITS)}
NEXT = UPOS[('in', 1, 0)]


def host_constants():
    c = np.zeros((P, NC), np.float32)

    def put(name, a):
        o, w = CCOL[name]
        c[:a.shape[0], o:o + w] = a.reshape(a.shape[0], -1)

    f = np.float32
    put('ident', np.eye(P, dtype=f))
    put('ones', np.ones((P, P), f))
    hd = np.arange(P) // HD
    put('heads', (hd[:, None] == hd[None, :]).astype(f))
    half = HD // 2
    swap = np.zeros((P, P), f)
    for m in range(P):
        if m % HD < half:
            swap[m + half, m] = -1.0
        else:
            swap[m - half, m] = 1.0
    put('swap', swap)
    put('later', (np.arange(P)[:, None] > np.arange(P)[None, :]).astype(f))
    inv = f(10000.0) ** (-np.arange(half, dtype=f) / f(half))
    pos = np.concatenate([np.arange(NP, dtype=f), np.full(NS, f(PAGE * NPAGE), f)])
    ang = (pos[None, :] * inv[:, None]).astype(f)
    put('cos', np.tile(np.cos(ang), (P // half, 1)))
    put('sin', np.tile(np.sin(ang), (P // half, 1)))
    put('reset', np.tile((np.arange(NP) % CH != 0).astype(f), (P, 1)))
    put('slot', np.tile(np.arange(P, dtype=f), (P, 1)))
    lg = np.log(1.0 - np.exp2(-5.0 - np.arange(NH)))
    rel = np.arange(NP)[None, :] - np.arange(P)[:, None]
    put('decay', np.stack([np.where(rel >= 0, np.exp(np.maximum(rel, 0) * g), 0.0) for g in lg], 1).astype(f))
    tri = np.where(np.arange(P)[None, :] <= np.arange(P)[:, None], f(0), f(-1e30))
    put('causal', np.concatenate([tri, np.zeros((P, P), f), tri], 1))
    put('chunk', (np.arange(P)[:, None] // CH == np.arange(8)[None, :]).astype(f))
    put('half', (hd[:, None] == np.arange(2)[None, :]).astype(f))
    tok = np.arange(P)[:, None] + P * np.arange(2)[None, :]
    put('dk', np.exp((NP - 1 - tok)[:, :, None] * lg[None, None, :]).astype(f))
    put('gamma', np.exp(lg).astype(f)[2 * np.arange(2)[None, :] + hd[:, None]])
    put('sub', (np.arange(P)[:, None] % SUB + SUB * np.arange(L)[None, :]).astype(f))
    put('eio', np.tile(np.arange(NE, dtype=f), (P, 1)))
    return c


def trunk_kernel(nc, xT, cT, vt, consts, conv_in, gla_in, ret_in, ptr, cache_k, cache_v, cache_logf,
                 w_in, w_out, w_ada, gate2, ffn_w1, ffn_w3, ffn_w2, router, moe_w1, moe_w3, moe_w2,
                 y_out, conv_out, k_out, v_out, logf_out, gla_out, ret_out):
    ctx = ExitStack()
    with ctx:
        def sb(name, shape, dt=F32):
            return ctx.enter_context(nc.sbuf_tensor(name, shape, dt))

        def sem(name):
            return ctx.enter_context(nc.semaphore(name))

        early = ExitStack()

        def sbe(name, shape, dt=F32):
            return early.enter_context(nc.sbuf_tensor(name, shape, dt))

        ring_low = sb("ring_low", [P, NLOW, SLOT])
        C = sb("C", [P, NC])
        VT = sb("VT", [P, L, NV])
        X = sb("X", [P, KC, T])
        H = sb("H", [P, KC, T])
        MOD = sb("MOD", [P, L, 6 * KC, NS + 1])
        CT = sb("CT", [P, KC, NS + 1])
        MA = sb("MA", [P, KC, NS + 1])
        R = sb("R", [P, T])
        G2 = sb("G2", [LR, L, GW])
        RW = sb("RW", [P, KC, NE])
        LF = sb("LF", [NH, T])
        SM = sb("SM", [P, 256])
        IDXI = sb("IDXI", [P, NS], I32)
        IDX = sb("IDX", [P, L, NS], I32)
        DEC = sb("DEC", [P, 2, NCH])[:, :, :]
        MI = sb("MI", [P, 3, 8], U32)
        PASSES = sb("PASSES", [P, 1], I32)
        ring_high = sbe("ring_high", [P, NSLOT + 1 - NLOW, SLOT])
        Z = sbe("Z", [P, NZ, T])
        ROWS = sbe("ROWS", [NS + 1, 2, COLS])
        PR = sbe("PR", [P, NH * P])
        UP = sbe("UP", [P, 2, KW - 1 + NP])
        UB = sbe("UB", [P, 2, NS, KW])
        TMK = sbe("TMK", [P, 2, GW])
        TMV = sbe("TMV", [P, 2, GW])
        PT = sbe("PT", [P, 3 * P])
        BC = sbe("BC", [P, 2, NP])
        O = sbe("O", [P, 2, T])
        SG = sbe("SG", [P, 2, NS * HD])
        SR = sbe("SR", [P, 2, NS * HD])

        def c_(name, rows=P, a=0, b=None):
            o, w = CCOL[name]
            return C[0:rows, o + a:o + (w if b is None else b)]

        def v_(l, name, i=0, n=1):
            return VT[:, l, VCOL[name] + i:VCOL[name] + i + n]

        ident, ones, heads = c_('ident'), c_('ones'), c_('heads')

        def slot(n):
            return ring_low[:, n, :] if n < NLOW else ring_high[:, n - NLOW, :]

        scr = slot(NSLOT)
        QB = scr[:, 0:2048].rearrange("p (b f) -> p b f", b=NS)
        RN = scr[:, 0:4 * T].rearrange("p (c t) -> p c t", c=4)
        SQ = scr[:, 2048:2048 + 4 * T].rearrange("p (c t) -> p c t", c=4)
        SC = scr[:, 2048:2560].rearrange("p (b h t) -> p b h t", b=NS, h=NH)
        SUF = scr[:, 2560:3072].rearrange("p (b h t) -> p b h t", b=NS, h=NH)
        LP = scr[:, 3072:3584].rearrange("p (b t h) -> p b t h", b=NS, t=TPP)
        PS = scr[:, 0:NH * 3 * P].rearrange("p (h c) -> p h c", h=NH)
        VX = scr[:, 0:2048].rearrange("p (h n v) -> p h n v", h=NH, n=8)
        SH = scr[:, 2048:4096].rearrange("p (c n v) -> p c n v", c=2, n=NCH)
        VE = scr[0:NS, 0:2048].rearrange("p (h b v) -> p h b v", h=NH, b=NS)
        EX = [scr[:, 2048 + 512 * i:2560 + 512 * i] for i in range(2)]
        WX = [scr[:, 3072 + 512 * i:3584 + 512 * i] for i in range(2)]
        TA = [scr[:, 512 * i:512 + 512 * i] for i in range(2)]
        TA2 = scr[:, 1024:1024 + 2 * T].rearrange("p (c t) -> p c t", c=2)
        GM = scr[:, 0:2 * T].rearrange("p (c t) -> p c t", c=2)
        GA = scr[:, 2 * T:4 * T].rearrange("p (c t) -> p c t", c=2)
        BCT, RNG = GM, GA
        GX = Z[:, ZT['cg']:ZT['cg'] + 2, :]
        GQD = Z[:, ZT['fq']:ZT['fq'] + 2, 0:NP]
        GKD = Z[:, ZT['fk']:ZT['fk'] + 2, 0:NP]
        PR4 = PR[:, :].rearrange("p (b h t) -> p b h t", b=NS, h=NH)
        CAT = H
        QS = PT[0:NS, 0:GW]
        KV8 = Z[0:NS, ZT['ca']:ZT['ca'] + 2, :].rearrange("p c t -> p (c t)")[:, 0:2 * GW]
        FX = Z[0:NH, ZT['ff'], :]
        FS = TMK[0:NH].rearrange("p a b -> p (a b)")[:, 0:T]
        SG4 = SG[:, :, :].rearrange("p c (b v) -> p c b v", b=NS)
        SR4 = SR[:, :, :].rearrange("p c (b v) -> p c b v", b=NS)
        early.close()
        WH = sb("WH", [P, NSPLIT, PIECE], F32R)
        WL = sb("WL", [P, NSPLIT, PIECE], F32R)
        dense = ExitStack()

        def sbd(name, shape, dt=F32):
            return dense.enter_context(nc.sbuf_tensor(name, shape, dt))

        HH = sbd("HH", [P, KC, T], F32R)
        HL = sbd("HL", [P, KC, T], F32R)
        FAH = sbd("FAH", [P, 2, 4, T], F32R)
        FAL = sbd("FAL", [P, 2, 4, T], F32R)
        YF = sbd("YF", [P, KC, T])
        SA = sbd("SA", [P, 4, T])
        FA = sbd("FA", [P, 2, T])
        dense.close()
        HTH = sb("HTH", [P, 3, DM], F32R)
        HTL = sb("HTL", [P, 3, DM], F32R)
        Y = sb("Y", [P, KC, T])
        HGH = sb("HGH", [P, KC, P], F32R)
        HGL = sb("HGL", [P, KC, P], F32R)
        SILU = sb("SILU", [P, COLS])
        AM = sb("AM", [P, COLS])
        ATH = sb("ATH", [P, 4, P], F32R)
        ATL = sb("ATL", [P, 4, P], F32R)
        SEL = sb("SEL", [P, 3, P], F32R)
        GSEL = sb("GSEL", [P, 3, P])
        GST = sb("GST", [P, T])
        SLG = sb("SLG", [P, 2, 3, NE + 1])
        YS = H[:, :, :].rearrange("p c t -> p (c t)")[:, 0:DM]
        raw = [ring_low[:, i // 2, (i % 2) * PIECE:(i % 2 + 1) * PIECE] for i in range(NRAW)]
        RAW_SLOT = (4, 5, 6, 0, 1, 2, 3)
        eraw = [raw[i] for i in RAW_SLOT]

        def small(a, n=1, rows=P):
            return SM[0:rows, a:a + n]

        EPSB = small(250)
        def RP(h):
            return scr[:, 1024 + 3 * P * (h % 2):1024 + 3 * P * (h % 2 + 1)]

        def MASK(tt, n):
            return small(128 + NE * tt, NE, n)

        psum = [ctx.enter_context(nc.psum_tensor(f"bank{i}", [P, 512], F32)) for i in range(8)]

        slot_full = [sem(f"slot_full{i}") for i in range(NSLOT)]
        raw_full = [sem(f"raw_full{i}") for i in range(NRAW)]
        pages_full = [sem(f"pages_full{i}") for i in range(NSLOT)]
        consts_in, more_consts_in = sem("consts_in"), sem("more_consts_in")
        states_in = sem("states_in")
        page_idx = sem("page_idx")
        logf_in = sem("logf_in")
        row_done, row_copied = sem("row_done"), sem("row_copied")
        row_turned, row_used = sem("row_turned"), sem("row_used")
        z_done = sem("z_done")
        z_ready = sem("z_ready")
        job_done = sem("job_done")
        job_read = {'a': sem("job_read_act"), 'v': sem("job_read_dve")}
        k_used = sem("k_used")
        out_done = sem("out_done")
        out_added = sem("out_added")
        fraw_full = [sem(f"ffn_raw_full{i}") for i in range(NRAW)]
        fhigh_ready, flow_ready, fpiece_used = sem("ffn_high_ready"), sem("ffn_low_ready"), sem("ffn_piece_used")
        eps_ready = sem("eps_ready")
        x_ready = sem("x_ready")
        hh_ready, hl_ready = sem("h_high"), sem("h_low")
        silu_ready, act_made, act_high, act_low = sem("silu_ready"), sem("act_made"), sem("act_high"), sem("act_low")
        y_done = sem("y_done")
        y_added = sem("y_added")
        h_turned, ht_high, ht_low = sem("h_turned"), sem("ht_high"), sem("ht_low")
        router_done, gates_read, masks_ready = sem("router_done"), sem("gates_read"), sem("masks_ready")
        passes_ready, slots_ready = sem("passes_ready"), sem("slots_ready")
        gather_done, gathered_high, gathered = sem("gather_done"), sem("gathered_high"), sem("gathered")
        gst_done, gst_ready = sem("gate_turn_done"), sem("gate_turned")
        esilu_ready, ea_ready = sem("expert_silu"), sem("expert_act")
        high_ready, low_ready, piece_used = sem("high_ready"), sem("low_ready"), sem("piece_used")
        turn_done, turned_high, turned = sem("act_turn_done"), sem("act_turned_high"), sem("act_turned")
        y_copied, banks_zeroed = sem("y_copied"), sem("banks_zeroed")
        sel_ready, slots_moved = sem("sel_ready"), sem("slots_moved")
        scatter_done, scattered = sem("scatter_done"), sem("scattered")
        stored = sem("stored")
        k_stored = sem("k_stored")
        ev_ffln = sem("fox_ln")
        idx_ready = sem("idx_ready")
        dve_chain = sem("dve_chain")
        act_chain = sem("act_chain")
        pool_chain = sem("pool_chain")
        ct_ready = sem("ct_ready")
        ev = {n: sem(n) for n in (
            "squares1", "h1", "fox_squares", "fox_qk", "fox_logf", "probs_max", "probs_exp", "probs",
            "row_terms", "past_totals", "max_part", "max_diag", "dec_shift", "dec_exp", "dec_sum", "dec_probs",
            "glu_gate", "glu", "conv_taps", "conv_y", "conv_sq", "conv_out", "gla_abs", "gla_ln", "gla_b", "gla_decays",
            "gla_kq", "lag_diff", "lag_exp", "lag_w", "gla_vx", "gla_states", "ve_gla", "s_gla", "gla_sq",
            "gate_silu", "gla_cat", "rope", "ret_p", "ret_kd", "ve_ret", "s_ret", "ret_sq", "cat",
            "squares2", "h2", "x_final", "dense_out", "ff_exp")}

        block = ctx.enter_context(nc.Block())

        def unit(u):
            return slot((UPOS[u] + SHIFT) % NSLOT)

        def unit_full(u):
            n, pages = UPOS[u], u[0] in 'kv'
            count = sum((v[0] in 'kv') == pages for v in UNITS[n % NSLOT:n + 1:NSLOT])
            return (pages_full if pages else slot_full)[n % NSLOT], 16 * count

        def wait_unit(eng, u):
            eng.wait_ge(*unit_full(u))

        def z_unit_end(l, i):
            return l * NZ + max(n for n, t in enumerate(ZORDER) if t[1] == i) + 1

        def wait_unit_used(eng, u):
            kind, l, i = u
            if kind == 'ada':
                eng.wait_ge(row_done, RPOS[u] + 1)
            elif kind == 'in':
                eng.wait_ge(z_done, z_unit_end(l, i))
            elif kind == 'k':
                eng.wait_ge(k_used, l * NS + i + 1)
            elif kind == 'v':
                eng.wait_ge(row_done, RPOS[('pv', l, i // 2)] + 1)
            else:
                eng.wait_ge(out_done, l * KC + 4 * (i + 1))



        def wait_slot_free(eng, u):
            n = UPOS[u]
            if n >= NSLOT:
                wait_unit_used(eng, UNITS[n - NSLOT])
            if NEXT <= n < NEXT + NSLOT:
                if (n + SHIFT) % NSLOT < NLOW:
                    eng.wait_ge(flow_ready, max(q for q in range(NFP) if q % NRAW // 2 == (n + SHIFT) % NSLOT) + 1)
                else:
                    eng.wait_ge(fpiece_used, NFP)

        def bank(l, name):
            return psum[2 + job_no(l, name) % NBANK]

        class Chain:

            def __init__(self, eng, semaphore):
                self.eng, self.sem, self.n = eng, semaphore, 0

            def add(self, ins):
                self.n += 1
                ins.then_inc(self.sem, 1)

            def wait(self):
                self.eng.wait_ge(self.sem, self.n)

            def __call__(self, ins):
                self.add(ins)
                self.wait()

        row_place, turn_place = {}, {}

        def y_tile_no(j, m):
            return 6 * j + m - m // 4 + 1 if FB[j][1] == COLS else 6 * j + m + 1

        GATHER = (2, 3, 6, 7)
        nstored = [0]

        def store(eng, dst, src):
            nstored[0] += 1
            eng.dma_start(dst, src).then_inc(stored, 16)

        @block.sync
        def _(sp):
            early_c = CCOL['cos'][0]
            for dst, src in ((CT[:, :, :], cT), (C[:, 0:early_c], consts[:, 0:early_c]), (VT[:, :, :], vt)):
                sp.dma_start(dst, src).then_inc(consts_in, 16)

            def load_dense():
                for q, (kind, j, i) in enumerate(FSTREAM):
                    if q < NRAW and q % 2 == 0:
                        wait_unit_used(sp, [u for n, u in enumerate(UNITS[:NEXT]) if (n + SHIFT) % NSLOT == q // 2][-1])
                    if q >= NRAW:
                        sp.wait_ge(flow_ready, q - NRAW + 1)
                    a, n = FB[j]
                    if kind != 'w2':
                        w = (ffn_w1 if kind == 'w1' else ffn_w3)[0, :, a + i * PW:a + (i + 1) * PW]
                    else:
                        m = PIECE // (n // P)
                        w = ffn_w2[0, a:a + n, i * m:(i + 1) * m]
                    w = w.rearrange("(c p) n -> p c n", p=P)
                    sp.dma_start(raw[q % NRAW].rearrange("p (c n) -> p c n", c=w.shape[1]),
                                 w).then_inc(fraw_full[q % NRAW], 16)

            for u in UNITS:
                kind, l, i = u
                if kind in 'kv':
                    continue
                if UPOS[u] == len(ROWS_FIRST):
                    for dst, src in ((X[:, :, :], xT), (C[:, early_c:], consts[:, early_c:]),
                                     (G2[:, :, :], gate2.rearrange("l r n -> r l n")),
                                     (RW[:, :, :], router.rearrange("(c p) e -> p c e", p=P))):
                        sp.dma_start(dst, src).then_inc(more_consts_in, 16)
                if UPOS[u] == NEXT:
                    load_dense()
                wait_slot_free(sp, u)
                dst, full = unit(u), unit_full(u)[0]
                if kind == 'ada':
                    w, n = w_ada[l, :, i * COLS:(i + 1) * COLS], COLS
                elif kind == 'in':
                    n = sum(ZW[g] for g in ZUNITS[i])
                    w = w_in[l, :, ZCOL[ZUNITS[i][0]]:ZCOL[ZUNITS[i][0]] + n]
                elif kind == 'out':
                    w, n = w_out[l, :, i * COLS:(i + 1) * COLS], COLS
                sp.dma_start(dst[:, 0:KC * n].rearrange("p (c n) -> p c n", n=n),
                             w.rearrange("(c p) n -> p c n", p=P)).then_inc(full, 16)

            def load_piece(e, q):
                kind, j, half = STREAM[q]
                if kind < 2:
                    w = (moe_w1, moe_w3)[kind][0, bass.ds(e, 1), half * 512:(half + 1) * 512, j * COLS:(j + 1) * COLS]
                    n = COLS
                else:
                    w = moe_w2[0, bass.ds(e, 1), j * COLS + half * 256:j * COLS + (half + 1) * 256, :]
                    n = DM
                sp.dma_start(eraw[q % NRAW].rearrange("p (c n) -> p c n", n=n),
                             w.rearrange("e (c p) n -> p (e c) n", p=P)).then_inc(raw_full[q % NRAW], 16)

            def raw_free(p, e, q):
                if q == SPOS[(2, 0, 0)]:
                    return
                if q == SPOS[(2, 0, 0)] - 1:
                    q += 1
                sp.wait_ge(low_ready, p * (NE * NPC) + e * NPC + q - NRAW + 1)

            for q in range(NRAW):
                wait_unit_used(sp, [u for n, u in enumerate(UNITS) if (n + SHIFT) % NSLOT == RAW_SLOT[q] // 2][-1])
                load_piece(0, q)
            sp.wait_ge(passes_ready, 1)
            passes = sp.value_load(PASSES[0:1, 0:1], min_val=1, max_val=NPASS)
            with sp.Fori(0, NPASS) as p:
                with sp.If(p < passes):
                    with sp.Fori(0, NE - 1) as e:
                        for q in range(NRAW, NPC + NRAW):
                            raw_free(p, e, q)
                            load_piece(e if q < NPC else e + 1, q % NPC)
                    for q in range(NRAW, NPC):
                        raw_free(p, NE - 1, q)
                        load_piece(NE - 1, q)
                    with sp.If(p + 1 < passes):
                        for q in range(NPC, NPC + NRAW):
                            raw_free(p, NE - 1, q)
                            load_piece(0, q % NPC)
            sp.wait_ge(stored, 16 * NSTORES)

        @block.gpsimd
        def _(pool):
            chain = Chain(pool, pool_chain)
            pool.dma_start(IDXI[:, :], ptr).then_inc(page_idx, 16)
            chain(nc.gpsimd.memset(UP[:, :, 0:KW - 1], 0.0))
            G = nc.gpsimd

            def glu(l):
                ca = Z[:, ZT['ca']:ZT['ca'] + 2, :]
                cg = Z[:, ZT['cg']:ZT['cg'] + 2, :]
                pool.wait_ge(ev["glu_gate"], l + 1)
                pool.wait_ge(states_in, 64 * (l + 1))
                chain.add(G.tensor_tensor(UB[:, :, :, KW - 1], ca[:, :, NP:T], cg[:, :, NP:T], ALU.mult))
                G.tensor_tensor(UP[:, :, KW - 1:], ca[:, :, 0:NP], cg[:, :, 0:NP], ALU.mult).then_inc(ev["glu"], 1)
                chain.wait()
                pool.wait_ge(ev["glu"], l + 1)

            def taps(l, first, last):
                y = Z[:, ZT['ca']:ZT['ca'] + 2, 0:NP]
                cw = v_(l, 'conv_w', 0, 2 * KW).rearrange("p (c k) -> p c k", c=2)
                t = O[:, :, 0:NP]
                for k in range(first, last):
                    w = cw[:, :, k:k + 1].to_broadcast([P, 2, NP])
                    chain(G.tensor_tensor(y if k == 0 else t, UP[:, :, k:k + NP], w, ALU.mult))
                    if k:
                        chain(G.tensor_tensor(y, y, t, ALU.add))
                if last == KW:
                    G.memset(small(249), 0.0).then_inc(ev["conv_taps"], 1)
                    pool.wait_ge(ev["conv_taps"], l + 1)

            pool.wait_ge(idx_ready, L)

            def gather_logf(l):
                pool.wait_ge(ev["fox_qk"], l + 1)
                for b in range(NS):
                    nc.gpsimd.indirect_dma_start(
                        scr[:, 3072 + b * TPP * NH:3072 + (b + 1) * TPP * NH], None,
                        cache_logf.rearrange("n l (s t) h -> (n l s) (t h)", t=TPP),
                        bass.IndirectOffsetOnAxis(ap=IDX[:, l, b:b + 1], axis=0)).then_inc(logf_in, 16)

            for l in range(L):
                if l:
                    pool.wait_ge(ev["cat"], l)
                    pool.wait_ge(stored, 16 * STORES_PER_LAYER * l)
                    pool.wait_ge(ev["dense_out"], 1)
                    chain(G.memset(UP[:, :, 0:KW - 1], 0.0))
                for c in range(2):
                    pool.dma_start(UB[:, c, :, 0:KW - 1], conv_in[l, :, c]).then_inc(states_in, 16)
                pool.dma_start(SG[:, :, :], gla_in[l]).then_inc(states_in, 16)
                pool.dma_start(SR[:, :, :], ret_in[l]).then_inc(states_in, 16)
                for kind, cache in (('k', cache_k), ('v', cache_v)):
                    rows = cache.rearrange("n l (s t) h d -> (n l s) (t h d)", t=TPP)
                    for b in range(NS):
                        u = (kind, l, b)
                        if (kind, b) == ('k', 3):
                            glu(l)
                            taps(l, 0, 12)
                        elif kind == 'k' and b > 3:
                            taps(l, 12 + 3 * (b - 4), 15 + 3 * (b - 4))
                        elif (kind, b) == ('v', 0):
                            taps(l, 24, KW)
                        wait_slot_free(pool, u)
                        nc.gpsimd.indirect_dma_start(
                            unit(u), None, rows,
                            bass.IndirectOffsetOnAxis(ap=IDX[:, l, b:b + 1], axis=0)
                        ).then_inc(unit_full(u)[0], 16)
                        if (kind, b) == ('k', 2):
                            gather_logf(l)

        @block.tensor
        def _(pe):
            mm = nc.tensor.matmul
            emitted = {'job': 0, 'step': 0, 'closed': 0}

            def open_job(l, name):
                n = job_no(l, name)
                if n >= NBANK:
                    who, count = read_no(*divmod_job(n - NBANK))
                    pe.wait_ge(job_read[who], count)
                return psum[2 + n % NBANK]

            def close(ins):
                emitted['closed'] += 1
                ins.then_inc(job_done, 1)

            def one(l, name, lhsT, rhs, rows=P, at=0):
                b = open_job(l, name)
                n = rhs.free_size()
                close(mm(b[at:at + rows, 0:n], lhsT, rhs, start=True, stop=True))

            def norm_sum(l, name, src, squares):
                b = open_job(l, name)
                for c in range(KC):
                    pe.wait_ge(squares, l * KC + c + 1)
                    ins = mm(b[:, 0:T], ones, src[:, c, :], start=(c == 0), stop=(c == KC - 1))
                close(ins)

            def project(l, i):
                wait_unit(pe, ('in', l, i))
                n = sum(ZW[g] for g in ZUNITS[i])
                w = unit(('in', l, i))[:, 0:KC * n].rearrange("p (c n) -> p c n", n=n)
                for pos, (z, u, col, m) in enumerate(ZORDER):
                    if u != i:
                        continue
                    if l * NZ + pos >= 2:
                        pe.wait_ge(z_ready, l * NZ + pos - 1)
                    for c in range(KC):
                        if pos == 0:
                            pe.wait_ge(ev["h1"], l * KC + c + 1)
                        ins = mm(psum[pos % 2][0:m, 0:T], w[:, c, col:col + m], H[:, c, :],
                                 start=(c == 0), stop=(c == KC - 1))
                    ins.then_inc(z_done, 1)

            def turn(out, src, rows):
                return nc.tensor.transpose(out, src, ident[0:rows, 0:rows])

            def token_major(l, name, tt, tiles):
                b = open_job(l, name)
                for n, src in enumerate(tiles):
                    ins = turn(b[:, n * P:(n + 1) * P], src[:, tt * P:(tt + 1) * P], P)
                close(ins)

            def sample_outer(l, names, kcol):
                for pr in range(2):
                    b = open_job(l, names[pr])
                    for s in range(2):
                        h = 2 * pr + s
                        ins = mm(b[s * HD:(s + 1) * HD, :], KV8[:, kcol + h * HD:kcol + (h + 1) * HD],
                                 VE[:, h].rearrange("p b v -> p (b v)"), start=True, stop=True)
                    close(ins)

            def sample_read(l, names, S4, q):
                for s in range(2):
                    b = open_job(l, names[s])
                    for pr in range(2):
                        for i in range(NS):
                            ins = mm(b[s * HD:(s + 1) * HD, pr * NS + i:pr * NS + i + 1],
                                     S4[s * HD:(s + 1) * HD, pr, i, :],
                                     q[s * HD:(s + 1) * HD, pr, NP + i:NP + i + 1], start=True, stop=True)
                    close(ins)

            def three(out, sh, sl, mh, ml, start, stop):
                mm(out, sh, mh, start=start, stop=False)
                mm(out, sh, ml, start=False, stop=False)
                return mm(out, sl, mh, start=False, stop=stop)

            def row_product(job, step):
                kind, l, i = job
                n = RPOS[job]
                if step == 0:
                    if n >= 1:
                        pe.wait_ge(row_copied, n)
                    if kind == 'pv' and i == 0:
                        pe.wait_ge(ev["dec_probs"], l + 1)
                if kind == 'ada':
                    if step == 0:
                        wait_unit(pe, job)
                    w = unit(job).rearrange("p (c n) -> p c n", n=COLS)
                    ins = mm(psum[0][0:NS + 1, :], CT[:, step, :], w[:, step, :],
                             start=(step == 0), stop=(step == KC - 1))
                else:
                    half, t = step // TPP, step % TPP
                    v = ('v', l, 2 * i + half)
                    if t == 0:
                        wait_unit(pe, v)
                    ins = mm(psum[0][0:NH, half * GW:(half + 1) * GW], PR4[:, v[2], :, t],
                             unit(v)[:, t * GW:(t + 1) * GW], start=(t == 0), stop=(t == TPP - 1))
                if step == row_steps(job) - 1:
                    ins.then_inc(row_done, 1)
                    row_place[n] = emitted['closed']

            def turn_rows(job):
                n = RPOS[job]
                pe.wait_ge(row_copied, n + 1)
                if n >= 1:
                    pe.wait_ge(row_used, n)
                r = ROWS[:, n % 2, :]
                if job[0] == 'ada':
                    for q in range(4):
                        ins = mm(psum[1][:, q * (NS + 1):(q + 1) * (NS + 1)], r[:, q * P:(q + 1) * P],
                                 ident[0:NS + 1, 0:NS + 1], start=True, stop=True)
                else:
                    for q in range(4):
                        ins = mm(psum[1][:, 2 * q:2 * q + 2], r[0:NH, q * P:(q + 1) * P],
                                 ident[0:NH, 2 * (q % 2):2 * (q % 2) + 2], start=True, stop=True)
                ins.then_inc(row_turned, 1)
                turn_place[n] = emitted['closed']

            def row_steps(job):
                return KC if job[0] == 'ada' else 2 * TPP


            def background(jobs, count):
                for _ in range(count):
                    if emitted['job'] >= RPOS[jobs[-1]] + 1:
                        return
                    job, step = ROWJOBS[emitted['job']], emitted['step']
                    row_product(job, step)
                    if step == row_steps(job) // 2 - 1 and job != jobs[0]:
                        turn_rows(ROWJOBS[emitted['job'] - 1])
                    emitted['step'] += 1
                    if emitted['step'] == row_steps(job):
                        emitted['job'] += 1
                        emitted['step'] = 0

            def finish_background(jobs):
                background(jobs, 1000)
                turn_rows(jobs[-1])

            pe.wait_ge(consts_in, 16 * 3)
            for l in range(L):
                def fill(place):
                    background(ROWS_OF[l], FILL[place][l])

                if l == 0:
                    pe.wait_ge(ct_ready, 1)
                    background(ROWS_FIRST, KC * len(ROWS_FIRST))
                    turn_rows(ROWS_FIRST[-1])
                norm_sum(l, 'rms1', H, ev["squares1"])
                if l == 0:
                    pe.wait_ge(more_consts_in, 16 * 4)
                    pe.wait_ge(row_used, len(ROWS_FIRST))
                for i in range(2):
                    project(l, i)
                pe.wait_ge(ev["fox_squares"], l + 1)
                for i in range(4):
                    one(l, f'fn{i}', heads, SQ[:, i, :])
                project(l, 2)
                pe.wait_ge(ev["fox_qk"], l + 1)
                fk = Z[:, ZT['fk']:ZT['fk'] + 2, :]
                fq = Z[:, ZT['fq']:ZT['fq'] + 2, :]
                fv = Z[:, ZT['fv']:ZT['fv'] + 2, :]
                for tt in range(2):
                    token_major(l, f'tkv{tt}', tt, (fv[:, 0, :], fv[:, 1, :]))
                b = open_job(l, 'tqs')
                for n in range(2):
                    ins = turn(b[0:NS, n * P:(n + 1) * P], fq[:, n, NP:T], P)
                close(ins)
                for i in range(4):
                    b = open_job(l, f'qb{i}')
                    if i == 0:
                        who, count = read_no(l, 'tqs')
                        pe.wait_ge(job_read[who], count)
                    for n in range(2):
                        ins = mm(b[:, n * GW:(n + 1) * GW], ident[0:NS, 2 * i + n:2 * i + n + 1].to_broadcast([NS, P]),
                                 QS[:, :], start=True, stop=True)
                    close(ins)
                for i in range(3, 8):
                    project(l, i)
                pe.wait_ge(z_ready, (l + 1) * NZ)
                pe.wait_ge(ev["fox_logf"], l + 1)
                for h in range(NH):
                    c, s = h // 2, (h % 2) * HD
                    b = open_job(l, f's{h}')
                    row = ident[0:NH, h:h + 1].to_broadcast([NH, P])
                    for at, qt, kt in ((0, 0, 0), (P, 1, 0), (2 * P, 1, 1)):
                        o = b[:, at:at + P]
                        mm(o, fq[s:s + HD, c, qt * P:(qt + 1) * P], fk[s:s + HD, c, kt * P:(kt + 1) * P],
                           start=True, stop=False)
                        mm(o, FS[:, qt * P:(qt + 1) * P], row, start=False, stop=False)
                        ins = mm(o, row, FX[:, kt * P:(kt + 1) * P], start=False, stop=True)
                    close(ins)
                fill('s')
                for h in range(NH):
                    c, s = h // 2, (h % 2) * HD
                    fill('pt')
                    pe.wait_ge(ev["probs"], l * NH + h + 1)
                    b = open_job(l, f'pt{h}')
                    for at in range(3):
                        ins = turn(b[:, at * P:(at + 1) * P], PS[:, h, at * P:(at + 1) * P], P)
                    close(ins)
                    b = open_job(l, f'o{h}')
                    who, count = read_no(l, f'pt{h}')
                    pe.wait_ge(job_read[who], count)
                    o = b[s:s + HD, :]
                    mm(o[:, 0:NP], TMV[:, 0, h * HD:(h + 1) * HD], PT[:, 0:NP], start=True, stop=False)
                    close(mm(o[:, P:NP], TMV[:, 1, h * HD:(h + 1) * HD], PT[:, NP:3 * P], start=False, stop=True))
                fill('snew')
                pe.wait_ge(ev["row_terms"], l + 1)
                one(l, 'snew', ones, small(64, 32))
                fill('suf')
                pe.wait_ge(ev["past_totals"], l + 1)
                b = open_job(l, 'suf')
                mm(b[:, 0:32], c_('later'), small(96, 32), start=True, stop=False)
                close(mm(b[:, 0:32], c_('ones', NH), small(128, 32, NH), start=False, stop=True))
                fill('mxt')
                pe.wait_ge(ev["max_part"], l + 1)
                b = open_job(l, 'mxt')
                close(turn(b[0:32, 0:P], small(160, 32), P))
                fill('mxb')
                pe.wait_ge(ev["max_diag"], l + 1)
                one(l, 'mxb', c_('ones', 32), small(192, 32, 32))
                fill('sumb')
                pe.wait_ge(ev["dec_sum"], l + 1)
                one(l, 'sumb', ones, small(64, 32))
                cy = Z[:, ZT['ca']:ZT['ca'] + 2, :]
                fill('mean')
                pe.wait_ge(ev["conv_y"], l + 1)
                b = open_job(l, 'mean')
                for c in range(2):
                    ins = mm(b[:, 0:T], ones, cy[:, c, :], start=(c == 0), stop=(c == 1))
                close(ins)
                fill('var')
                pe.wait_ge(ev["conv_sq"], l + 1)
                b = open_job(l, 'var')
                for c in range(2):
                    ins = mm(b[:, 0:T], ones, TA2[:, c, :], start=(c == 0), stop=(c == 1))
                close(ins)
                gv = Z[:, ZT['gv']:ZT['gv'] + 2, :]
                gq = Z[:, ZT['gq']:ZT['gq'] + 2, :]
                gk = Z[:, ZT['gk']:ZT['gk'] + 2, :]
                fill('gate')
                for c in range(2):
                    one(l, f'gate{c}', G2[:, l, c * P:(c + 1) * P], Z[0:LR, ZT['glr'], :])
                for lag in range(CH):
                    fill('lag')
                    pe.wait_ge(ev["lag_w"], l * CH + lag + 1)
                    b = open_job(l, f'att{lag}')
                    n = NCH * (CH - lag)
                    for c in range(2):
                        ins = mm(b[:, c * n:(c + 1) * n], heads, WX[lag % 2][:, c * n:(c + 1) * n],
                                 start=True, stop=True)
                    close(ins)
                fill('kq')
                pe.wait_ge(ev["gla_kq"], l + 1)
                for tt in range(2):
                    token_major(l, f'gkv{tt}', tt, (GKD[:, 0, :], GKD[:, 1, :], gv[:, 0, :], gv[:, 1, :]))
                b = open_job(l, 'gts')
                for n, src in enumerate((gk[:, 0, NP:T], gk[:, 1, NP:T], gv[:, 0, NP:T], gv[:, 1, NP:T])):
                    ins = turn(b[0:NS, n * P:(n + 1) * P], src, P)
                close(ins)
                for tt in range(2):
                    fill('vx')
                    pe.wait_ge(ev["gla_vx"], l * 2 + tt + 1)
                    for pr in range(2):
                        b = open_job(l, f'kv{tt}{pr}')
                        for s in range(2):
                            h = 2 * pr + s
                            ins = mm(b[s * HD:(s + 1) * HD, :], TMK[:, tt, h * HD:(h + 1) * HD],
                                     VX[:, h].rearrange("p n v -> p (n v)"), start=True, stop=True)
                        close(ins)
                fill('states')
                pe.wait_ge(ev["gla_states"], l + 1)
                for s in range(2):
                    b = open_job(l, f'gi{s}')
                    for pr in range(2):
                        for n in range(1, NCH):
                            o = pr * NP + n * CH
                            ins = mm(b[s * HD:(s + 1) * HD, o:o + CH], SH[s * HD:(s + 1) * HD, pr, n - 1, :],
                                     GQD[s * HD:(s + 1) * HD, pr, n * CH:(n + 1) * CH], start=True, stop=True)
                    close(ins)
                fill('gx')
                pe.wait_ge(ev["ve_gla"], l + 1)
                sample_outer(l, ('gx0', 'gx1'), 0)
                fill('gs')
                pe.wait_ge(ev["s_gla"], l + 1)
                sample_read(l, ('gs0', 'gs1'), SG4, gq)
                fill('gn')
                pe.wait_ge(ev["gla_sq"], l + 1)
                for c in range(2):
                    one(l, f'gn{c}', heads, BCT[:, c, :])
                rv = Z[:, ZT['rv']:ZT['rv'] + 2, :]
                rq = Z[:, ZT['rq']:ZT['rq'] + 2, :]
                rk = Z[:, ZT['rk']:ZT['rk'] + 2, :]
                fill('rr')
                for i in range(4):
                    one(l, f'rr{i}', c_('swap'), Z[:, ZT['rq'] + i, :])
                fill('rope')
                pe.wait_ge(ev["rope"], l + 1)
                for tt in range(2):
                    token_major(l, f'rkv{tt}', tt, (rk[:, 0, :], rk[:, 1, :], rv[:, 0, :], rv[:, 1, :]))
                b = open_job(l, 'rts')
                for n, src in enumerate((rk[:, 0, NP:T], rk[:, 1, NP:T], rv[:, 0, NP:T], rv[:, 1, NP:T])):
                    ins = turn(b[0:NS, n * P:(n + 1) * P], src, P)
                close(ins)
                who, count = read_no(l, 'rts')
                pe.wait_ge(job_read[who], count)
                for h in range(NH):
                    c, s = h // 2, (h % 2) * HD
                    b = open_job(l, f'rs{h}')
                    mm(b[:, 0:NP], rk[s:s + HD, c, 0:P], rq[s:s + HD, c, 0:NP], start=True, stop=True)
                    close(mm(b[:, NP:3 * P], rk[s:s + HD, c, P:NP], rq[s:s + HD, c, P:NP], start=True, stop=True))
                    fill('rp')
                    pe.wait_ge(ev["ret_p"], l * NH + h + 1)
                    b = open_job(l, f'ro{h}')
                    o = b[s:s + HD, :]
                    mm(o[:, 0:NP], TMV[:, 0, h * HD:(h + 1) * HD], RP(h)[:, 0:NP], start=True, stop=False)
                    close(mm(o[:, P:NP], TMV[:, 1, h * HD:(h + 1) * HD], RP(h)[:, NP:3 * P], start=False, stop=True))
                fill('rst')
                pe.wait_ge(ev["ret_kd"], l + 1)
                b = open_job(l, 'rst')
                for h in range(NH):
                    c, s = h // 2, (h % 2) * HD
                    for tt in range(2):
                        ins = mm(b[s:s + HD, c * HD:(c + 1) * HD], TMK[:, tt, h * HD:(h + 1) * HD],
                                 TMV[:, tt, h * HD:(h + 1) * HD], start=(tt == 0), stop=(tt == 1))
                close(ins)
                fill('rx')
                pe.wait_ge(ev["ve_ret"], l + 1)
                sample_outer(l, ('rx0', 'rx1'), 0)
                fill('rd')
                pe.wait_ge(ev["s_ret"], l + 1)
                sample_read(l, ('rd0', 'rd1'), SR4, rq)
                finish_background(ROWS_OF[l])
                pe.wait_ge(ev["ret_sq"], l + 1)
                for c in range(2):
                    one(l, f'rn{c}', heads, BCT[:, c, :])
                pe.wait_ge(row_used, RPOS[ROWS_OF[l][-1]] + 1)
                pe.wait_ge(ev["cat"], l + 1)
                for m in range(KC):
                    if m % 4 == 0:
                        wait_unit(pe, ('out', l, m // 4))
                    w = unit(('out', l, m // 4)).rearrange("p (c n) -> p c n", n=COLS)
                    if m >= 2:
                        pe.wait_ge(out_added, l * KC + m - 1)
                    for c in range(KC):
                        ins = mm(psum[m % 2][:, 0:T], w[:, c, (m % 4) * P:(m % 4 + 1) * P], CAT[:, c, :],
                                 start=(c == 0), stop=(c == KC - 1))
                    ins.then_inc(out_done, 1)
                norm_sum(l, 'rms2', Z[:, 0:KC, :], ev["squares2"])
                if l % 2 == 0:
                    def dense_piece(q):
                        kind, j, i = FSTREAM[q]
                        pe.wait_ge(flow_ready, q + 1)
                        n = PW if kind != 'w2' else PIECE // (FB[j][1] // P)
                        return [t[:, q % NSPLIT, :].rearrange("p (c n) -> p c n", n=n) for t in (WH, WL)]

                    for q, (kind, j, i) in enumerate(FSTREAM):
                        wh, wl = dense_piece(q)
                        if kind != 'w2':
                            for t in range(2):
                                n = 2 * PAIRS.index(('w1', j, i)) + t
                                if n >= 2:
                                    pe.wait_ge(silu_ready if kind == 'w1' else act_made, n - 1)
                                for c in range(KC):
                                    if q == 0 and t == 0:
                                        pe.wait_ge(hl_ready, c + 1)
                                    cols = slice(t * P, (t + 1) * P)
                                    ins = three(psum[t + 2 * (kind == 'w3')][:, 0:T], wh[:, c, cols], wl[:, c, cols],
                                                HH[:, c, :], HL[:, c, :], c == 0, c == KC - 1)
                        else:
                            nk = FB[j][1] // P
                            pe.wait_ge(act_low, sum(w // P for _, w in FB[:j + 1]))
                            for mm_ in range(16 // nk if nk == 4 else KC):
                                m = 4 * i + mm_
                                if KC * j + m >= 4:
                                    pe.wait_ge(y_added, KC * j + m - 3)
                                for k in range(nk):
                                    cols = slice(mm_ * P, (mm_ + 1) * P)
                                    ins = three(psum[4 + m % 4][:, 0:T], wh[:, k, cols], wl[:, k, cols],
                                                FAH[:, j % 2, k, :], FAL[:, j % 2, k, :], k == 0, k == nk - 1)
                                if mm_ < (4 if nk == 4 else KC) - 1:
                                    ins.then_inc(y_done, 1)
                        ins.then_inc(fpiece_used, 1)
                else:
                    rows = (P, P, NS)
                    pe.wait_ge(ev["h2"], (l + 1) * KC)
                    for tt, n in enumerate(rows):
                        for c in range(KC):
                            ins = mm(psum[0][0:n, tt * NE:(tt + 1) * NE], H[:, c, tt * P:tt * P + n], RW[:, c, :],
                                     start=(c == 0), stop=(c == KC - 1))
                    ins.then_inc(router_done, 1)
                    pe.wait_ge(out_added, l * KC + KC)
                    for i in range(6):
                        tt, half = i // 2, i % 2
                        n = rows[tt]
                        for q in range(4):
                            ins = turn(psum[2 + i][0:n, q * P:(q + 1) * P], H[:, 4 * half + q, tt * P:tt * P + n], P)
                        ins.then_inc(h_turned, 1)
                    pe.wait_ge(masks_ready, 1)
                    for tt, n in enumerate(rows):
                        o = psum[1][0:n, tt * NE:(tt + 1) * NE]
                        mm(o, c_('later', n, 0, n), MASK(tt, n), start=True, stop=(tt == 2))
                        for t2 in range(tt + 1, 3):
                            mm(o, c_('ones', rows[t2], 0, n), MASK(t2, rows[t2]), start=False, stop=(t2 == 2))
                    for tt, n in enumerate(rows):
                        ins = mm(psum[1][:, 3 * NE:4 * NE], c_('ones', n), MASK(tt, n), start=(tt == 0), stop=(tt == 2))
                    ins.then_inc(router_done, 1)
                    pe.wait_ge(ht_high, 6)
                    pe.wait_ge(ht_low, 6)
                    pe.wait_ge(passes_ready, 1)
                    passes = pe.value_load(PASSES[0:1, 0:1], min_val=1, max_val=NPASS)

                    def gather(slots, free):
                        pe.wait_ge(slots_ready, slots)
                        for n, (half, part) in enumerate(((0, HTH), (0, HTL), (1, HTH), (1, HTL))):
                            if n >= 2 and free:
                                pe.wait_ge(*free[n - 2])
                            b = psum[GATHER[n]]
                            for q in range(4):
                                c = 4 * half + q
                                for tt, k in enumerate(rows):
                                    ins = mm(b[:, q * P:(q + 1) * P], part[0:k, tt, c * P:(c + 1) * P],
                                             SEL[0:k, tt, :], start=(tt == 0), stop=(tt == 2))
                            ins.then_inc(gather_done, 1)

                    def expert(p, e):
                        def at(per, n):
                            return p * (NE * per) + e * per + n

                        def piece(kind, j, half):
                            q = SPOS[(kind, j, half)]
                            pe.wait_ge(low_ready, at(NPC, q + 1))
                            n = DM if kind == 2 else COLS
                            return [t[:, q % NSPLIT, :].rearrange("p (c n) -> p c n", n=n) for t in (WH, WL)]

                        def up(kind, j):
                            for half in range(2):
                                wh, wl = piece(kind, j, half)
                                for i in range(4):
                                    c = 4 * half + i
                                    ins = three(psum[2 * (j % 2) + kind][:, :], HGH[:, c, :], HGL[:, c, :],
                                                wh[:, i, :], wl[:, i, :], c == 0, c == KC - 1)
                                    if i == 3:
                                        ins.then_inc(piece_used, 1)
                                    if j == 1 and kind == 0:
                                        scatter(at, c)

                        def turn_block(j):
                            pe.wait_ge(ea_ready, at(EB, j + 2))
                            pe.wait_ge(*((scattered, at(KC, KC + 7)), (turned, at(EB, 1)), (gst_ready, at(1, 1)))[j] if j < 3
                                       else (turned, at(EB, j - 1)))
                            b = 6 + (j > 0) * (j + 1) % 2
                            for k in range(4):
                                ins = turn(psum[b][:, k * P:(k + 1) * P], AM[:, k * P:(k + 1) * P], P)
                            ins.then_inc(turn_done, 1)

                        def down(j):
                            pe.wait_ge(turned, at(EB, j + 1))
                            for i in range(2):
                                wh, wl = piece(2, j, i)
                                for half in range(2):
                                    if j == 0 and i == 0:
                                        pe.wait_ge(y_copied, at(2, 1 + half))
                                    for k in range(2):
                                        cols = slice(half * 512, (half + 1) * 512)
                                        ins = three(psum[4 + half][:, :], ATH[:, 2 * i + k, :], ATL[:, 2 * i + k, :],
                                                    wh[:, k, cols], wl[:, k, cols], j == 0 and i == 0 and k == 0,
                                                    j == EB - 1 and i == 1 and k == 1)
                                ins.then_inc(piece_used, 1)

                        for j in range(EB):
                            if j == 0:
                                pe.wait_ge(gathered_high, at(2, 2))
                                pe.wait_ge(gathered, at(2, 2))
                            if j != 1:
                                pe.wait_ge(ea_ready, at(EB, max(j, 1)))
                            up(0, j)
                            if j >= 1:
                                turn_block(j - 1)
                            if j == 1:
                                pe.wait_ge(scattered, at(KC, 2 * KC))
                                for tt, n in enumerate(rows):
                                    ins = turn(psum[7][:, tt * P:tt * P + n], GSEL[0:n, tt, :], n)
                                ins.then_inc(gst_done, 1)
                            up(1, j)
                            if j >= 1:
                                down(j - 1)
                        turn_block(EB - 1)
                        gather(at(1, 2), [(turned, at(EB, EB - 1)), (turned, at(EB, EB))])
                        down(EB - 1)
                    def scatter(at, m):
                        if m % 4 == 0:
                            pe.wait_ge(y_copied, at(2, 1 + m // 4))
                        if m < 2:
                            pe.wait_ge((gathered_high, gathered)[m], at(2, 2))
                        else:
                            pe.wait_ge(scattered, at(KC, KC + m - 1))
                        mm(psum[6 + m % 2][:, 0:T], YS[:, m * P:(m + 1) * P], GST[:, :], start=True,
                           stop=True).then_inc(scatter_done, 1)

                    gather(1, None)
                    with pe.Fori(0, NPASS) as p:
                        with pe.If(p < passes):
                            with pe.Fori(0, NE) as e:
                                expert(p, e)
                    for m in range(KC):
                        scatter(lambda per, n: passes * (NE * per) + n, m)

        @block.scalar
        def _(act):
            chain = Chain(act, act_chain)
            A = nc.scalar.activation
            act.wait_ge(eps_ready, 1)
            act.wait_ge(consts_in, 16 * 3)
            A(CT[:, :, :], CT[:, :, :], ACT.Silu).then_inc(ct_ready, 1)

            def rows(l, name):
                n = job_no(l, name)
                while True:
                    if turned[0] in turn_place and turned[0] < copied[0] and turn_place[turned[0]] <= n and (
                            copied[0] not in row_place or turn_place[turned[0]] <= row_place[copied[0]]):
                        use_rows(ROWJOBS[turned[0]])
                        turned[0] += 1
                    elif copied[0] in row_place and row_place[copied[0]] <= n:
                        copy_rows(ROWJOBS[copied[0]])
                        copied[0] += 1
                    else:
                        return

            copied, turned = [0], [0]

            def copy_rows(job):
                n, kind = RPOS[job], job[0]
                act.wait_ge(row_done, n + 1)
                if n >= 2:
                    act.wait_ge(row_turned, n - 1)
                r = NS + 1 if kind == 'ada' else NH
                A(ROWS[0:r, n % 2, :], psum[0][0:r, :], ACT.Copy).then_inc(row_copied, 1)

            def use_rows(job):
                kind, l, i = job
                act.wait_ge(row_turned, RPOS[job] + 1)
                if kind == 'ada':
                    for q in range(4):
                        ins = A(MOD[:, l, 4 * i + q, :], psum[1][:, q * (NS + 1):(q + 1) * (NS + 1)], ACT.Identity,
                                bias=v_(l, 'b_ada', 4 * i + q))
                        if q < 3:
                            chain.add(ins)
                    chain.wait()
                else:
                    ins = A(small(96 + 8 * i, 8), psum[1][:, 0:8], ACT.Copy)
                ins.then_inc(row_used, 1)

            def job(l, name):
                rows(l, name)
                act.wait_ge(job_done, job_no(l, name) + 1)
                return bank(l, name)

            def read(ins):
                ins.then_inc(job_read['a'], 1)

            def wait_read(l, name):
                act.wait_ge(job_read['a'], read_no(l, name)[1])

            def evacuate(l, i):
                for pos, (z, u, col, m) in enumerate(ZORDER):
                    if u == i:
                        act.wait_ge(z_done, l * NZ + pos + 1)
                        A(Z[0:m, z, :], psum[pos % 2][0:m, 0:T], ACT.Copy).then_inc(z_ready, 1)

            def log_sigmoid(x, e, ready, ready_n, exp_done, done):
                act.wait_ge(ready, ready_n)
                chain(A(e, e, ACT.Exp, scale=-1.0))
                A(e, e, ACT.Ln, bias=1.0).then_inc(done, 1)

            def round_dense(q):
                act.wait_ge(fraw_full[q % NRAW], 16 * (q // NRAW + 1))
                A(WH[:, q % NSPLIT, :], raw[q % NRAW], ACT.Copy).then_inc(fhigh_ready, 1)

            for l in range(L):
                if l:
                    act.wait_ge(stored, 16 * nstored[0])
                if l:
                    for c in range(KC):
                        act.wait_ge(x_ready, c + 1)
                        A(H[:, c, :], X[:, c, :], ACT.Square).then_inc(ev["squares1"], 1)
                A(R[:, :], job(l, 'rms1')[:, 0:T], ACT.Sqrt, bias=EPSB, scale=1.0 / DM).then_inc(job_read['a'], 1)
                for i in range(2):
                    evacuate(l, i)
                for i in range(4):
                    read(A(RN[:, i, :], job(l, f'fn{i}')[:, 0:T], ACT.Sqrt, bias=EPSB, scale=1.0 / HD))
                evacuate(l, 2)
                act.wait_ge(z_ready, l * NZ + ZPOS[ZT['cg'] + 1] + 1)
                cg = Z[:, ZT['cg']:ZT['cg'] + 2, :]
                A(cg, cg, ACT.Sigmoid).then_inc(ev["glu_gate"], 1)
                for tt in range(2):
                    b = job(l, f'tkv{tt}')
                    read(A(TMV[:, tt, :], b[:, 0:GW], ACT.Copy))
                read(A(QS[:, :], job(l, 'tqs')[0:NS, 0:GW], ACT.Copy))
                for i in range(4):
                    read(A(QB[:, 2 * i:2 * i + 2, :].rearrange("p b f -> p (b f)"), job(l, f'qb{i}')[:, :], ACT.Copy))
                act.wait_ge(ev["fox_qk"], l + 1)
                act.dma_start(k_out[l], Z[:, ZT['fk']:ZT['fk'] + 2, :]).then_inc(k_stored, 16)
                act.wait_ge(z_ready, l * NZ + ZPOS[ZT['fv'] + 1] + 1)
                store(act, v_out[l], Z[:, ZT['fv']:ZT['fv'] + 2, :])
                act.wait_ge(ev["ff_exp"], l + 1)
                chain(A(LF[:, :], LF[:, :], ACT.Exp, scale=-1.0))
                A(LF[:, :], LF[:, :], ACT.Ln, bias=1.0).then_inc(ev_ffln, 1)
                act.wait_ge(ev["fox_logf"], l + 1)
                store(act, logf_out[l], LF[:, :])
                for i in range(3, 8):
                    evacuate(l, i)
                act.wait_ge(ev["glu"], l + 1)
                for c in range(2):
                    store(act, conv_out[l, :, c, 0:KW - 1], UP[:, c, NP:NP + KW - 1])
                    store(act, conv_out[l, :, c, KW - 1:(NS + 1) * (KW - 1)].rearrange("p (b k) -> p b k", b=NS),
                          UB[:, c, :, 1:KW])
                rows(l, 'pt0')
                for h in range(NH):
                    act.wait_ge(ev["probs_max"], l * NH + h + 1)
                    A(PS[:, h, 0:P], PS[:, h, 0:P], ACT.Exp, bias=small(2 * h), accum_out=small(8 + 2 * h)).then_inc(ev["probs_exp"], 1)
                    A(PS[:, h, P:3 * P], PS[:, h, P:3 * P], ACT.Exp, bias=small(2 * h + 1),
                      accum_out=small(9 + 2 * h)).then_inc(ev["probs_exp"], 1)
                for h in range(NH):
                    c, s = h // 2, (h % 2) * HD
                    read(A(PT[:, :], job(l, f'pt{h}')[:, 0:3 * P], ACT.Copy))
                    read(A(CAT[s:s + HD, 2 + c, 0:NP], job(l, f'o{h}')[s:s + HD, 0:NP], ACT.Copy))
                rows(l, 'mxb')
                act.wait_ge(ev["dec_shift"], l + 1)
                chain.add(A(PR[:, :], PR[:, :], ACT.Exp))
                A(small(32, 32), small(32, 32), ACT.Exp).then_inc(ev["dec_exp"], 1)
                read(A(R[:, :], job(l, 'var')[:, 0:T], ACT.Sqrt, bias=EPSB, scale=1.0 / GW))
                act.wait_ge(ev["conv_out"], l + 1)
                A(CAT[:, 0:2, :], CAT[:, 0:2, :], ACT.Silu).then_inc(ev["gate_silu"], 1)
                for g in ('go', 'rg'):
                    z = Z[:, ZT[g]:ZT[g] + 2, :]
                    A(z, z, ACT.Silu).then_inc(ev["gate_silu"], 1)
                rows(l, 'gate1')
                act.wait_ge(ev["gla_abs"], l + 1)
                chain(A(GA, GA, ACT.Exp, scale=-1.0))
                A(GA, GA, ACT.Ln, bias=1.0).then_inc(ev["gla_ln"], 1)
                act.wait_ge(ev["gla_b"], l + 1)
                chain.add(A(GQD, BC[:, :, :], ACT.Exp))
                chain.add(A(GKD, GKD, ACT.Exp))
                chain.add(A(DEC, DEC, ACT.Exp))
                A(GX, GX, ACT.Exp).then_inc(ev["gla_decays"], 1)
                for lag in range(1, CH):
                    rows(l, f'att{lag}')
                    act.wait_ge(ev["lag_diff"], l * (CH - 1) + lag)
                    n = 2 * NCH * (CH - lag)
                    A(EX[lag % 2][:, 0:n], EX[lag % 2][:, 0:n], ACT.Exp).then_inc(ev["lag_exp"], 1)
                for tt in range(2):
                    b = job(l, f'gkv{tt}')
                    chain.add(A(TMK[:, tt, :], b[:, 0:GW], ACT.Copy))
                    read(A(TMV[:, tt, :], b[:, GW:2 * GW], ACT.Copy))
                read(A(KV8[:, :], job(l, 'gts')[0:NS, :], ACT.Copy))
                rows(l, 'kv11')
                act.wait_ge(ev["gla_states"], l + 1)
                store(act, gla_out[l, :, :, 0:HD], SH[:, :, NCH - 1, :])
                rows(l, 'gx1')
                act.wait_ge(ev["s_gla"], l + 1)
                store(act, gla_out[l, :, :, HD:(NS + 1) * HD], SG[:, :, :])
                for c in range(2):
                    read(A(RNG[:, c, :], job(l, f'gn{c}')[:, 0:T], ACT.Sqrt, bias=EPSB, scale=1.0 / HD))
                for tt in range(2):
                    b = job(l, f'rkv{tt}')
                    chain.add(A(TMK[:, tt, :], b[:, 0:GW], ACT.Copy))
                    read(A(TMV[:, tt, :], b[:, GW:2 * GW], ACT.Copy))
                read(A(KV8[:, :], job(l, 'rts')[0:NS, :], ACT.Copy))
                act.wait_ge(ev["gla_cat"], l + 1)
                for h in range(NH):
                    c, s = h // 2, (h % 2) * HD
                    read(A(O[s:s + HD, c, 0:NP], job(l, f'ro{h}')[s:s + HD, 0:NP], ACT.Copy))
                read(A(PT[:, 0:P], job(l, 'rst')[:, 0:P], ACT.Copy))
                wait_read(l, 'rst')
                store(act, ret_out[l, :, :, 0:HD], PT[:, 0:P].rearrange("p (c v) -> p c v", c=2))
                rows(l, 'rx1')
                act.wait_ge(ev["s_ret"], l + 1)
                store(act, ret_out[l, :, :, HD:(NS + 1) * HD], SR[:, :, :])
                for c in range(2):
                    read(A(RNG[:, c, :], job(l, f'rn{c}')[:, 0:T], ACT.Sqrt, bias=EPSB, scale=1.0 / HD))
                act.wait_ge(stored, 16 * nstored[0])
                act.wait_ge(k_stored, 16 * (l + 1))
                if l == 0:
                    for n in range(NLOW, NSLOT):
                        wait_unit_used(act, [u for i, u in enumerate(UNITS[:NEXT]) if (i + SHIFT) % NSLOT == n][-1])
                    for q in range(NSPLIT):
                        round_dense(q)
                for c in range(KC):
                    act.wait_ge(out_added, l * KC + c + 1)
                    A(Z[:, c, :], X[:, c, :], ACT.Square).then_inc(ev["squares2"], 1)
                read(A(R[:, :], job(l, 'rms2')[:, 0:T], ACT.Sqrt, bias=EPSB, scale=1.0 / DM))
                if l % 2 == 0:
                    act.wait_ge(stored, 16 * nstored[0])
                    for q in range(NFP + 5):
                        if NSPLIT <= q < NFP:
                            act.wait_ge(fpiece_used, q - NSPLIT + 1)
                            round_dense(q)
                        if q == 0:
                            for c in range(KC):
                                act.wait_ge(ev["h2"], l * KC + c + 1)
                                A(HH[:, c, :], H[:, c, :], ACT.Copy).then_inc(hh_ready, 1)
                        for n, (_, j, i) in enumerate(PAIRS):
                            at = FPOS[('w1', j, i)]
                            for t in range(2):
                                if q == at + 3:
                                    act.wait_ge(fpiece_used, at + 1)
                                    if 2 * n + t >= 4:
                                        act.wait_ge(act_made, 2 * n + t - 3)
                                    A(SA[:, (2 * n + t) % 4, :], psum[t][:, 0:T], ACT.Silu).then_inc(silu_ready, 1)
                                if q == at + 5:
                                    act.wait_ge(act_made, 2 * n + t + 1)
                                    A(FAH[:, j % 2, 2 * i + t, :], FA[:, t, :], ACT.Copy).then_inc(act_high, 1)
                else:
                    act.wait_ge(stored, 16 * nstored[0])
                    act.wait_ge(gates_read, 1)
                    A(small(56, 3), small(56, 3), ACT.Exp).then_inc(gates_read, 1)
                    for i in range(6):
                        n = P if i < 4 else NS
                        act.wait_ge(h_turned, i + 1)
                        A(HTH[0:n, i // 2, (i % 2) * 512:(i % 2 + 1) * 512], psum[2 + i][0:n, :],
                          ACT.Copy).then_inc(ht_high, 1)
                    act.wait_ge(passes_ready, 1)
                    passes = act.value_load(PASSES[0:1, 0:1], min_val=1, max_val=NPASS)

                    def high_gathered(half, count):
                        act.wait_ge(gather_done, count)
                        A(HGH[:, 4 * half:4 * half + 4, :].rearrange("p c s -> p (c s)"), psum[GATHER[2 * half]][:, :],
                          ACT.Copy).then_inc(gathered_high, 1)

                    def copy_sum(at):
                        act.wait_ge(piece_used, at(NPC, NSPLIT))
                        for half in range(2):
                            A(YS[:, half * 512:(half + 1) * 512], psum[4 + half][:, :], ACT.Copy).then_inc(y_copied, 1)

                    act.wait_ge(banks_zeroed, 3)
                    for n in range(NLOW, NSLOT):
                        wait_unit_used(act, [u for i, u in enumerate(UNITS) if (i + SHIFT) % NSLOT == n][-1])
                    for half in range(2):
                        high_gathered(half, 2 * half + 1)

                    def expert(p, e):
                        def at(per, n):
                            return p * (NE * per) + e * per + n

                        def round_piece(q):
                            act.wait_ge(raw_full[q % NRAW], at(16 * (NPC // NRAW), 16 * (q // NRAW + 1)))
                            act.wait_ge(piece_used, at(NPC, q + 1))
                            A(WH[:, q % NSPLIT, :], eraw[q % NRAW], ACT.Copy).then_inc(high_ready, 1)

                        def round_turned(j):
                            act.wait_ge(turn_done, at(EB, j + 1))
                            A(ATH[:, :, :].rearrange("p k s -> p (k s)"), psum[6 + (j > 0) * (j + 1) % 2][:, :],
                              ACT.Copy).then_inc(turned_high, 1)

                        for q in range(NPC):
                            round_piece(q)
                            if q == NSPLIT - 1:
                                copy_sum(at)
                            for j in range(EB):
                                if q == SPOS[(0, j, 0)] + 3:
                                    if j >= 1:
                                        round_turned(j - 1)
                                    if j == 1:
                                        act.wait_ge(gst_done, at(1, 1))
                                        A(GST[:, :], psum[7][:, 0:T], ACT.Copy).then_inc(gst_ready, 1)
                                    act.wait_ge(piece_used, at(NPC, SPOS[(0, j, 1)] + 1 + NSPLIT))
                                    act.wait_ge(ea_ready, at(EB, j + 1))
                                    A(SILU[:, :], psum[2 * (j % 2)][:, :], ACT.Silu).then_inc(esilu_ready, 1)
                        round_turned(EB - 1)
                        for half in range(2):
                            high_gathered(half, at(4, 5 + 2 * half))
                    with act.Fori(0, NPASS) as p:
                        with act.If(p < passes):
                            with act.Fori(0, NE) as e:
                                expert(p, e)
                    copy_sum(lambda per, n: passes * (NE * per) + n)
            for half in range(2):
                c = slice(4 * half, 4 * half + 4)
                act.wait_ge(ev["x_final"], half + 1)
                store(act, y_out[:, c, :], X[:, c, :])

        @block.vector
        def _(dve):
            d = Chain(dve, dve_chain)
            V = nc.vector
            tt_, ts, stt = V.tensor_tensor, V.tensor_scalar, V.scalar_tensor_tensor

            def job(l, name):
                dve.wait_ge(job_done, job_no(l, name) + 1)
                return bank(l, name)

            def read(l, name, ins):
                ins.then_inc(job_read['v'], 1)
                dve.wait_ge(job_read['v'], read_no(l, name)[1])

            def wait_act_read(l, name):
                dve.wait_ge(job_read['a'], read_no(l, name)[1])

            def wait_z(l, g, i=None):
                dve.wait_ge(z_ready, l * NZ + ZPOS[ZT[g] + (max(ZW[g] // P - 1, 0) if i is None else i)] + 1)

            def signal(ins, name, count):
                ins.then_inc(ev[name], 1)
                dve.wait_ge(ev[name], count)

            def bmid(ap, n):
                return ap[:, None, :].to_broadcast([ap.shape[0], n, ap.shape[1]])

            def bend(ap, n):
                shape = list(ap.shape) + [n]
                return (ap[:, :, None] if len(ap.shape) == 2 else ap[:, :, :, None]).to_broadcast(shape)

            def norm(l, job_name, gain, scale, shift, signal_h):
                d(ts(MA[:, :, :], MOD[:, l, scale * KC:(scale + 1) * KC, :], 1.0, None, ALU.add))
                d(tt_(MA[:, :, :], MA[:, :, :], bend(v_(l, gain, 0, KC), NS + 1), ALU.mult))
                sh = MOD[:, l, shift * KC:(shift + 1) * KC, :]
                wait_act_read(l, job_name)
                d(V.reciprocal(R[:, :], R[:, :]))
                d(tt_(H[:, :, NP:T], X[:, :, NP:T], bmid(R[:, NP:T], KC), ALU.mult))
                d(tt_(H[:, :, NP:T], H[:, :, NP:T], MA[:, :, 1:], ALU.mult))
                d.add(tt_(H[:, :, NP:T], H[:, :, NP:T], sh[:, :, 1:], ALU.add))
                for c in range(KC + 1):
                    if c < KC:
                        d.add(stt(H[:, c, 0:NP], X[:, c, 0:NP], MA[:, c, 0:1], R[:, 0:NP], ALU.mult, ALU.mult))
                    if c:
                        dve.wait_ge(dve_chain, d.n - (c < KC))
                        ts(H[:, c - 1, 0:NP], H[:, c - 1, 0:NP], sh[:, c - 1, 0:1], None,
                           ALU.add).then_inc(ev[signal_h], 1)
                dve.wait_ge(ev[signal_h], (l + 1) * KC)

            def rest(out, full, high):
                return tt_(out, full, high.bitcast(F32), ALU.subtract)

            def low_dense(q):
                dve.wait_ge(fhigh_ready, q + 1)
                rest(WL[:, q % NSPLIT, :], raw[q % NRAW], WH[:, q % NSPLIT, :]).then_inc(flow_ready, 1)

            def add_residual(l, dst, src, m, gate):
                g = MOD[:, l, gate * KC + m, :]
                d.add(tt_(small(208, NS), src[:, NP:T], g[:, 1:], ALU.mult))
                d.add(stt(dst[:, 0:NP], src[:, 0:NP], g[:, 0:1], dst[:, 0:NP], ALU.mult, ALU.add))
                d.wait()
                return tt_(dst[:, NP:T], dst[:, NP:T], small(208, NS), ALU.add)

            def value_rows(v_off, signal_name, count):
                for h in range(NH):
                    v = KV8[:, v_off + h * HD:v_off + (h + 1) * HD]
                    ins = tt_(VE[:, h], bmid(v, NS), bend(ident[0:NS, 0:NS], HD), ALU.mult)
                    if h < NH - 1:
                        d.add(ins)
                d.wait()
                signal(ins, signal_name, count)

            def head_norm(l, squares, jobs, gain, gate, first, last, cat):
                signal(tt_(BCT, O[:, :, :], O[:, :, :], ALU.mult), squares, l + 1)
                wait_act_read(l, jobs[1])
                d(V.reciprocal(RNG, RNG))
                d(tt_(O[:, :, :], O[:, :, :], RNG, ALU.mult))
                for c in range(2):
                    ins = stt(CAT[:, cat + c, :], O[:, c, :], v_(l, gain, c), Z[:, ZT[gate] + c, :],
                              ALU.mult, ALU.mult)
                    if c == 0:
                        d(ins)
                return ins

            V.memset(EPSB, EPS).then_inc(eps_ready, 1)
            dve.wait_ge(consts_in, 16 * 3)
            dve.wait_ge(page_idx, 16)
            for l in range(L):
                ts(IDX[:, l, :], IDXI[:, :], float(L * SUB), c_('sub', P, l, l + 1), ALU.mult,
                   ALU.add).then_inc(idx_ready, 1)
            for l in range(L):
                if l == 0:
                    dve.wait_ge(more_consts_in, 16 * 4)
                    for c in range(KC):
                        tt_(H[:, c, :], X[:, c, :], X[:, c, :], ALU.mult).then_inc(ev["squares1"], 1)
                    dve.wait_ge(ev["squares1"], KC)
                dve.wait_ge(row_used, RPOS[('ada', l, ADA1 - 1)] + 1)
                norm(l, 'rms1', 'norm1', 1, 0, "h1")
                wait_z(l, 'fk')
                fqk = Z[:, ZT['fq']:ZT['fq'] + 4, :]
                signal(tt_(SQ, fqk, fqk, ALU.mult), "fox_squares", l + 1)
                wait_z(l, 'ff')
                d(ts(FX[:, :], FX[:, :], VT[0:NH, l, VCOL['fb']:VCOL['fb'] + 1], None, ALU.add))
                d(ts(FS[:, :], FX[:, :], 0.0, None, ALU.min))
                signal(stt(LF[:, :], FS[:, :], -2.0, FX[:, :], ALU.mult, ALU.add), "ff_exp", l + 1)
                wait_act_read(l, 'fn3')
                d(V.reciprocal(RN, RN))
                for i in range(4):
                    d.add(stt(fqk[:, i, :], fqk[:, i, :], v_(l, 'qn' if i < 2 else 'kn'), RN[:, i, :],
                              ALU.mult, ALU.mult))
                d.wait()
                signal(ts(fqk[:, 0:2, :], fqk[:, 0:2, :], HD ** -0.5, None, ALU.mult), "fox_qk", l + 1)
                dve.wait_ge(ev_ffln, l + 1)
                d(tt_(LF[:, :], FS[:, :], LF[:, :], ALU.subtract))
                for i in range(2):
                    a, b = i * P, (i + 1) * P
                    d(V.tensor_tensor_scan(FS[:, a:b], c_('ones', NH), LF[:, a:b],
                                           0.0 if i == 0 else FS[:, a - 1:a], ALU.mult, ALU.add))
                signal(ts(FX[:, 0:NP], FS[:, 0:NP], -1.0, None, ALU.mult), "fox_logf", l + 1)
                wait_act_read(l, 'qb3')
                for b in range(NS):
                    wait_unit(dve, ('k', l, b))
                    k3 = unit(('k', l, b)).rearrange("p (t f) -> p t f", t=TPP)
                    d(tt_(k3, k3, bmid(QB[:, b, :], TPP), ALU.mult))
                    V.tensor_reduce(SC[:, b].rearrange("p h t -> p t h"),
                                    k3.rearrange("p t (h d) -> p t h d", h=NH), AX.X, ALU.add).then_inc(k_used, 1)
                dve.wait_ge(k_used, NS * (l + 1))
                dve.wait_ge(logf_in, 16 * NS * (l + 1))
                LT = LP.rearrange("p b t h -> p b h t")
                d(V.memset(SUF[:, :, :, TPP - 1], 0.0))
                for t in range(TPP - 2, -1, -1):
                    d(tt_(SUF[:, :, :, t], SUF[:, :, :, t + 1], LT[:, :, :, t + 1], ALU.add))
                tot = small(96, 32).rearrange("p (b h) -> p b h", b=NS)
                d(tt_(tot, SUF[:, :, :, 0], LT[:, :, :, 0], ALU.add))
                lf = small(128, 32, NH).rearrange("p (b h) -> p b h", b=NS)
                signal(tt_(lf, bend(LF[:, NP:T], NH), bmid(ident[0:NH, 0:NH], NS), ALU.mult), "past_totals", l + 1)
                qk = small(224, 16).rearrange("p (c b) -> p c b", c=2)
                d(tt_(qk, fqk[:, 0:2, NP:T], fqk[:, 2:4, NP:T], ALU.mult))
                rt = small(64, 32).rearrange("p (b c s) -> p b c s", b=NS, c=2)
                d(tt_(rt[:, :, 0, :], bend(qk[:, 0, :], 2), bmid(c_('half'), NS), ALU.mult))
                signal(tt_(rt[:, :, 1, :], bend(qk[:, 1, :], 2), bmid(c_('half'), NS), ALU.mult), "row_terms", l + 1)
                for h in range(NH):
                    read(l, f's{h}', tt_(PS[:, h, :], job(l, f's{h}')[:, 0:3 * P], c_('causal'), ALU.add))
                    d.add(V.tensor_reduce(small(2 * h), PS[:, h, 0:P], AX.X, ALU.max, negate=True))
                    V.tensor_reduce(small(2 * h + 1), PS[:, h, P:3 * P], AX.X, ALU.max,
                                    negate=True).then_inc(ev["probs_max"], 1)
                for h in range(NH):
                    dve.wait_ge(ev["probs_exp"], 2 * (NH * l + h + 1))
                    d(V.reciprocal(small(8 + 2 * h, 2), small(8 + 2 * h, 2)))
                    d.add(ts(PS[:, h, 0:P], PS[:, h, 0:P], small(8 + 2 * h), None, ALU.mult))
                    ts(PS[:, h, P:3 * P], PS[:, h, P:3 * P], small(9 + 2 * h), None,
                       ALU.mult).then_inc(ev["probs"], 1)
                sn = small(32, 32)
                d(tt_(PR4, SC, SUF, ALU.add))
                read(l, 'snew', V.tensor_copy(sn, job(l, 'snew')[:, 0:32]))
                sf = job(l, 'suf')[:, 0:32].rearrange("p (b h) -> p b h", b=NS)
                read(l, 'suf', tt_(PR4, PR4, bend(sf, TPP), ALU.add))
                mx = small(160, 32)
                pr3 = PR[:, :].rearrange("p (r t) -> p r t", t=TPP)
                d(V.tensor_reduce(mx, pr3, AX.X, ALU.max))
                signal(tt_(mx, mx, sn, ALU.max), "max_part", l + 1)
                read(l, 'mxt', V.tensor_reduce(small(240, 1, 32), job(l, 'mxt')[0:32, 0:P], AX.X, ALU.max))
                signal(ts(small(192, 32, 32), ident[0:32, 0:32], small(240, 1, 32), None, ALU.mult), "max_diag", l + 1)
                mb = job(l, 'mxb')[:, 0:32]
                d(tt_(sn, sn, mb, ALU.subtract))
                read(l, 'mxb', tt_(pr3, pr3, bend(mb, TPP), ALU.subtract))
                signal(V.memset(small(241), 0.0), "dec_shift", l + 1)
                dve.wait_ge(ev["dec_exp"], l + 1)
                signal(V.tensor_reduce(small(64, 32), pr3, AX.X, ALU.add), "dec_sum", l + 1)
                read(l, 'sumb', tt_(small(160, 32), job(l, 'sumb')[:, 0:32], sn, ALU.add))
                d(V.reciprocal(small(160, 32), small(160, 32)))
                d(tt_(sn, sn, small(160, 32), ALU.mult))
                signal(tt_(pr3, pr3, bend(small(160, 32), TPP), ALU.mult), "dec_probs", l + 1)
                ca = Z[:, ZT['ca']:ZT['ca'] + 2, :]
                dve.wait_ge(job_done, job_no(l, 'o3') + 1)
                cw = v_(l, 'conv_w', 0, 2 * KW).rearrange("p (c k) -> p c k", c=2)
                UBW = TA[0][:, 0:2 * NS * KW].rearrange("p (c b k) -> p c b k", c=2, b=NS)
                dve.wait_ge(ev["conv_taps"], l + 1)
                for c in range(2):
                    d.add(tt_(UBW[:, c], UB[:, c], bmid(cw[:, c, :], NS), ALU.mult))
                d.wait()
                for c in range(2):
                    d.add(V.tensor_reduce(ca[:, c, NP:T], UBW[:, c], AX.X, ALU.add))
                d.wait()
                signal(tt_(ca, ca, bend(v_(l, 'conv_b', 0, 2), T), ALU.add), "conv_y", l + 1)
                b = job(l, 'mean')[:, 0:T]
                read(l, 'mean', ts(R[:, :], b, -1.0 / GW, None, ALU.mult))
                d(tt_(ca, ca, bmid(R[:, :], 2), ALU.add))
                signal(tt_(TA2, ca, ca, ALU.mult), "conv_sq", l + 1)
                wait_act_read(l, 'var')
                d(V.reciprocal(R[:, :], R[:, :]))
                d(tt_(ca, ca, bmid(R[:, :], 2), ALU.mult))
                for c in range(2):
                    d.add(ts(CAT[:, c, :], ca[:, c, :], v_(l, 'ln_g', c), v_(l, 'ln_b', c), ALU.mult, ALU.add))
                d.wait()
                signal(V.memset(small(241), 0.0), "conv_out", l + 1)
                for c in range(2):
                    read(l, f'gate{c}', ts(GX[:, c, :], job(l, f'gate{c}')[:, 0:T], v_(l, 'b_gate', c), None, ALU.add))
                d(ts(GM, GX, 0.0, None, ALU.min))
                signal(stt(GA, GM, -2.0, GX, ALU.mult, ALU.add), "gla_abs", l + 1)
                dve.wait_ge(ev["gla_ln"], l + 1)
                d(tt_(GX, GM, GA, ALU.subtract))
                d(ts(GX, GX, 1.0 / 16.0, None, ALU.mult))
                for c in range(2):
                    d.add(V.tensor_tensor_scan(BC[:, c, :], c_('reset'), GX[:, c, 0:NP], 0.0, ALU.mult, ALU.add))
                d.wait()
                bc4 = BC[:, :, :].rearrange("p c (n i) -> p c n i", i=CH)
                kd4 = GKD.rearrange("p c (n i) -> p c n i", i=CH)
                last = bc4[:, :, :, CH - 1]
                d.add(V.tensor_copy(DEC, last))
                dve.wait_ge(k_stored, 16 * (l + 1))
                for c in range(2):
                    ins = tt_(kd4[:, c], bend(last[:, c, :], CH), bc4[:, c], ALU.subtract)
                    if c == 0:
                        d.add(ins)
                d.wait()
                signal(ins, "gla_b", l + 1)
                gq = Z[:, ZT['gq']:ZT['gq'] + 2, :]
                gk = Z[:, ZT['gk']:ZT['gk'] + 2, :]
                gv = Z[:, ZT['gv']:ZT['gv'] + 2, :]
                wait_z(l, 'gv')
                d(ts(gq, gq, HD ** -0.5, None, ALU.mult))
                dve.wait_ge(ev["gla_decays"], l + 1)
                d.add(tt_(GQD, GQD, gq[:, :, 0:NP], ALU.mult))
                signal(tt_(GKD, GKD, gk[:, :, 0:NP], ALU.mult), "gla_kq", l + 1)
                q4, k4, v4 = (t[:, :, 0:NP].rearrange("p c (n i) -> p c n i", i=CH) for t in (gq, gk, gv))
                o4 = O[:, :, 0:NP].rearrange("p c (n i) -> p c n i", i=CH)

                def lag_view(t, lag):
                    return t[:, 0:2 * NCH * (CH - lag)].rearrange("p (c n i) -> p c n i", c=2, n=NCH)

                def difference(lag):
                    if lag >= 1:
                        tt_(lag_view(EX[lag % 2], lag), bc4[:, :, :, lag:], bc4[:, :, :, 0:CH - lag],
                            ALU.subtract).then_inc(ev["lag_diff"], 1)

                def weights(lag):
                    w = lag_view(WX[lag % 2], lag)
                    if lag >= 2:
                        dve.wait_ge(job_done, job_no(l, f'att{lag - 2}') + 1)
                    ins = tt_(w, q4[:, :, :, lag:], k4[:, :, :, 0:CH - lag], ALU.mult)
                    if lag >= 1:
                        d(ins)
                        dve.wait_ge(ev["lag_exp"], l * (CH - 1) + lag)
                        ins = tt_(w, w, lag_view(EX[lag % 2], lag), ALU.mult)
                    signal(ins, "lag_w", l * CH + lag + 1)

                def gather_lag(lag):
                    b = lag_view(job(l, f'att{lag}'), lag)
                    if lag == 0:
                        read(l, 'att0', tt_(o4, b, v4, ALU.mult))
                        return
                    t = lag_view(TA[lag % 2], lag)
                    read(l, f'att{lag}', tt_(t, b, v4[:, :, :, 0:CH - lag], ALU.mult))
                    d(tt_(o4[:, :, :, lag:], o4[:, :, :, lag:], t, ALU.add))

                for lag in range(CH + 1):
                    if lag < CH:
                        difference(lag)
                        weights(lag)
                    if lag >= 1:
                        gather_lag(lag - 1)
                for tt in range(2):
                    wait_act_read(l, 'gkv1')
                    if tt:
                        dve.wait_ge(job_done, job_no(l, 'kv01') + 1)
                    for h in range(NH):
                        ins = tt_(VX[:, h], bmid(TMV[:, tt, h * HD:(h + 1) * HD], 8), bend(c_('chunk'), HD), ALU.mult)
                        if h < NH - 1:
                            d.add(ins)
                    d.wait()
                    signal(ins, "gla_vx", 2 * l + tt + 1)
                    for pr in range(2):
                        b = job(l, f'kv{tt}{pr}')[:, :].rearrange("p (n v) -> p n v", n=8)
                        for n in range(8):
                            g = 8 * tt + n
                            if g == 0:
                                ins = V.tensor_copy(SH[:, pr, 0, :], b[:, 0, :])
                            else:
                                ins = stt(SH[:, pr, g, :], SH[:, pr, g - 1, :], DEC[:, pr, g:g + 1], b[:, n, :],
                                          ALU.mult, ALU.add)
                            if n < 7:
                                d(ins)
                        read(l, f'kv{tt}{pr}', ins)
                signal(V.memset(small(241), 0.0), "gla_states", l + 1)
                for s in range(2):
                    r = slice(s * HD, (s + 1) * HD)
                    b = job(l, f'gi{s}')[r, :].rearrange("p (c t) -> p c t", c=2)
                    read(l, f'gi{s}', tt_(O[r, :, CH:NP], O[r, :, CH:NP], b[:, :, CH:NP], ALU.add))
                wait_act_read(l, 'gts')
                dve.wait_ge(job_done, job_no(l, 'kv11') + 1)
                value_rows(GW, "ve_gla", l + 1)
                for c in range(2):
                    d.add(tt_(SG4[:, c], SG4[:, c], bend(GX[:, c, NP:T], HD), ALU.mult))
                d.wait()
                for c in range(2):
                    read(l, f'gx{c}', tt_(SG[:, c, :], SG[:, c, :], job(l, f'gx{c}')[:, :], ALU.add))
                signal(V.memset(small(241), 0.0), "s_gla", l + 1)
                for s in range(2):
                    r = slice(s * HD, (s + 1) * HD)
                    b = job(l, f'gs{s}')[r, 0:2 * NS].rearrange("p (c b) -> p c b", c=2)
                    read(l, f'gs{s}', V.tensor_copy(O[r, :, NP:T], b))
                dve.wait_ge(ev["gate_silu"], 3 * (l + 1))
                signal(head_norm(l, "gla_sq", ('gn0', 'gn1'), 'gla_g', 'go', None, None, 4), "gla_cat", l + 1)
                for i in range(4):
                    z, t = Z[:, ZT['rq'] + i, :], TA[i % 2][:, 0:T]
                    sc = 1.0 if i < 2 else HD ** -0.5
                    read(l, f'rr{i}', stt(t, job(l, f'rr{i}')[:, 0:T], sc, c_('sin'), ALU.mult, ALU.mult))
                    d(stt(z, z, sc, c_('cos'), ALU.mult, ALU.mult))
                    d(tt_(z, z, t, ALU.add))
                signal(V.memset(small(241), 0.0), "rope", l + 1)
                dec = c_('decay').rearrange("p (h t) -> p h t", h=NH)
                for h in range(NH):
                    b = job(l, f'rs{h}')
                    d(tt_(RP(h)[:, 0:NP], b[:, 0:NP], dec[:, h, :], ALU.mult))
                    read(l, f'rs{h}', tt_(RP(h)[:, NP:3 * P], b[:, NP:3 * P], dec[:, h, 0:P], ALU.mult))
                    V.memset(small(241), 0.0).then_inc(ev["ret_p"], 1)
                    dve.wait_ge(ev["ret_p"], NH * l + h + 1)
                wait_act_read(l, 'rkv1')
                dk = c_('dk').rearrange("p (t h) -> p t h", h=NH)
                for tt in range(2):
                    ins = tt_(TMK[:, tt, :].rearrange("p (h d) -> p h d", h=NH),
                              TMK[:, tt, :].rearrange("p (h d) -> p h d", h=NH), bend(dk[:, tt, :], HD), ALU.mult)
                    if tt == 0:
                        d(ins)
                signal(ins, "ret_kd", l + 1)
                dve.wait_ge(job_done, job_no(l, 'ro3') + 1)
                value_rows(GW, "ve_ret", l + 1)
                for c in range(2):
                    d(ts(SR[:, c, :], SR[:, c, :], c_('gamma', P, c, c + 1), None, ALU.mult))
                for c in range(2):
                    read(l, f'rx{c}', tt_(SR[:, c, :], SR[:, c, :], job(l, f'rx{c}')[:, :], ALU.add))
                signal(V.memset(small(241), 0.0), "s_ret", l + 1)
                for s in range(2):
                    r = slice(s * HD, (s + 1) * HD)
                    b = job(l, f'rd{s}')[r, 0:2 * NS].rearrange("p (c b) -> p c b", c=2)
                    read(l, f'rd{s}', V.tensor_copy(O[r, :, NP:T], b))
                wait_act_read(l, 'ro3')
                fv = Z[:, ZT['fv']:ZT['fv'] + 2, :]
                dve.wait_ge(row_used, RPOS[('pv', l, NS // 2 - 1)] + 1)
                pv4 = small(96, 32).rearrange("p (b c s) -> p c s b", b=NS, c=2)
                sn4 = sn.rearrange("p (b c s) -> p c s b", b=NS, c=2)
                for s in range(2):
                    r = slice(s * HD, (s + 1) * HD)
                    d(tt_(CAT[r, 2:4, NP:T], sn4[r, :, s, :], fv[r, :, NP:T], ALU.mult))
                    d(tt_(CAT[r, 2:4, NP:T], CAT[r, 2:4, NP:T], pv4[r, :, s, :], ALU.add))
                signal(head_norm(l, "ret_sq", ('rn0', 'rn1'), 'ret_g', 'rg', None, None, 6), "cat", l + 1)
                dve.wait_ge(stored, 16 * STORES_PER_LAYER * (l + 1))
                if l == 0:
                    for q in range(NSPLIT):
                        low_dense(q)
                dve.wait_ge(row_used, RPOS[('ada', l, NADA - 1)] + 1)
                for m in range(KC):
                    dve.wait_ge(out_done, l * KC + m + 1)
                    add_residual(l, X[:, m, :], psum[m % 2], m, 2).then_inc(out_added, 1)
                    dve.wait_ge(out_added, l * KC + m + 1)
                if l % 2 == 0:
                    norm(l, 'rms2', 'norm2', 4, 3, "h2")
                    added = 0
                    for q in range(NFP + 7):
                        if NSPLIT <= q < NFP:
                            low_dense(q)
                        if q == 0:
                            for c in range(KC):
                                dve.wait_ge(hh_ready, c + 1)
                                rest(HL[:, c, :], H[:, c, :], HH[:, c, :]).then_inc(hl_ready, 1)
                        for n, (_, j, i) in enumerate(PAIRS):
                            at = FPOS[('w1', j, i)]
                            for t in range(2):
                                if q == at + 4:
                                    dve.wait_ge(fpiece_used, at + 2)
                                    dve.wait_ge(silu_ready, 2 * n + t + 1)
                                    if n >= 1:
                                        dve.wait_ge(act_low, 2 * n + t - 1)
                                    tt_(FA[:, t, :], SA[:, (2 * n + t) % 4, :], psum[2 + t][:, 0:T],
                                        ALU.mult).then_inc(act_made, 1)
                                if q == at + 6:
                                    dve.wait_ge(act_high, 2 * n + t + 1)
                                    rest(FAL[:, j % 2, 2 * i + t, :], FA[:, t, :],
                                         FAH[:, j % 2, 2 * i + t, :]).then_inc(act_low, 1)
                        p = q - 2
                        if 0 <= p < NFP and FSTREAM[p][0] == 'w2':
                            _, j, i = FSTREAM[p]
                            for m in range(4 * i, 4 * i + 4) if FB[j][1] == COLS else range(KC):
                                last = m % 4 == 3 if FB[j][1] == COLS else m == KC - 1
                                if last:
                                    dve.wait_ge(fpiece_used, p + 1)
                                else:
                                    dve.wait_ge(y_done, y_tile_no(j, m))
                                b = psum[4 + m % 4][:, 0:T]
                                if j == 0:
                                    V.tensor_copy(YF[:, m, :], b).then_inc(y_added, 1)
                                else:
                                    tt_(YF[:, m, :], YF[:, m, :], b, ALU.add).then_inc(y_added, 1)
                                added += 1
                                dve.wait_ge(y_added, added)
                    for m in range(KC):
                        add_residual(l, X[:, m, :], YF[:, m, :], m, 5).then_inc(x_ready, 1)
                        dve.wait_ge(x_ready, m + 1)
                    signal(V.memset(small(241), 0.0), "dense_out", 1)
                else:
                    norm(l, 'rms2', 'norm2', 4, 3, "h2")
                    V.memset(GST[:, :], 0.0).then_inc(banks_zeroed, 1)
                    d.add(V.memset(Y[:, :, :], 0.0))
                    V.memset(small(241), 0.0).then_inc(ea_ready, 1)
                    V.memset(small(242), 0.0).then_inc(scattered, KC)
                    V.memset(small(243), 0.0).then_inc(piece_used, NSPLIT)
                    logits, top, index = (t.rearrange("p (a e) -> p a e", a=3)
                                          for t in (small(0, 24), small(24, 24), small(48, 6)))
                    gap, g1, g2 = (small(56 + 4 * i, 3)[:, :, None] for i in range(3))
                    m1, m2, mask = (t.rearrange("p (a e) -> p a e", a=3)
                                    for t in (small(72, 24), small(96, 24), small(128, 24)))
                    eio = bmid(c_('eio'), 3)
                    SLOTS, GATES = SLG[:, 0], SLG[:, 1]
                    d.add(V.memset(logits, 0.0))
                    d(V.memset(SLG[:, :, :, :], 0.0))
                    dve.wait_ge(router_done, 1)
                    d.add(V.tensor_copy(logits[:, 0:2, :], psum[0][:, 0:2 * NE].rearrange("p (a e) -> p a e", a=2)))
                    d(V.tensor_copy(logits[0:NS, 2, :], psum[0][0:NS, 2 * NE:3 * NE]))
                    for tt in range(3):
                        d.add(V.max(top[:, tt, :], logits[:, tt, :]))
                    d.wait()
                    tt_(gap, top[:, :, 1:2], top[:, :, 0:1], ALU.subtract).then_inc(gates_read, 1)
                    for tt in range(3):
                        d.add(V.max_index(MI[:, tt, :], top[:, tt, :], logits[:, tt, :]))
                    d.wait()
                    d(V.tensor_copy(index, MI[:, :, 0:2]))
                    d.add(tt_(m1, eio, index[:, :, 0:1].to_broadcast([P, 3, NE]), ALU.is_equal))
                    d(tt_(m2, eio, index[:, :, 1:2].to_broadcast([P, 3, NE]), ALU.is_equal))
                    tt_(mask, m1, m2, ALU.add).then_inc(masks_ready, 1)
                    dve.wait_ge(gates_read, 2)
                    d(ts(g1, gap, 1.0, None, ALU.add))
                    d(V.reciprocal(g1, g1))
                    d.add(tt_(g2, g1, gap, ALU.mult))
                    d(tt_(m1, m1, g1.to_broadcast([P, 3, NE]), ALU.mult))
                    d(tt_(m2, m2, g2.to_broadcast([P, 3, NE]), ALU.mult))
                    d(tt_(GATES[:, :, 0:NE], m1, m2, ALU.add))
                    d.add(V.tensor_copy(GATES[:, :, NE:], GATES[:, :, 0:1]))
                    for i in range(6):
                        n = P if i < 4 else NS
                        cols = slice((i % 2) * 512, (i % 2 + 1) * 512)
                        dve.wait_ge(ht_high, i + 1)
                        tt_(HTL[0:n, i // 2, cols], psum[2 + i][0:n, :], HTH[0:n, i // 2, cols].bitcast(F32),
                            ALU.subtract).then_inc(ht_low, 1)
                    dve.wait_ge(masks_ready, 1)
                    dve.wait_ge(router_done, 2)
                    d(V.tensor_reduce(small(160), psum[1][:, 3 * NE:4 * NE], AX.X, ALU.max))
                    d(ts(small(161), small(160), CAP + 0.5, None, ALU.is_gt))
                    d(stt(small(162), small(160), 2 * CAP + 0.5, small(161), ALU.is_gt, ALU.add))
                    signal_passes = ts(PASSES[:, :], small(162), 1.0, 1.0, ALU.mult, ALU.add)
                    signal_passes.then_inc(passes_ready, 1)

                    d.add(stt(SLOTS[:, 0:2, 0:NE], psum[1][:, 0:2 * NE].rearrange("p (a e) -> p a e", a=2), 1.0,
                              mask[:, 0:2, :], ALU.add, ALU.mult))
                    d(stt(SLOTS[0:NS, 2, 0:NE], psum[1][0:NS, 2 * NE:3 * NE], 1.0, mask[0:NS, 2, :], ALU.add, ALU.mult))
                    d(ts(SLOTS[:, :, 0:NE], SLOTS[:, :, 0:NE], -1.0, None, ALU.add))
                    d(ts(SLOTS[:, :, NE:], SLOTS[:, :, 0:1], -float(CAP), None, ALU.add))

                    def select(column):
                        s, g = SLG[:, 0, :, column], SLG[:, 1, :, column]
                        d(tt_(SEL[:, :, :], bmid(c_('slot'), 3), s.to_broadcast([P, 3, P]), ALU.is_equal))
                        return tt_(GSEL[:, :, :], SEL[:, :, :].bitcast(F32), g.to_broadcast([P, 3, P]), ALU.mult)

                    select(slice(0, 1)).then_inc(slots_ready, 1)
                    dve.wait_ge(ht_low, 6)
                    for half in range(2):
                        V.memset(psum[4 + half][:, :], 0.0).then_inc(banks_zeroed, 1)
                    dve.wait_ge(passes_ready, 1)
                    passes = dve.value_load(PASSES[0:1, 0:1], min_val=1, max_val=NPASS)

                    def low_gathered(half, count):
                        dve.wait_ge(gather_done, count)
                        c = slice(4 * half, 4 * half + 4)
                        V.tensor_copy(HGL[:, c, :].rearrange("p c s -> p (c s)"),
                                      psum[GATHER[2 * half + 1]][:, :]).then_inc(gathered, 1)

                    for half in range(2):
                        low_gathered(half, 2 * half + 2)

                    def add_scattered(at, tiles):
                        for m in tiles:
                            dve.wait_ge(scatter_done, at(KC, m + 1))
                            dve.wait_ge(scattered, at(KC, m + 1))
                            tt_(Y[:, m, :], Y[:, m, :], psum[6 + m % 2][:, 0:T], ALU.add).then_inc(scattered, 1)

                    def expert(p, e):
                        def at(per, n):
                            return p * (NE * per) + e * per + n

                        def low_turned(j):
                            dve.wait_ge(turned_high, at(EB, j + 1))
                            rest(ATL[:, :, :].rearrange("p k s -> p (k s)"), psum[6 + (j > 0) * (j + 1) % 2][:, :],
                                 ATH[:, :, :].rearrange("p k s -> p (k s)")).then_inc(turned, 1)

                        for q in range(NPC):
                            dve.wait_ge(high_ready, at(NPC, q + 1))
                            rest(WL[:, q % NSPLIT, :], eraw[q % NRAW], WH[:, q % NSPLIT, :]).then_inc(low_ready, 1)
                            for j in range(EB):
                                if q == SPOS[(0, j, 0)] + 3 and j >= 1:
                                    low_turned(j - 1)
                                if q == SPOS[(0, j, 0)] + 5:
                                    dve.wait_ge(piece_used, at(NPC, SPOS[(1, j, 1)] + 1 + NSPLIT))
                                    dve.wait_ge(esilu_ready, at(EB, j + 1))
                                    tt_(AM[:, :], SILU[:, :], psum[2 * (j % 2) + 1][:, :], ALU.mult).then_inc(ea_ready, 1)
                                if q == SPOS[(0, j, 0)] + 5 and j == 3:
                                    s, g = SLG[:, 0, :, bass.ds(e + 1, 1)], SLG[:, 1, :, bass.ds(e + 1, 1)]
                                    tt_(SEL[:, :, :], bmid(c_('slot'), 3), s.to_broadcast([P, 3, P]),
                                        ALU.is_equal).then_inc(sel_ready, 1)
                                    dve.wait_ge(sel_ready, at(1, 1))
                                    tt_(GSEL[:, :, :], SEL[:, :, :].bitcast(F32), g.to_broadcast([P, 3, P]),
                                        ALU.mult).then_inc(slots_ready, 1)
                            if q == 5:
                                add_scattered(at, range(4))
                            if q == 6:
                                add_scattered(at, range(4, KC))
                        low_turned(EB - 1)
                        for half in range(2):
                            low_gathered(half, at(4, 6 + 2 * half))
                    with dve.Fori(0, NPASS) as p:
                        with dve.If(p < passes):
                            with dve.Fori(0, NE) as e:
                                expert(p, e)
                            ts(SLOTS, SLOTS, -float(CAP), None, ALU.add).then_inc(slots_moved, 1)
                            dve.wait_ge(slots_moved, p + 1)
                            V.memset(small(241), 0.0)
                    G2S = MOD[:, l, 5 * KC:6 * KC, :]
                    for half in range(2):
                        c = slice(4 * half, 4 * half + 4)
                        for m in range(4 * half, 4 * half + 4):
                            add_scattered(lambda per, n: passes * (NE * per) + n, (m,))
                            dve.wait_ge(scattered, passes * (NE * KC) + KC + m + 1)
                            d.add(stt(X[:, m, 0:NP], Y[:, m, 0:NP], G2S[:, m, 0:1], X[:, m, 0:NP], ALU.mult, ALU.add))
                        d(tt_(Y[:, c, NP:T], Y[:, c, NP:T], G2S[:, c, 1:], ALU.mult))
                        tt_(X[:, c, NP:T], X[:, c, NP:T], Y[:, c, NP:T], ALU.add).then_inc(ev["x_final"], 1)


def kernel(**inputs):
    import numpy as np
    import concourse.bacc as bacc
    from concourse.bass_utils import run_bass_kernel_spmd

    a = {k: np.asarray(v) for k, v in inputs.items()}

    def features(x):
        return np.ascontiguousarray(x.T.reshape(-1, P, x.shape[0]).transpose(1, 0, 2))

    def columns(v):
        return v.reshape(-1, P).T

    x = np.concatenate([a['x_prompt'][0], a['x_sample'][:, 0]])
    c = np.concatenate([a['c_prompt'], a['c_sample']])
    vt = []
    for l in range(L):
        parts = [columns(a['norm1_g'][l]), columns(a['norm2_g'][l]), columns(a['b_ada'][l]), columns(a['conv_b'][l]),
                 columns(a['conv_ln_g'][l]), columns(a['conv_ln_b'][l]), columns(a['gla_b_gate'][l]),
                 columns(a['gla_norm_g'][l]), columns(a['ret_norm_g'][l]), np.tile(a['fox_qn_g'][l], 2)[:, None],
                 np.tile(a['fox_kn_g'][l], 2)[:, None], np.tile(a['fox_fb'][l], P // NH)[:, None],
                 a['conv_w'][l].T.reshape(2, P, KW).transpose(1, 0, 2).reshape(P, 2 * KW)]
        vt.append(np.concatenate(parts, 1))

    def states(s):
        return np.ascontiguousarray(
            s.reshape(L, NS, 2, 2, HD, HD).transpose(0, 3, 4, 2, 1, 5).reshape(L, P, 2, NS * HD))

    arrays = {
        'xT': features(x), 'cT': features(c), 'vt': np.ascontiguousarray(np.stack(vt, 1)),
        'consts': host_constants(),
        'conv_in': np.ascontiguousarray(
            a['state_conv'].reshape(L, NS, KW - 1, 2, P).transpose(0, 4, 3, 1, 2)),
        'gla_in': states(a['state_gla']), 'ret_in': states(a['state_ret']),
        'ptr': np.ascontiguousarray(np.repeat(a['page_table'].T, SUB, axis=0)),
        'cache_k': a['cache_k'], 'cache_v': a['cache_v'], 'cache_logf': a['cache_logf'],
        'w_in': a['w_in'], 'w_out': a['w_out'], 'w_ada': a['w_ada'], 'gate2': a['gla_w_gate2'],
        'ffn_w1': a['ffn_w1'], 'ffn_w3': a['ffn_w3'], 'ffn_w2': a['ffn_w2'],
        'router': a['moe_router'][0], 'moe_w1': a['moe_w1'], 'moe_w3': a['moe_w3'], 'moe_w2': a['moe_w2'],
    }
    outs = {'y_out': (P, KC, T), 'conv_out': (L, P, 2, (NS + 1) * (KW - 1)), 'k_out': (L, P, 2, T),
            'v_out': (L, P, 2, T), 'logf_out': (L, NH, T), 'gla_out': (L, P, 2, (NS + 1) * HD),
            'ret_out': (L, P, 2, (NS + 1) * HD)}
    nc = bacc.Bacc("TRN2", target_bir_lowering=False, num_devices=1)
    args = [nc.dram_tensor(k, v.shape, mybir.dt.from_np(v.dtype), kind="ExternalInput").ap()
            for k, v in arrays.items()]
    args += [nc.dram_tensor(k, v, F32, kind="ExternalOutput").ap() for k, v in outs.items()]
    trunk_kernel(nc, *args)
    r = run_bass_kernel_spmd(nc, [arrays], core_ids=[0]).results[0]

    def tokens(y):
        y = np.moveaxis(y, -1, -3)
        return np.swapaxes(y, -1, -2).reshape(*y.shape[:-2], -1)

    y = tokens(r['y_out'])
    conv = np.asarray(r['conv_out']).reshape(L, P, 2, NS + 1, KW - 1).transpose(0, 3, 4, 2, 1)
    conv = conv.reshape(L, NS + 1, KW - 1, GW)
    k, v = (tokens(r[n]).reshape(L, T, NH, HD) for n in ('k_out', 'v_out'))
    logf = np.asarray(r['logf_out']).transpose(0, 2, 1)

    def split(s):
        s = np.asarray(s).reshape(L, 2, HD, 2, NS + 1, HD).transpose(0, 4, 3, 1, 2, 5)
        s = s.reshape(L, NS + 1, NH, HD, HD)
        return s[:, :1], s[:, 1:]

    def by_sample(t):
        return t[:, NP:].swapaxes(0, 1)[:, :, None]

    gla, ret = split(r['gla_out']), split(r['ret_out'])
    result = (y[None, :NP], y[NP:, None], conv[:, :1], conv[:, 1:], k[None, :, :NP], by_sample(k),
              v[None, :, :NP], by_sample(v), logf[None, :, :NP], by_sample(logf), gla[0], gla[1], ret[0], ret[1])
    return tuple(np.ascontiguousarray(t) for t in result)
```
